# Optimizing a Trainium2 kernel written in Bass

```python
import math
import jax
import jax.numpy as jnp
from jax import lax
import numpy as np

D_MODEL = 1024
BATCH = 1
SEQ = 256
DEPTH = 2
DEC_BATCH = 8
DEC_SEQ = 1
PAST_LEN = 1024
PAGE_SIZE = 128

HG_HEADS = 4
HG_DK = 128
HG_DV = 128
HG_WIDTH = HG_HEADS * HG_DV
HG_CHUNK = 64
SB_HEADS = 8
SB_HEAD_DIM = 64
SB_WIDTH = SB_HEADS * SB_HEAD_DIM
SB_BLOCK = 128
ML_HEADS = 4
ML_HEAD_DIM = 128
ML_WIDTH = ML_HEADS * ML_HEAD_DIM
ML_CHUNK = 128
ML_CONV = 4
D_FF = 2816
FFN_RES = 0.5
N_SUB = 3
NORM_EPS = 1e-6
IN_COLS = 2 * HG_HEADS * HG_DK + 2 * HG_WIDTH + 3 * SB_WIDTH + 2 * ML_WIDTH + 3 * D_MODEL

kernel_name = 'hybrid_hgrn2_stickbreak_mlstm_step'

def _in_split_points():
    sizes = (HG_HEADS * HG_DK, HG_HEADS * HG_DK, HG_WIDTH, HG_WIDTH,
             SB_WIDTH, SB_WIDTH, SB_WIDTH, ML_WIDTH, ML_WIDTH,
             D_MODEL, D_MODEL, D_MODEL)
    pts, acc = [], 0
    for s in sizes[:-1]:
        acc += s
        pts.append(acc)
    return pts

def _rmsnorm(x, g):
    xf = x.astype(jnp.float32)
    y = xf * lax.rsqrt(jnp.mean(xf * xf, axis=-1, keepdims=True) + NORM_EPS)
    return (y * g.astype(jnp.float32)).astype(x.dtype)

def _head_norm(o, gain):
    B, T, H, d = o.shape
    o = o * lax.rsqrt(jnp.mean(o * o, axis=-1, keepdims=True) + NORM_EPS)
    return o.reshape(B, T, H * d) * gain.astype(jnp.float32)

def _swiglu(h, w_in, w_down):
    gate, up = jnp.split(h @ w_in, 2, axis=-1)
    return (jax.nn.silu(gate) * up) @ w_down

def _to_chunks(a, nc):
    return jnp.moveaxis(a.reshape(a.shape[0], nc, a.shape[1] // nc, *a.shape[2:]), 1, 0)

def _from_chunks(a):
    a = jnp.moveaxis(a, 0, 1)
    return a.reshape(a.shape[0], a.shape[1] * a.shape[2], *a.shape[3:])

def _hgrn_lower_bound(lb_logits, l):
    p = jax.nn.softmax(lb_logits.astype(jnp.float32), axis=0)
    cum = jnp.cumsum(p, axis=0)
    return cum[l] - cum[0]

def _hgrn_chunk(S, inp):
    q, logf, k, i = inp
    L = q.shape[1]
    b = jnp.cumsum(logf, axis=1)
    causal = jnp.tril(jnp.ones((L, L), dtype=bool))
    diff = b[:, :, None] - b[:, None, :]
    decay = jnp.exp(jnp.where(causal[None, :, :, None, None], diff, -jnp.inf))
    scores = jnp.einsum('bthc,btshc,bshc->bhts', q, decay, k)
    o = (jnp.einsum('bthc,bhcv->bthv', q * jnp.exp(b), S)
         + jnp.einsum('bhts,bshv->bthv', scores, i))
    kd = jnp.exp(b[:, -1:] - b) * k
    S_new = jnp.exp(b[:, -1])[..., None] * S + jnp.einsum('bshc,bshv->bhcv', kd, i)
    return S_new, o

def _hgrn2(hq, hf, hi, hg, lb, S0, gain, chunk):
    B, T, _ = hq.shape
    f32 = jnp.float32
    q = hq.astype(f32).reshape(B, T, HG_HEADS, HG_DK)
    z = hf.astype(f32).reshape(B, T, HG_HEADS, HG_DK)
    i = hi.astype(f32).reshape(B, T, HG_HEADS, HG_DV)
    lbh = lb.reshape(HG_HEADS, HG_DK)
    logf = jnp.logaddexp(jnp.log(lbh), jnp.log1p(-lbh) + jax.nn.log_sigmoid(z))
    k = (1.0 - lbh) * jax.nn.sigmoid(-z)
    nc = T // chunk
    S, o = lax.scan(_hgrn_chunk, S0.astype(f32),
                    (_to_chunks(q, nc), _to_chunks(logf, nc), _to_chunks(k, nc), _to_chunks(i, nc)))
    o = _head_norm(_from_chunks(o), gain) * jax.nn.silu(hg.astype(f32))
    return o, S

def _sb_attend(q, k, v, q_pos, k_pos, bias):
    f32 = jnp.float32
    z = (jnp.einsum('bqhd,bkhd->bhqk', q.astype(f32), k.astype(f32)) * (SB_HEAD_DIM ** -0.5)
         + bias.astype(f32)[None, :, None, None])
    mask = k_pos[None, :] < q_pos[:, None]
    log_1m = jnp.where(mask, jax.nn.log_sigmoid(-z), 0.0)
    suffix = lax.cumsum(log_1m, axis=3, reverse=True) - log_1m
    A = jnp.where(mask, jnp.exp(jax.nn.log_sigmoid(z) + suffix), 0.0)
    return jnp.einsum('bhqk,bkhd->bqhd', A, v.astype(f32))

def _sb_prompt(q, k, v, bias):
    B, T, H, d = q.shape
    nb = T // SB_BLOCK
    qb = jnp.moveaxis(q.reshape(B, nb, SB_BLOCK, H, d), 1, 0)
    starts = jnp.arange(nb) * SB_BLOCK
    k_pos = jnp.arange(T)

    def block(args):
        qi, s = args
        return _sb_attend(qi, k, v, s + jnp.arange(SB_BLOCK), k_pos, bias)

    o = lax.map(block, (qb, starts))
    return jnp.moveaxis(o, 0, 1).reshape(B, T, H, d)

def _mlstm_chunk(carry, inp):
    C, n, m = carry
    q, k, v, it, logf = inp
    L = q.shape[1]
    b = jnp.cumsum(logf, axis=1)
    causal = jnp.tril(jnp.ones((L, L), dtype=bool))
    logD = b[:, :, None, :] - b[:, None, :, :] + it[:, None, :, :]
    logD = jnp.where(causal[None, :, :, None], logD, -jnp.inf)
    m_t = jnp.maximum(b + m[:, None, :], jnp.max(logD, axis=2))
    Dm = jnp.exp(logD - m_t[:, :, None, :])
    inter = jnp.exp(b + m[:, None, :] - m_t)
    W = jnp.einsum('bthd,bshd->btsh', q, k) * Dm
    numer = (inter[..., None] * jnp.einsum('bhvd,bthd->bthv', C, q)
             + jnp.einsum('btsh,bshv->bthv', W, v))
    denom = inter * jnp.einsum('bhd,bthd->bth', n, q) + jnp.sum(W, axis=2)
    h = numer / jnp.maximum(jnp.abs(denom), jnp.exp(-m_t))[..., None]
    m_new = m_t[:, -1]
    w_end = jnp.exp(b[:, -1:] - b + it - m_new[:, None])
    dec = jnp.exp(b[:, -1] + m - m_new)
    C_new = dec[..., None, None] * C + jnp.einsum('bsh,bshv,bshd->bhvd', w_end, v, k)
    n_new = dec[..., None] * n + jnp.einsum('bsh,bshd->bhd', w_end, k)
    return (C_new, n_new, m_new), h

def _mlstm(hx, ho, buf0, l, prm, C0, n0, m0, chunk):
    B, T, _ = hx.shape
    f32 = jnp.float32
    x = hx.astype(f32)
    xpad = jnp.concatenate([buf0.astype(f32), x], axis=1)
    w = prm['ml_conv_w'][l].astype(f32)
    xc = jax.nn.silu(sum(xpad[:, j:j + T] * w[j] for j in range(ML_CONV)) + prm['ml_conv_b'][l])
    buf_new = xpad[:, T:]
    xch = xc.reshape(B, T, ML_HEADS, ML_HEAD_DIM)
    xh = x.reshape(B, T, ML_HEADS, ML_HEAD_DIM)
    q = jnp.einsum('bthd,hde->bthe', xch, prm['ml_wq'][l])
    k = jnp.einsum('bthd,hde->bthe', xch, prm['ml_wk'][l])
    v = jnp.einsum('bthd,hde->bthe', xh, prm['ml_wv'][l])
    qkv = jnp.concatenate([q, k, v], axis=2).reshape(B, T, 3 * ML_WIDTH)
    gates = (qkv @ prm['ml_w_if'][l] + prm['ml_b_if'][l]).astype(f32)
    it = gates[..., :ML_HEADS]
    logf = jax.nn.log_sigmoid(gates[..., ML_HEADS:])
    ks = k * (ML_HEAD_DIM ** -0.5)
    nc = T // chunk
    (C, n, m), hh = lax.scan(
        _mlstm_chunk, (C0.astype(f32), n0.astype(f32), m0.astype(f32)),
        (_to_chunks(q, nc), _to_chunks(ks, nc), _to_chunks(v, nc), _to_chunks(it, nc), _to_chunks(logf, nc)))
    o = _head_norm(_from_chunks(hh), prm['ml_gain'][l]) * jax.nn.sigmoid(ho.astype(f32))
    return o, (C, n, m, buf_new)

def _mix(h, l, prm, past):
    B, T, _ = h.shape
    f32 = jnp.float32
    proj = h @ prm['w_in'][l]
    hq, hf, hi, hg, sq, sk, sv, mx, mo, ga, gb, gc = jnp.split(proj, _in_split_points(), axis=-1)
    if past is None:
        S0 = jnp.zeros((B, HG_HEADS, HG_DK, HG_DV), f32)
        C0 = jnp.zeros((B, ML_HEADS, ML_HEAD_DIM, ML_HEAD_DIM), f32)
        n0 = jnp.zeros((B, ML_HEADS, ML_HEAD_DIM), f32)
        m0 = jnp.zeros((B, ML_HEADS), f32)
        buf0 = jnp.zeros((B, ML_CONV - 1, ML_WIDTH), f32)
        hg_chunk, ml_chunk = HG_CHUNK, ML_CHUNK
    else:
        S0 = past['hgrn'][:, l]
        C0 = past['mc'][:, l]
        n0 = past['mn'][:, l]
        m0 = past['mm'][:, l]
        buf0 = past['mconv'][:, l]
        hg_chunk, ml_chunk = T, T
    lb = _hgrn_lower_bound(prm['hg_lb_logits'], l)
    o_a, S_new = _hgrn2(hq, hf, hi, hg, lb, S0, prm['hg_gain'][l], hg_chunk)
    sbb = prm['sb_bias'][l]
    q = sq.reshape(B, T, SB_HEADS, SB_HEAD_DIM)
    k = sk.reshape(B, T, SB_HEADS, SB_HEAD_DIM)
    v = sv.reshape(B, T, SB_HEADS, SB_HEAD_DIM)
    if past is None:
        o_b = _sb_prompt(q, k, v, sbb)
    else:
        pk = past['k'][past['page_table'], l].reshape(B, -1, SB_HEADS, SB_HEAD_DIM)
        pv = past['v'][past['page_table'], l].reshape(B, -1, SB_HEADS, SB_HEAD_DIM)
        P = pk.shape[1]
        o_b = _sb_attend(q, jnp.concatenate([pk.astype(k.dtype), k], axis=1),
                         jnp.concatenate([pv.astype(v.dtype), v], axis=1),
                         P + jnp.arange(T), jnp.arange(P + T), sbb)
    o_b = o_b.reshape(B, T, SB_WIDTH)
    o_c, (C_new, n_new, m_new, buf_new) = _mlstm(mx, mo, buf0, l, prm, C0, n0, m0, ml_chunk)
    merged = (jax.nn.sigmoid(ga.astype(f32)) * (o_a @ prm['w_hg_proj'][l])
              + jax.nn.sigmoid(gb.astype(f32)) * (o_b @ prm['w_sb_proj'][l])
              + jax.nn.sigmoid(gc.astype(f32)) * (o_c @ prm['w_ml_proj'][l]))
    y = (merged @ prm['w_out'][l]).astype(h.dtype)
    st = dict(k=k, v=v, hgrn=S_new, mc=C_new, mn=n_new, mm=m_new, mconv=buf_new)
    return y, st

def _layer(x, c, l, prm, past):
    B, _, D = x.shape
    ada = jax.nn.silu(c) @ prm['w_ada'][l] + prm['b_ada'][l]
    ada = ada.reshape(B, N_SUB, 3, D)[:, :, :, None, :]

    def pre(j, z):
        return _rmsnorm(z, prm['g_pre'][l, j]) * (1 + ada[:, j, 1]) + ada[:, j, 0]

    def post(j, z, y, w):
        return (z + w * (1 + ada[:, j, 2]) * _rmsnorm(y, prm['g_post'][l, j])).astype(z.dtype)

    x = post(0, x, _swiglu(pre(0, x), prm['w_ffn_in'][l, 0], prm['w_ffn_down'][l, 0]), FFN_RES)
    y, st = _mix(pre(1, x), l, prm, past)
    x = post(1, x, y, 1.0)
    x = post(2, x, _swiglu(pre(2, x), prm['w_ffn_in'][l, 1], prm['w_ffn_down'][l, 1]), FFN_RES)
    return x, st

def _run(x, c, prm, past):
    outs = []
    for l in range(DEPTH):
        x, st = _layer(x, c, l, prm, past)
        outs.append(st)
    stacked = {name: jnp.stack([o[name] for o in outs], axis=1).astype(x.dtype) for name in outs[0]}
    return x, stacked

def setup_inputs(seed: int = 0) -> dict:
    key = jax.random.key(seed)
    keys = jax.random.split(key, 48)
    cnt = [0]

    def nk():
        cnt[0] += 1
        return keys[cnt[0] - 1]

    def nrm(shape, scale):
        return jax.random.normal(nk(), shape, jnp.float32) * scale

    n_pages = PAST_LEN // PAGE_SIZE
    n_phys = (DEC_BATCH * n_pages * 5) // 4
    D = D_MODEL
    inp = {}
    inp['x_prompt'] = nrm((BATCH, SEQ, D), 1.0)
    inp['x_sample'] = nrm((DEC_BATCH, DEC_SEQ, D), 1.0)
    inp['cache_sb_k'] = nrm((n_phys, DEPTH, PAGE_SIZE, SB_HEADS, SB_HEAD_DIM), 1.0)
    inp['cache_sb_v'] = nrm((n_phys, DEPTH, PAGE_SIZE, SB_HEADS, SB_HEAD_DIM), 1.0)
    inp['state_hgrn'] = nrm((DEC_BATCH, DEPTH, HG_HEADS, HG_DK, HG_DV), 1.0)
    inp['state_mlstm_c'] = nrm((DEC_BATCH, DEPTH, ML_HEADS, ML_HEAD_DIM, ML_HEAD_DIM), 0.3)
    inp['state_mlstm_n'] = nrm((DEC_BATCH, DEPTH, ML_HEADS, ML_HEAD_DIM), 0.3)
    inp['state_mlstm_m'] = nrm((DEC_BATCH, DEPTH, ML_HEADS), 1.0)
    inp['state_mlstm_conv'] = nrm((DEC_BATCH, DEPTH, ML_CONV - 1, ML_WIDTH), 1.0)
    perm = jax.random.permutation(nk(), n_phys)
    inp['page_table'] = perm[:DEC_BATCH * n_pages].reshape(DEC_BATCH, n_pages).astype(jnp.int32)
    inp['c_prompt'] = nrm((BATCH, D), 1.0)
    inp['c_sample'] = nrm((DEC_BATCH, D), 1.0)
    inp['w_ada'] = nrm((DEPTH, D, N_SUB * 3 * D), 0.2 * D ** -0.5)
    inp['b_ada'] = nrm((DEPTH, N_SUB * 3 * D), 0.01)
    inp['g_pre'] = 1.0 + nrm((DEPTH, N_SUB, D), 0.05)
    inp['g_post'] = 1.0 + nrm((DEPTH, N_SUB, D), 0.05)
    inp['w_ffn_in'] = nrm((DEPTH, 2, D, 2 * D_FF), D ** -0.5)
    inp['w_ffn_down'] = nrm((DEPTH, 2, D_FF, D), D_FF ** -0.5)
    inp['w_in'] = nrm((DEPTH, D, IN_COLS), D ** -0.5)
    inp['sb_bias'] = -jnp.linspace(4.0, 9.0, SB_HEADS)[None, :] + nrm((DEPTH, SB_HEADS), 0.1)
    inp['hg_lb_logits'] = nrm((DEPTH, HG_HEADS * HG_DK), 1.0)
    inp['hg_gain'] = 1.0 + nrm((DEPTH, HG_WIDTH), 0.05)
    inp['ml_conv_w'] = nrm((DEPTH, ML_CONV, ML_WIDTH), ML_CONV ** -0.5)
    inp['ml_conv_b'] = nrm((DEPTH, ML_WIDTH), 0.01)
    inp['ml_wq'] = nrm((DEPTH, ML_HEADS, ML_HEAD_DIM, ML_HEAD_DIM), ML_HEAD_DIM ** -0.5)
    inp['ml_wk'] = nrm((DEPTH, ML_HEADS, ML_HEAD_DIM, ML_HEAD_DIM), ML_HEAD_DIM ** -0.5)
    inp['ml_wv'] = nrm((DEPTH, ML_HEADS, ML_HEAD_DIM, ML_HEAD_DIM), ML_HEAD_DIM ** -0.5)
    inp['ml_w_if'] = nrm((DEPTH, 3 * ML_WIDTH, 2 * ML_HEADS), 0.1 * (3 * ML_WIDTH) ** -0.5)
    b_i = nrm((DEPTH, ML_HEADS), 0.1)
    b_f = jnp.linspace(3.0, 6.0, ML_HEADS)[None, :] + nrm((DEPTH, ML_HEADS), 0.1)
    inp['ml_b_if'] = jnp.concatenate([b_i, b_f], axis=-1)
    inp['ml_gain'] = 1.0 + nrm((DEPTH, ML_WIDTH), 0.05)
    inp['w_hg_proj'] = nrm((DEPTH, HG_WIDTH, D), HG_WIDTH ** -0.5)
    inp['w_sb_proj'] = nrm((DEPTH, SB_WIDTH, D), SB_WIDTH ** -0.5)
    inp['w_ml_proj'] = nrm((DEPTH, ML_WIDTH, D), ML_WIDTH ** -0.5)
    inp['w_out'] = nrm((DEPTH, D, D), D ** -0.5)
    return inp

def reference(x_prompt, x_sample, cache_sb_k, cache_sb_v, state_hgrn, state_mlstm_c, state_mlstm_n,
              state_mlstm_m, state_mlstm_conv, page_table, c_prompt, c_sample, w_ada, b_ada, g_pre, g_post,
              w_ffn_in, w_ffn_down, w_in, sb_bias, hg_lb_logits, hg_gain, ml_conv_w, ml_conv_b, ml_wq, ml_wk,
              ml_wv, ml_w_if, ml_b_if, ml_gain, w_hg_proj, w_sb_proj, w_ml_proj, w_out):
    prm = dict(w_ada=w_ada, b_ada=b_ada, g_pre=g_pre, g_post=g_post, w_ffn_in=w_ffn_in,
               w_ffn_down=w_ffn_down, w_in=w_in, sb_bias=sb_bias, hg_lb_logits=hg_lb_logits,
               hg_gain=hg_gain, ml_conv_w=ml_conv_w, ml_conv_b=ml_conv_b, ml_wq=ml_wq, ml_wk=ml_wk,
               ml_wv=ml_wv, ml_w_if=ml_w_if, ml_b_if=ml_b_if, ml_gain=ml_gain, w_hg_proj=w_hg_proj,
               w_sb_proj=w_sb_proj, w_ml_proj=w_ml_proj, w_out=w_out)
    y_prompt, sp = _run(x_prompt, c_prompt, prm, None)
    past = dict(k=cache_sb_k, v=cache_sb_v, page_table=page_table, hgrn=state_hgrn, mc=state_mlstm_c,
                mn=state_mlstm_n, mm=state_mlstm_m, mconv=state_mlstm_conv)
    y_sample, ss = _run(x_sample, c_sample, prm, past)
    return (y_prompt, y_sample, sp['k'], sp['v'], ss['k'], ss['v'], sp['hgrn'], ss['hgrn'],
            sp['mc'], ss['mc'], sp['mn'], ss['mn'], sp['mm'], ss['mm'], sp['mconv'], ss['mconv'])


_drawn_inputs = setup_inputs


def setup_inputs(seed=0):
    import zlib

    import numpy as np

    out = dict(_drawn_inputs(seed))
    spreads = {}
    factors = {}
    for name, (base, spread) in spreads.items():
        noise = np.random.default_rng([zlib.crc32(name.encode()), seed]).standard_normal(out[name].shape)
        drawn = base * np.exp(spread * noise) if base else spread * noise
        out[name] = jnp.asarray(drawn.astype(out[name].dtype))
    for name, factor in factors.items():
        out[name] = (out[name] * factor).astype(out[name].dtype)
    return out
```

```python
from collections import namedtuple
from contextlib import ExitStack, contextmanager

import concourse.bass as bass
from concourse import mybir

F32 = mybir.dt.float32
I32 = mybir.dt.int32
ALU = mybir.AluOpType
ACT = mybir.ActivationFunctionType
AX = mybir.AxisListType

P = 128
D = 1024
KC = D // P
TP = 256
NB = 8
T = TP + NB
DEPTH = 2
DFF = 2816
FC = DFF // P
HEADS = 4
SBH = 8
PAGES = 8
PHYS = 80
ADA_N = 9 * KC
ADA_HEAD = 28
EPS = 1e-6
SB_SCALE = 64 ** -0.5
ML_SCALE = P ** -0.5
NEVER = -30000.0
SLOT = 24
SLOTS = 4
SQ_, SK_, SV_, MX_, HQ_, HF_, HI_, HG_ = range(KC)
WQ, WIF, CW, CBIAS, HGG, CST, SBB2, HPN = 0, 384, 408, 412, 413, 414, 438, 440
BADA, GPRE, GPOST, SBB, N0, MLG, LPN = 0, 72, 96, 120, 128, 160, 164
STORES_A, STORES_B = 6, 4
LEVELS = 8


class Count:

    def __init__(self):
        self.n, self.i, self.per = 0, None, 0

    @contextmanager
    def loop(self, i, times, per):
        before, self.i, self.per = self.n, i, per
        yield
        assert self.n - before == per, f"{self.n - before} in a round, not {per}"
        self.i, self.n = None, before + per * times

    def __call__(self, k=1):
        now = self.n if self.i is None or not self.per else self.i * self.per + self.n
        self.last = now
        self.n += k
        return now


class Slots:

    def __init__(self):
        self.pos = 0
        self.loads, self.parts = [Count() for _ in range(SLOTS)], [Count() for _ in range(SLOTS)]

    @contextmanager
    def loop(self, i, times, parts, at=None):
        with ExitStack() as stack:
            for r in range(SLOTS):
                mine = [p for j, p in enumerate(parts) if (self.pos + j) % SLOTS == r] if at is None \
                    else (parts if r == at else [])
                stack.enter_context(self.loads[r].loop(i, times, len(mine)))
                stack.enter_context(self.parts[r].loop(i, times, sum(mine)))
            yield

    def take(self, parts, at=None):
        r = self.pos if at is None else at
        if at is None:
            self.pos = (self.pos + 1) % SLOTS
        return r, self.loads[r](), self.parts[r](parts)


class Products:

    def __init__(self):
        self.count, self.pos = Count(), 0

    def take(self, banks=4):
        b = self.pos
        self.pos = (self.pos + 1) % banks
        return b, self.count()


class Chain:

    def __init__(self, eng, sem):
        self.eng, self.sem, self.n, self.i, self.per = eng, sem, 0, None, 0

    def __call__(self, ins):
        self.n += 1
        ins.then_inc(self.sem, 1)
        self.eng.wait_ge(self.sem, self.n if self.i is None else self.i * self.per + self.n)

    @contextmanager
    def loop(self, i, times, per):
        before = self.n
        self.i, self.per = i, per
        yield
        assert self.n - before == per, f"{self.n - before} links a round, not {per}"
        self.i, self.n = None, before + per * times


def build(nc, ins, outs):
    ctx = ExitStack()
    with ctx:
        def sb(name, shape, dt=F32):
            return ctx.enter_context(nc.sbuf_tensor(name, shape, dt))

        def sems(names):
            return namedtuple("Semaphores", names)(*(ctx.enter_context(nc.semaphore(n)) for n in names.split()))

        x = sb("x", [P, KC, T])
        xn = sb("xn", [P, KC, T])
        ring = sb("ring", [P, SLOTS, SLOT * P])
        pages = sb("pages", [P, PAGES, 4 * P])
        consts = sb("consts", [P, 6, P])
        ident, ones, tri = consts[:, 0, :], consts[:, 1, :], consts[:, 2, :]
        strict01, strictneg, causalpos = consts[:, 3, :], consts[:, 4, :], consts[:, 5, :]
        hmask = sb("hmask", [P, LEVELS, P], mybir.dt.uint8)
        onerow = sb("onerow", [P, TP])
        eps = sb("eps", [P, 1])
        ctok = sb("ctok", [P, KC, NB + 1])
        ctmp = sb("ctmp", [P, KC, NB + 1])
        csil = sb("csil", [P, KC, NB + 1])
        lbl = sb("lbl", [P, DEPTH, HEADS])
        lbt = sb("lbt", [P, DEPTH * HEADS, 2])
        lbx = sb("lbx", [P, 4, HEADS])
        lbh = sb("lbh", [P, 2])
        ptab = sb("ptab", [1, NB * PAGES], I32)
        lp = sb("lp", [P, LPN])
        lp4 = sb("lp4", [4, 2 + NB])
        ada = sb("ada", [P, ADA_N, NB + 1])
        atab = sb("atab", [P, KC, NB + 1])
        gtab = sb("gtab", [P, KC, NB + 1])
        rs = sb("rs", [P, T])
        lnt = sb("lnt", [P, T])
        smpt = sb("smpt", [P, KC, NB])
        wbuf = sb("wbuf", [P, 6, T])
        w1, w2, w3, w4, w5, w6 = (wbuf[:, n, :] for n in range(6))
        sq, acc = wbuf[:, 4:6, :], w1
        fe = sb("fe", [P, 2, T])
        ft = sb("ft", [P, 2, T])
        big = sb("big", [P, 28, T])
        qkv = big[:, 0:12, :].rearrange("p (j h) t -> p j h t", j=3)
        oa, ob, oc = big[:, 12:16, :], big[:, 16:20, :], big[:, 20:24, :]
        mo = big[:, 24:28, :]
        hid = big[:, 0:FC, :]
        merged = big[:, 0:KC, :]
        gates = sb("gates", [P, 3 * KC, T])
        pj = sb("pj", [P, 9, T])
        y = pj[:, 0:KC, :]
        xp = sb("xp", [P, 3 + T])
        hp = sb("hp", [P, HPN])
        arena = sb("arena", [P, 2 * LEVELS * TP])
        e8 = arena[:, 0:LEVELS * TP].rearrange("p (v t) -> p v t", v=LEVELS)
        ql = arena[:, LEVELS * TP:2 * LEVELS * TP].rearrange("p (v t) -> p v t", v=LEVELS)
        kl = e8

        def part(at, n, *shape):
            v = arena[:, at:at + n]
            return v.rearrange("p (a b) -> p a b", a=shape[0]) if shape else v

        zp, sbt, spt = part(0, 768, 2), part(768, 768, 2), part(1536, 768, 2)
        tt8 = part(0, NB * P, NB)
        dg8 = part(NB * P, NB * P, NB)
        st8 = sb("st8", [P, NB, P])
        sn8 = sb("sn8", [P, NB, P])
        vi = sb("vi", [P, 4, P])
        sct = sb("sct", [P, 3, P])
        kdt = sb("kdt", [P, 2, P])
        hsp = sb("hsp", [P, P])
        sgt = sb("sgt", [P, 2, T])
        xc = sb("xc", [P, T])
        nbs = sb("nbs", [P, 3, NB])
        s8a, s8b, s8c = sb("s8a", [P, NB]), sb("s8b", [P, NB]), sb("s8c", [P, NB])
        ot = sb("ot", [P, T])
        gi = sb("gi", [4, T])
        gf = sb("gf", [4, T])
        r4 = arena[0:4, 3072:3072 + 3 * T].rearrange("p (a t) -> p a t", a=3)
        rows = arena[0:4, 0:TP + 3 * NB + TP]
        nrow = TP + 3 * NB + TP
        bd = pj[0:4, :, :].rearrange("p c t -> p (c t)")[:, 0:4 * nrow].rearrange("p (h n) -> p h n", h=4)
        gcol = sb("gcol", [P, 2, 4])
        qm = sb("qm", [P, NB, HEADS, 2])
        zs = part(2048, 512)
        zt = part(2560, 512)
        as_ = sb("as_", [P, 512])
        ks, vs, qs = fe[:, 0, :], fe[:, 1, :], sgt[:, 0, :]
        vk, dm, wt = part(2048, 512, 4), part(2560, 384), part(2944, 384)
        vw2 = sb("vw2", [P, 2, P])
        nst = sb("nst", [P, 1])
        sw = sb("sw", [P, 3 * NB])
        ps = ctx.enter_context(nc.psum_tensor("ps", [P, 8, 512], F32))
        M0, M1, M2, Z = 4, 5, 6, 7

        slot_full = [ctx.enter_context(nc.semaphore(f"slot_full{r}")) for r in range(SLOTS)]
        slot_done = [ctx.enter_context(nc.semaphore(f"slot_done{r}")) for r in range(SLOTS)]
        page_full = [ctx.enter_context(nc.semaphore(f"page_full{r}")) for r in range(PAGES)]
        page_free = [ctx.enter_context(nc.semaphore(f"page_free{r}")) for r in range(PAGES)]
        S = sems(
            "evac ada_evac lpar dchain achain pchain store hpar "
            "x2_ready ss_ready rs_ready xn_ready y_ready yss_ready yrs_ready e_ready "
            "sqc qmr tr zz spr suf t_ready ar av obr xcr qkv_ps qkv_sb gt gir kdr kdtp kdtr accd nnr nqr lfr ibr ho hos osq hss "
            "lvl lvc klr qlr snr pe_it act_it dve_it pool_it vir zpr l1r lnr accr xer tzr ur l2r khr "
            "dlr elr kder fsr sge rsh ger snp snm otr "
            "zpsr lnsr spsr sufs t2r asr rw1 rl1 rw2 rw3 bdr gcp gcr "
            "stg trb kqr exr dmr vwr ndr adr htr cst cev kbr cnr cnp qbr qcr dns dna sqh hbs rsb mg x_fin "
        )

        with nc.Block() as block:
            @block.sync
            def _(sp):
                for dst, src in ((consts[:], ins.consts), (tt8, ins.masks), (x[:], ins.x),
                                 (ctok[:], ins.c), (lbl[:], ins.lb), (ptab[:], ins.page_table)):
                    sp.dma_start(dst, src).then_inc(S.lpar, 16)
                sp.wait_ge(S.lpar, 96)

            @block.gpsimd
            def _(pool):
                nc.gpsimd.memset(onerow[:], 1.0)
                nc.gpsimd.memset(eps[:], EPS)
                nc.gpsimd.memset(qm[:], 0.0)
                nc.gpsimd.memset(xp[:], 0.0)

            @block.scalar
            def _(act):
                act.wait_ge(S.lpar, 96)
                nc.scalar.activation(ctmp[:], ctok[:], ACT.Exp, scale=-1.0).then_inc(S.achain, 1)
                act.wait_ge(S.dchain, 3)
                nc.scalar.activation(lbx[:, 1:3, :], lbx[:, 1:3, :], ACT.Exp).then_inc(S.achain, 1)
                act.wait_ge(S.x_fin, 1)
                nc.scalar.activation(lbx[:, 3, :], lbx[:, 3, :], ACT.Ln).then_inc(S.achain, 1)

            @block.vector
            def _(dve):
                link = Chain(dve, S.dchain)
                dve.wait_ge(S.lpar, 96)
                nc.vector.tensor_copy(hmask[:], tt8)
                link(nc.vector.tensor_tensor(lbx[:, 0, :], lbl[:, 0, :], lbl[:, 1, :], ALU.max))
                for j in range(2):
                    link(nc.vector.tensor_tensor(lbx[:, 1 + j, :], lbl[:, j, :], lbx[:, 0, :], ALU.subtract))
                link(nc.vector.memset(lbt[:, 0:HEADS, 0:1], -1e30))
                link(nc.vector.memset(lbt[:, 0:HEADS, 1:2], 0.0))
                dve.wait_ge(S.achain, 2)
                nc.vector.tensor_tensor(lbx[:, 3, :], lbx[:, 1, :], lbx[:, 2, :], ALU.add).then_inc(S.x_fin, 1)
                dve.wait_ge(S.x_fin, 1)
                dve.wait_ge(S.achain, 3)
                link(nc.vector.tensor_tensor(lbx[:, 0, :], lbx[:, 0, :], lbx[:, 3, :], ALU.add))
                for j in range(2):
                    link(nc.vector.tensor_tensor(lbt[:, HEADS:2 * HEADS, j], lbl[:, 1 - j, :],
                                                 lbx[:, 0, :], ALU.subtract))
                link(nc.vector.tensor_scalar_add(ctmp[:], ctmp[:], 1.0))
                link(nc.vector.reciprocal(ctmp[:], ctmp[:]))
                link(nc.vector.tensor_tensor(csil[:], ctmp[:], ctok[:], ALU.mult))

        clear = list(S) + slot_full + slot_done + page_full + page_free

        def clear_all():
            nc.all_engine_barrier()
            for s in clear:
                nc.sync.sem_clear(s)
            nc.all_engine_barrier()

        clear_all()

        def one_layer(block, layer):
            bds = bass.ds

            def apart(eng):
                eng.nop(nofuse=True)

            @block.sync
            def _(sp):
                slots, page_loads = Slots(), Count()
                nc.sync.dma_start(lp[:], ins.layer_par[layer]).then_inc(S.lpar, 16)
                nc.sync.dma_start(lp4[:], ins.layer_par4[layer]).then_inc(S.lpar, 16)

                def load(src, parts, at=None):
                    tiles = src.shape[-1] // P
                    r, _, before = slots.take(parts, at)
                    sp.wait_ge(slot_done[r], before + 1)
                    sp.dma_start(ring[:, r, 0:tiles * P], src).then_inc(slot_full[r], 16)

                def load_pages(pool_of_pages, b):
                    before = page_loads()
                    for j in range(PAGES):
                        page = sp.value_load(ptab[0:1, bds(b * PAGES + j, 1)], min_val=0, max_val=PHYS - 1)
                        sp.wait_ge(page_free[j], before + 1)
                        sp.dma_start(pages[:, j, :], pool_of_pages[layer, page]).then_inc(page_full[j], 16)

                with sp.Fori(0, 3) as i, slots.loop(i, 3, [1] * 4):
                    for k in range(4):
                        load(ins.w_ada[layer, i * 4 + k], 1)
                for s in (12, 13):
                    load(ins.w_ada[layer, s], 1)
                with sp.Fori(0, FC // 2) as i, slots.loop(i, FC // 2, [2, 1] * 2):
                    for k in range(2):
                        load(ins.w_ffn_in[layer, 0, i * 2 + k], 2)
                        load(ins.w_ada[layer, i * 2 + (ADA_HEAD // 2 + k)], 1)
                with sp.Fori(0, 2) as i, slots.loop(i, 2, [1] * 4):
                    for k in range(4):
                        load(ins.w_ffn_down[layer, 0, i * 4 + k], 1)
                for s in range(2):
                    load(ins.w_sq[layer, s], 2)
                with sp.Fori(0, HEADS) as i, slots.loop(i, HEADS, [3] * 4), page_loads.loop(i, HEADS, 2):
                    for k in range(3):
                        load(ins.w_a[layer, i * 4 + k], 3)
                    load_pages(ins.k_pages, i * 2)
                    load(ins.w_a[layer, i * 4 + 3], 3)
                    load_pages(ins.k_pages, i * 2 + 1)
                at = slots.pos
                with sp.Fori(0, HEADS) as i, slots.loop(i, HEADS, [2], at), page_loads.loop(i, HEADS, 2):
                    load_pages(ins.v_pages, i * 2)
                    load(ins.w_b[layer, i], 2, at)
                    load_pages(ins.v_pages, i * 2 + 1)
                for s in range(4):
                    load(ins.w_proj[layer, s], 6)
                for s in range(4):
                    load(ins.w_out[layer, s], 2)
                with sp.Fori(0, 5) as i, slots.loop(i, 5, [2] * 4):
                    for k in range(4):
                        load(ins.w_ffn_in[layer, 1, i * 4 + k], 2)
                for s in (20, 21):
                    load(ins.w_ffn_in[layer, 1, s], 2)
                with sp.Fori(0, 2) as i, slots.loop(i, 2, [1] * 4):
                    for k in range(4):
                        load(ins.w_ffn_down[layer, 1, i * 4 + k], 1)

            @block.tensor
            def _(pe):
                slots, products, adas, page_uses = Slots(), Products(), Count(), Count()
                for s in slot_done + page_free:
                    pe.sem_inc(s, 1)
                mm = nc.tensor.matmul

                def open_slot(parts, at=None):
                    r, loads, _ = slots.take(parts, at)
                    pe.wait_ge(slot_full[r], loads * 16 + 16)
                    return r

                def tile_of(r, k):
                    return ring[:, r, k * P:(k + 1) * P]

                def product(r, first, rhs, depth, banks=4):
                    b, n = products.take(banks)
                    pe.wait_ge(S.evac, n + (1 + 4 - banks))
                    for k in range(depth):
                        last = mm(ps[:, b, 0:T], tile_of(r, first + k), rhs(k), start=(k == 0), stop=(k == depth - 1))
                    last.then_inc(slot_done[r], 1)

                def ada_slot(b):
                    r = open_slot(1)
                    pe.wait_ge(S.ada_evac, adas() + 1)
                    for n in range(2):
                        for k in range(KC):
                            last = mm(ps[:, M0 + b, n * 9:n * 9 + 9], tile_of(r, n * KC + k), csil[:, k, :],
                                      start=(k == 0), stop=(k == KC - 1))
                    last.then_inc(slot_done[r], 1)

                def xn_of(k):
                    return xn[:, k, :]

                def ffn_slot():
                    r = open_slot(2)
                    product(r, 0, xn_of, KC)
                    product(r, KC, xn_of, KC)

                def pre_sums(n):
                    for k in range(KC):
                        pe.wait_ge(S.x2_ready, (n - 1) * KC + k + 1)
                        last = mm(ps[:, Z, 0:T], ones, xn[:, k, :], start=(k == 0), stop=(k == KC - 1))
                    last.then_inc(S.ss_ready, 1)

                def post_sum(n):
                    pe.wait_ge(S.accd, n * KC + 2)
                    mm(ps[:, Z, 0:T], ones, acc, start=True, stop=True).then_inc(S.yss_ready, 1)

                def down():
                    pe.wait_ge(S.evac, products.count.n + 4)
                    with pe.Fori(0, 2) as i, slots.loop(i, 2, [1] * 4), products.count.loop(i, 2, 4):
                        for k in range(4):
                            r = open_slot(1)
                            product(r, 0, lambda k: hid[:, k, :], FC)

                with pe.Fori(0, 3) as i, slots.loop(i, 3, [1] * 4), adas.loop(i, 3, 4):
                    for k in range(4):
                        ada_slot(k % 2)
                for k in range(2):
                    ada_slot(k)
                pre_sums(1)
                pe.wait_ge(S.xn_ready, 1)
                with pe.Fori(0, FC // 2) as i, slots.loop(i, FC // 2, [2, 1] * 2), \
                        products.count.loop(i, FC // 2, 4), adas.loop(i, FC // 2, 2):
                    for k in range(2):
                        ffn_slot()
                        ada_slot(k)
                down()
                post_sum(1)
                pre_sums(2)
                pe.wait_ge(S.xn_ready, 2)

                for s in range(2):
                    r = open_slot(2)
                    product(r, 0, xn_of, KC)
                    product(r, KC, xn_of, KC)

                def key_pages(b):
                    loads = page_uses()
                    for j in range(PAGES):
                        pe.wait_ge(page_full[j], loads * 16 + 16)
                        for c in range(HEADS):
                            last = mm(ps[:, Z, bds(b * 64 + (j * 8 + 2 * c), 2)], pages[:, j, c * P:(c + 1) * P],
                                      qm[:, b, c, :], start=True, stop=True)
                        last.then_inc(page_free[j], 1)

                def value_pages(b):
                    loads = page_uses()
                    for j in range(PAGES):
                        pe.wait_ge(page_full[j], loads * 16 + 16)
                        for c in range(HEADS):
                            last = mm(ps[:, 3, bds(b * 8 + 2 * c, 2)], pages[:, j, c * P:(c + 1) * P],
                                      as_[:, bds(b * 64 + (j * 8 + 2 * c), 2)], start=(j == 0 and c == 0),
                                      stop=(j == PAGES - 1 and c == HEADS - 1), skip_group_check=True)
                        last.then_inc(page_free[j], 1)

                before_a = products.count.n
                with pe.Fori(0, HEADS) as i:
                    with slots.loop(i, HEADS, [3] * 4), products.count.loop(i, HEADS, 12), page_uses.loop(i, HEADS, 2):
                        for k in range(3):
                            r = open_slot(3)
                            for n in range(3):
                                product(r, n * KC, xn_of, KC)
                        pe.wait_ge(S.dve_it, i + 1)
                        pe.wait_ge(S.rsh, i + 1)
                        pe.wait_ge(S.sqc, i + 1)
                        pe.wait_ge(S.evac, i * 12 + (before_a + 6 + 4))
                        for n, (c, t) in enumerate(((SV_, 0), (SV_, 1), (HI_, 0), (HI_, 1))):
                            last = nc.tensor.transpose(ps[:, M0, n * P:(n + 1) * P], pj[:, c, t * P:(t + 1) * P], ident)
                        last.then_inc(S.tr, 1)
                        for h in range(2):
                            a, e = 64 * h, 64 * h + 64
                            mm(ps[:, M1 + h, 0:TP], pj[a:e, SK_, 0:P], pj[a:e, SQ_, 0:TP], start=True, stop=True)
                            last = mm(ps[:, M1 + h, TP:TP + P], pj[a:e, SK_, P:TP], pj[a:e, SQ_, P:TP],
                                      start=True, stop=True)
                        last.then_inc(S.zz, 1)
                        gslot = open_slot(3)
                        product(gslot, 0, xn_of, KC)
                        pe.wait_ge(S.spr, i + 1)
                        for h in range(2):
                            mm(ps[:, M1 + h, 0:TP], tri, spt[:, h, 0:TP], start=True, stop=False)
                            mm(ps[:, M1 + h, P:TP], ones, spt[:, h, TP:TP + P], start=False, stop=True)
                            last = mm(ps[:, M1 + h, TP:TP + P], tri, spt[:, h, TP:TP + P], start=True, stop=True)
                        last.then_inc(S.suf, 1)
                        product(gslot, KC, xn_of, KC)
                        pe.wait_ge(S.vir, i + 1)
                        pe.wait_ge(S.ar, i + 1)
                        for h in range(2):
                            a, e = 64 * h, 64 * h + 64
                            mm(ps[a:e, M0, 0:TP], vi[:, 0, a:e], sbt[:, h, 0:TP], start=True, stop=False)
                            last = mm(ps[a:e, M0, P:TP], vi[:, 1, a:e], sbt[:, h, TP:TP + P], start=False, stop=True)
                        last.then_inc(S.av, 1)
                        pe.wait_ge(S.xcr, i + 1)
                        pe.wait_ge(S.hpar, i * 32 + 32)
                        mm(ps[:, M1, 0:T], hp[:, WQ:WQ + P], xc[:], start=True, stop=True)
                        mm(ps[:, M2, 0:T], hp[:, WQ + P:WQ + 2 * P], xc[:], start=True, stop=True)
                        pe.wait_ge(S.obr, i + 1)
                        mm(ps[:, M0, 0:T], hp[:, WQ + 2 * P:WQ + 3 * P], xp[:, 3:3 + T], start=True, stop=True)\
                            .then_inc(S.qkv_ps, 1)
                        product(gslot, 2 * KC, xn_of, KC)
                        pe.wait_ge(S.qkv_sb, i + 1)
                        for g in range(2):
                            for j in range(3):
                                last = mm(ps[0:4, M1 + g, 0:T], hp[:, WIF + j * 8 + 4 * g:WIF + j * 8 + 4 * g + 4],
                                          qkv[:, j, i, :], start=(j == 0), stop=(j == 2))
                        last.then_inc(S.gt, 1)
                        pe.wait_ge(S.qmr, 1)
                        key_pages(i * 2)
                        pe.wait_ge(S.qlr, i + 1)
                        pe.wait_ge(S.klr, i + 1)
                        pe.wait_ge(S.gir, i + 1)

                        def level(b, at, v):
                            for t in range(2):
                                lhs = w4[:, t * P:(t + 1) * P] if v < 0 else kl[:, v, t * P:(t + 1) * P]
                                rhs = pj[:, HQ_, t * P:(t + 1) * P] if v < 0 else ql[:, v, t * P:(t + 1) * P]
                                last = mm(ps[:, b, at + t * P:at + (t + 1) * P], lhs, rhs, start=True, stop=True)
                            return last

                        level(M1, 0, -1)
                        level(M1, TP, 0).then_inc(S.lvl, 1)
                        level(M2, 0, 1)
                        level(M2, TP, 2).then_inc(S.lvl, 1)
                        mm(ps[:, M0, 0:P], kl[:, 7, 0:P], ql[:, 7, P:TP], start=True, stop=True).then_inc(S.lvl, 1)
                        pe.wait_ge(S.lvc, i * 5 + 1)
                        level(M1, 0, 3)
                        level(M1, TP, 4).then_inc(S.lvl, 1)
                        pe.wait_ge(S.lvc, i * 5 + 2)
                        level(M2, 0, 5)
                        level(M2, TP, 6).then_inc(S.lvl, 1)
                        pe.wait_ge(S.lvc, i * 5 + 3)
                        pe.wait_ge(S.kdr, i + 1)
                        for t in range(2):
                            last = nc.tensor.transpose(ps[:, M0, t * P:(t + 1) * P], w6[:, t * P:(t + 1) * P], ident)
                        last.then_inc(S.kdtp, 1)
                        key_pages(i * 2 + 1)
                        pe.wait_ge(S.lvc, i * 5 + 5)
                        pe.wait_ge(S.kdtr, i + 1)
                        pe.wait_ge(S.snp, i + 1)
                        for n in range(2):
                            last = mm(ps[:, M1 + n, 0:512], ones, dg8[:, 4 * n:4 * n + 4, :], start=True, stop=True)
                        last.then_inc(S.ibr, 1)
                        mm(ps[:, M0, 0:TP], vi[:, 2, :], sct[:, 0:2, :], start=True, stop=False)
                        mm(ps[:, M0, P:TP], vi[:, 3, :], sct[:, 2, :], start=False, stop=True)
                        mm(ps[:, M0, 384:512], kdt[:, 0, :], vi[:, 2, :], start=True, stop=False)
                        mm(ps[:, M0, 384:512], kdt[:, 1, :], vi[:, 3, :], start=False, stop=True).then_inc(S.ho, 1)
                        pe.wait_ge(S.snr, i + 1)
                        for b in range(NB):
                            last = mm(ps[:, M1, b:b + 1], sn8[:, b, :], pj[:, HQ_, TP + b:TP + b + 1],
                                      start=True, stop=True)
                        last.then_inc(S.hos, 1)
                        pe.wait_ge(S.osq, i + 1)
                        last = mm(ps[:, M2, 0:T], ones, w2, start=True, stop=True)
                        last.then_inc(S.hss, 1)

                pe.wait_ge(S.spsr, 1)
                mm(ps[:, Z, 0:512], tri, zt, start=True, stop=False)
                out4 = ps[:, Z, :].rearrange("p (b j h) -> p b j h", b=NB, j=PAGES)
                in4 = zt.rearrange("p (b j h) -> p b j h", b=NB, j=PAGES)
                for j in range(1, PAGES):
                    last = mm(out4[:, :, 0:PAGES - j, :], ones, in4[:, :, j:PAGES, :], start=False, stop=(j == PAGES - 1))
                last.then_inc(S.sufs, 1)
                pe.wait_ge(S.rw1, 1)
                pe.wait_ge(S.dve_it, HEADS + 1)
                pe.wait_ge(S.rsh, HEADS + 1)
                for t in range(2):
                    last = nc.tensor.transpose(ps[:, M0, t * 4:t * 4 + 4], r4[:, 0, t * P:(t + 1) * P], ident[0:4, 0:4])
                last.then_inc(S.gcp, 1)
                pe.wait_ge(S.asr, 1)
                pe.wait_ge(S.gcr, 1)
                pe.wait_ge(S.evac, products.count.n + 4)
                gate_slot, products.pos = slots.pos, 0

                with pe.Fori(0, HEADS) as i:
                    with slots.loop(i, HEADS, [2], gate_slot), products.count.loop(i, HEADS, 2), \
                            page_uses.loop(i, HEADS, 2):
                        pe.wait_ge(S.stg, i * 3 + 3)
                        pe.wait_ge(S.dve_it, i + HEADS + 1)
                        for n, src in enumerate((vs, vs, ks, ks)):
                            t = n % 2
                            last = nc.tensor.transpose(ps[:, M0, n * P:(n + 1) * P], src[:, t * P:(t + 1) * P], ident)
                        last.then_inc(S.trb, 1)
                        mm(ps[:, M1, 0:TP], ks[:, 0:P], qs[:, 0:TP], start=True, stop=True)
                        mm(ps[:, M1, TP:TP + P], ks[:, P:TP], qs[:, P:TP], start=True, stop=True)
                        pe.wait_ge(S.bdr, 1)
                        mm(ps[:, M2, 0:TP + 24], ones[0:4, :], bd[:, i, 0:TP + 24], start=True, stop=True)
                        mm(ps[:, Z, 0:TP], ones[0:4, :], bd[:, i, TP + 24:], start=True, stop=True).then_inc(S.kqr, 1)
                        value_pages(i * 2)
                        r = open_slot(2, gate_slot)
                        for n in range(2):
                            product(r, n * KC, xn_of, KC, banks=2)
                        pe.wait_ge(S.vwr, i + 1)
                        for b, lhs in ((M0, None), (M1, ones)):
                            mm(ps[:, b, 0:TP], lhs if lhs is not None else vk[:, 0, :], wt[:, 0:TP], start=True, stop=False)
                            last = mm(ps[:, b, P:TP], lhs if lhs is not None else vk[:, 1, :], wt[:, TP:TP + P],
                                      start=False, stop=True)
                        last.then_inc(S.ndr, 1)
                        for t in range(2):
                            mm(ps[:, M2, 0:P], vw2[:, t, :], vk[:, 2 + t, :], start=(t == 0), stop=(t == 1))
                        for t in range(2):
                            col = (TP - 1, TP + P - 1)[t]
                            last = mm(ps[:, M2, P:P + 1], vk[:, 2 + t, :], dm[:, col:col + 1],
                                      start=(t == 0), stop=(t == 1))
                        last.then_inc(S.cst, 1)
                        pe.wait_ge(S.htr, i + 1)
                        pe.wait_ge(S.cev, i + 1)
                        pe.wait_ge(S.snp, HEADS + 2 * i + 1)
                        for n in range(2):
                            last = mm(ps[:, M1 + n, 0:512], ones, dg8[:, 4 * n:4 * n + 4, :], start=True, stop=True)
                        last.then_inc(S.kbr, 1)
                        pe.wait_ge(S.nqr, i + 1)
                        mm(ps[:, M0, 0:NB], ones, s8b[:], start=True, stop=True).then_inc(S.dns, 1)
                        pe.wait_ge(S.cnr, i + 1)
                        pe.wait_ge(S.snp, HEADS + 2 * i + 2)
                        for n in range(2):
                            last = mm(ps[:, M1 + n, 0:512], ones, dg8[:, 4 * n:4 * n + 4, :], start=True, stop=True)
                        last.then_inc(S.qbr, 1)
                        value_pages(i * 2 + 1)
                        pe.wait_ge(S.sqh, i + 1)
                        mm(ps[:, M0, 0:T], ones, w2, start=True, stop=True).then_inc(S.hbs, 1)

                products.pos = 0
                pe.wait_ge(S.dve_it, 2 * HEADS + 2)
                for s in range(4):
                    r = open_slot(6)
                    for n in range(2):
                        for br, o in enumerate((oa, ob, oc)):
                            product(r, (n * 3 + br) * 4, (lambda o: lambda k: o[:, k, :])(o), HEADS)
                pe.wait_ge(S.mg, KC)
                for s in range(4):
                    r = open_slot(2)
                    for n in range(2):
                        product(r, n * KC, lambda k: merged[:, k, :], KC)
                post_sum(2)
                pre_sums(3)
                pe.wait_ge(S.xn_ready, 3)
                with pe.Fori(0, 5) as i, slots.loop(i, 5, [2] * 4), products.count.loop(i, 5, 8):
                    for k in range(4):
                        ffn_slot()
                for k in range(2):
                    ffn_slot()
                down()
                post_sum(3)

            @block.vector
            def _(dve):
                slots, products, adas, exps, sums = Slots(), Products(), Count(), Count(), Count()
                v = nc.vector
                link = Chain(dve, S.dchain)
                dve.sem_inc(S.evac, 4)
                dve.sem_inc(S.ada_evac, 2)
                dve.sem_inc(S.accd, 2)
                dve.sem_inc(S.dve_it, 1)
                dve.wait_ge(S.lpar, 32)

                def ada_slot(b, chunk):
                    r, _, before = slots.take(1)
                    adas()
                    dve.wait_ge(slot_done[r], before + 2)
                    v.tensor_tensor(ada[:, bds(chunk, 2), :], ps[:, M0 + b, 0:18].rearrange("p (n t) -> p n t", n=2),
                                    lp[:, bds(chunk + BADA, 2)].unsqueeze(2).broadcast_to([P, 2, NB + 1]), ALU.add)\
                        .then_inc(S.ada_evac, 1)

                def ffn_slot(k, chunk):
                    r, _, before = slots.take(2)
                    bg, _ = products.take()
                    bu, _ = products.take()
                    dve.wait_ge(S.e_ready, exps() + 1)
                    t = ft[:, k % 2, :]
                    link(v.tensor_scalar_add(t, fe[:, k % 2, :], 1.0))
                    link(v.reciprocal(t, t))
                    link(v.tensor_tensor(t, ps[:, bg, 0:T], t, ALU.mult))
                    dve.wait_ge(slot_done[r], before + 3)
                    v.tensor_tensor(hid[:, chunk, :], ps[:, bu, 0:T], t, ALU.mult).then_inc(S.evac, 2)

                def sum_squares():
                    n = sums()
                    products.take()
                    dve.wait_ge(S.evac, products.count.last + (1 + 4))
                    dve.wait_ge(S.accd, n + 2)
                    v.tensor_tensor(acc, acc, sq[:, sums.n % 2, :], ALU.add).then_inc(S.accd, 1)

                def clear_sum():
                    link(v.memset(acc, 0.0))

                def tables(sub):
                    at = sub * 3 * KC
                    gp = lp[:, GPRE + sub * KC:GPRE + (sub + 1) * KC].unsqueeze(2).broadcast_to([P, KC, NB + 1])
                    gq = lp[:, GPOST + sub * KC:GPOST + (sub + 1) * KC].unsqueeze(2).broadcast_to([P, KC, NB + 1])
                    link(v.scalar_tensor_tensor(atab[:], ada[:, at + KC:at + 2 * KC, :], 1.0, gp, ALU.add, ALU.mult))
                    link(v.scalar_tensor_tensor(gtab[:], ada[:, at + 2 * KC:at + 3 * KC, :], 1.0, gq, ALU.add, ALU.mult))
                    if sub != 1:
                        link(v.tensor_scalar_mul(gtab[:], gtab[:], 0.5))

                def normalise(n):
                    sub = n - 1
                    dve.wait_ge(S.rs_ready, n)
                    link(v.tensor_tensor(xn[:], x[:], rs[:].unsqueeze(1).broadcast_to([P, KC, T]), ALU.mult))
                    smp = xn[:, :, TP:T]
                    link(v.tensor_tensor(smp, smp, atab[:, :, 1:NB + 1], ALU.mult))
                    link(v.tensor_tensor(smp, smp, ada[:, sub * 3 * KC:sub * 3 * KC + KC, 1:NB + 1], ALU.add))
                    for c in range(KC):
                        last = v.tensor_scalar(xn[:, c, 0:TP], xn[:, c, 0:TP], atab[:, c, 0:1],
                                               ada[:, sub * 3 * KC + c, 0:1], ALU.mult, ALU.add)
                    last.then_inc(S.xn_ready, 1)

                def residual(n):
                    dve.wait_ge(S.yrs_ready, n)
                    rss = rs[:, TP:T].unsqueeze(1).broadcast_to([P, KC, NB])
                    link(v.tensor_tensor(smpt[:], y[:, :, TP:T], gtab[:, :, 1:NB + 1], ALU.mult))
                    link(v.tensor_tensor(smpt[:], smpt[:], rss, ALU.mult))
                    link(v.tensor_tensor(x[:, :, TP:T], x[:, :, TP:T], smpt[:], ALU.add))
                    for c in range(KC):
                        t = ft[:, c % 2, 0:TP]
                        link(v.scalar_tensor_tensor(t, y[:, c, 0:TP], gtab[:, c, 0:1], rs[:, 0:TP], ALU.mult, ALU.mult))
                        v.tensor_tensor(x[:, c, 0:TP], x[:, c, 0:TP], t, ALU.add).then_inc(S.x_fin, 1)
                    dve.wait_ge(S.x_fin, n * KC)

                def down():
                    clear_sum()
                    with dve.Fori(0, 2) as i, slots.loop(i, 2, [1] * 4), products.count.loop(i, 2, 4), sums.loop(i, 2, 4):
                        for k in range(4):
                            slots.take(1)
                            sum_squares()

                with dve.Fori(0, 3) as i, slots.loop(i, 3, [1] * 4), adas.loop(i, 3, 4):
                    for k in range(4):
                        ada_slot(k % 2, i * 8 + 2 * k)
                for k in range(2):
                    ada_slot(k, 24 + 2 * k)
                dve.wait_ge(S.ada_evac, adas.n + 2)
                tables(0)
                normalise(1)
                with dve.Fori(0, FC // 2) as i, slots.loop(i, FC // 2, [2, 1] * 2), products.count.loop(i, FC // 2, 4), \
                        adas.loop(i, FC // 2, 2), exps.loop(i, FC // 2, 2), link.loop(i, FC // 2, 6):
                    for k in range(2):
                        ffn_slot(k, i * 2 + k)
                        ada_slot(k, i * 4 + (ADA_HEAD + 2 * k))
                down()
                residual(1)
                dve.wait_ge(S.ada_evac, adas.n + 2)
                tables(1)
                normalise(2)

                for s in range(2):
                    slots.take(2)
                    products.take()
                    products.take()
                dve.wait_ge(S.evac, products.count.n + 4)
                for h in range(2):
                    a, e = 64 * h, 64 * h + 64
                    last = v.tensor_copy(qm[a:e, :, :, h], ob[a:e, :, TP:T].rearrange("p c b -> p b c"))
                last.then_inc(S.qmr, 1)
                link(v.memset(gi[:], 0.0))
                link(v.memset(gf[:], 0.0))

                before_a = products.count.n
                with dve.Fori(0, HEADS) as i, slots.loop(i, HEADS, [3] * 4), products.count.loop(i, HEADS, 12), \
                        link.loop(i, HEADS, 30):
                    for k in range(4):
                        slots.take(3)
                        for n in range(3):
                            products.take()
                    link(v.tensor_copy(lbh[:], lbt[:, bds(layer * HEADS + i, 1), :].rearrange("p a b -> p (a b)")))
                    link(v.memset(sct[:], 0.0))
                    dve.wait_ge(S.tr, i + 1)
                    v.tensor_copy(vi[:], ps[:, M0, :].rearrange("p (n t) -> p n t", n=4)).then_inc(S.vir, 1)
                    dve.wait_ge(S.hpar, i * 32 + 32)
                    dve.wait_ge(S.zz, i + 1)
                    for h in range(2):
                        last = v.tensor_scalar(zp[:, h, :], ps[:, M1 + h, 0:384], SB_SCALE, hp[:, SBB2 + h:SBB2 + h + 1],
                                               ALU.mult, ALU.add)
                    last.then_inc(S.zpr, 1)
                    dve.wait_ge(S.l1r, i + 1)
                    link(v.scalar_tensor_tensor(w2, pj[:, HF_, :], 0.0, w1, ALU.min, ALU.subtract))
                    link(v.tensor_scalar(w2, w2, lbh[:, 1:2], None, ALU.add))
                    v.tensor_scalar(w3, w2, lbh[:, 0:1], None, ALU.subtract).then_inc(S.ur, 1)
                    v.tensor_tensor(w4, w2, pj[:, HF_, :], ALU.subtract).then_inc(S.tzr, 1)
                    def cw(j):
                        return hp[:, CW + j:CW + j + 1]
                    xcp, xcs = xc[:, 0:TP], xc[:, TP:T]
                    link(v.tensor_scalar(xcp, xp[:, 0:TP], cw(0), hp[:, CBIAS:CBIAS + 1], ALU.mult, ALU.add))
                    link(v.tensor_scalar(xcs, xp[:, 3 + TP:3 + T], cw(3), hp[:, CBIAS:CBIAS + 1], ALU.mult, ALU.add))
                    for j in range(1, 4):
                        link(v.scalar_tensor_tensor(xcp, xp[:, j:j + TP], cw(j), xcp, ALU.mult, ALU.add))
                    for j in range(3):
                        ins_ = v.scalar_tensor_tensor(xcs, hp[:, CST + 8 * j:CST + 8 * j + 8], cw(j), xcs, ALU.mult, ALU.add)
                        link(ins_) if j < 2 else ins_.then_inc(S.accr, 1)
                    dve.wait_ge(S.lnr, i + 1)
                    link(v.scalar_tensor_tensor(spt, zp, 0.0, sbt, ALU.max, ALU.add))
                    for h in range(2):
                        d = diag_blocks(spt, h)
                        last = v.tensor_tensor(d, d, over2(strict01), ALU.mult)
                    last.then_inc(S.spr, 1)
                    dve.wait_ge(S.xer, i + 1)
                    link(v.tensor_scalar_add(fe[:, 0, :], fe[:, 0, :], 1.0))
                    link(v.reciprocal(fe[:, 0, :], fe[:, 0, :]))
                    v.tensor_tensor(xc[:], xc[:], fe[:, 0, :], ALU.mult).then_inc(S.xcr, 1)
                    dve.wait_ge(S.l2r, i + 1)
                    link(v.scalar_tensor_tensor(w5, w2, lbh[:, 0:1], w3, ALU.max, ALU.add))
                    link(v.tensor_tensor_scan(w1[:, 0:TP], onerow[:], w5[:, 0:TP], 0.0, ALU.mult, ALU.add))
                    dve.wait_ge(S.suf, i + 1)
                    link(v.tensor_tensor(zp, zp, ps[:, M1:M1 + 2, 0:384], ALU.subtract))
                    for h in range(2):
                        d = diag_blocks(zp, h)
                        last = v.scalar_tensor_tensor(d, d, 0.0, over2(strictneg), ALU.min, ALU.add)
                    last.then_inc(S.t_ready, 1)
                    dve.wait_ge(S.sge, i + 1)
                    link(v.tensor_scalar_add(sgt[:], sgt[:], 1.0))
                    link(v.reciprocal(sgt[:], sgt[:]))
                    link(v.tensor_copy(mo[:, i, :], sgt[:, 1, :]))
                    link(v.tensor_tensor(sgt[:, 0, :], sgt[:, 0, :], pj[:, HG_, :], ALU.mult))
                    dve.wait_ge(S.av, i + 1)
                    v.tensor_copy(ob[:, i, 0:TP], ps[:, M0, 0:TP]).then_inc(S.obr, 1)
                    for lv in range(LEVELS):
                        half = 1 << lv
                        src = w1[:, 0:TP].rearrange("p (n w) -> p n w", w=2 * half)
                        v.tensor_tensor(e8[:, lv, :].rearrange("p (n w) -> p n w", w=2 * half), src,
                                        src[:, :, half - 1:half].broadcast_to([P, TP // (2 * half), 2 * half]), ALU.subtract)
                    v.tensor_scalar(w6[:, 0:TP], w1[:, 0:TP], w1[:, TP - 1:TP], None, ALU.subtract).then_inc(S.dlr, 1)
                    dve.wait_ge(S.gt, i + 1)
                    link(v.tensor_tensor(gi[:], gi[:], ps[0:4, M1, 0:T], ALU.add))
                    v.tensor_tensor(gf[:], gf[:], ps[0:4, M2, 0:T], ALU.add).then_inc(S.gir, 1)
                    dve.wait_ge(S.elr, i + 1)
                    v.tensor_tensor(ql, e8, pj[:, HQ_, 0:TP].unsqueeze(1).broadcast_to([P, LEVELS, TP]), ALU.mult)\
                        .then_inc(S.qlr, 1)
                    dve.wait_ge(S.kder, i + 1)
                    dve.wait_ge(S.khr, i + 1)
                    v.tensor_tensor(w6[:, 0:TP], w6[:, 0:TP], w4[:, 0:TP], ALU.mult).then_inc(S.kdr, 1)

                    def pick(bank, at, mask):
                        return v.copy_predicated(sct[:, 0:3:2, :], over2(hmask[:, mask, :]),
                                                 ps[:, bank, at:at + TP].rearrange("p (t q) -> p t q", t=2))

                    for n, (bank, first) in enumerate(((M1, 0), (M2, 2), (M0, None), (M1, 4), (M2, 6))):
                        dve.wait_ge(S.lvl, i * 5 + n + 1)
                        if first is None:
                            v.tensor_copy(sct[:, 1, :], ps[:, M0, 0:P]).then_inc(S.lvc, 1)
                        else:
                            apart(dve)
                            link(pick(bank, 0, first))
                            apart(dve)
                            pick(bank, TP, first + 1).then_inc(S.lvc, 1)
                        dve.wait_ge(S.lvc, i * 5 + n + 1)
                    dve.wait_ge(S.kdtp, i + 1)
                    v.tensor_copy(kdt[:], ps[:, M0, 0:TP].rearrange("p (t q) -> p t q", t=2)).then_inc(S.kdtr, 1)
                    dve.wait_ge(S.ibr, i + 1)
                    dve.wait_ge(S.klr, i + 1)
                    link(v.tensor_tensor(tt8, ps[:, M1:M1 + 2, :].rearrange("p a (b k) -> p (a b) k", k=P),
                                         w4[:, TP:T].unsqueeze(2).broadcast_to([P, NB, P]), ALU.mult))
                    dve.wait_ge(S.snm, i + 1)
                    v.tensor_tensor(sn8[:], sn8[:], tt8, ALU.add).then_inc(S.snr, 1)
                    dve.wait_ge(S.evac, i * 12 + (before_a + 12 + 4))
                    g4 = gates[:, bds(i * 4, 4), :]
                    link(v.tensor_scalar_add(g4, g4, 1.0))
                    apart(dve)
                    link(v.reciprocal(g4, g4))
                    dve.wait_ge(S.rsh, i + 2)
                    link(v.scalar_tensor_tensor(ot[:], ot[:], hp[:, HGG:HGG + 1], rs[:], ALU.mult, ALU.mult))
                    v.tensor_tensor(oa[:, i, :], ot[:], sgt[:, 0, :], ALU.mult).then_inc(S.dve_it, 1)
                    dve.wait_ge(S.dve_it, i + 2)

                dve.wait_ge(page_free[PAGES - 1], NB + 1)
                sbb = lp[:, SBB:SBB + SBH].unsqueeze(1).broadcast_to([P, NB * PAGES, SBH])
                z3 = zs.rearrange("p (n h) -> p n h", h=SBH)
                v.scalar_tensor_tensor(z3, ps[:, Z, :].rearrange("p (n h) -> p n h", h=SBH), SB_SCALE, sbb, ALU.mult, ALU.add)\
                    .then_inc(S.zpsr, 1)
                link(v.tensor_scalar(gf[:], gf[:], lp4[:, 1:2], None, ALU.add))
                link(v.tensor_scalar(gi[:], gi[:], lp4[:, 0:1], None, ALU.add))
                v.nop().then_inc(S.rl1, 1)
                dve.wait_ge(S.lnsr, 1)
                v.scalar_tensor_tensor(zt, zs, 0.0, zt, ALU.max, ALU.add).then_inc(S.spsr, 1)
                dve.wait_ge(S.rl1, 2)
                link(v.scalar_tensor_tensor(gf[:], gf[:], 0.0, r4[:, 1, :], ALU.min, ALU.subtract))
                link(v.tensor_tensor_scan(r4[:, 1, 0:TP], onerow[0:4, :], gf[:, 0:TP], 0.0, ALU.mult, ALU.add))
                v.tensor_tensor(r4[:, 0, 0:TP], gi[:, 0:TP], r4[:, 1, 0:TP], ALU.subtract).then_inc(S.rw1, 1)
                dve.wait_ge(S.rw1, 1)
                link(v.tensor_tensor_scan(rows[:, 0:TP], onerow[0:4, :], r4[:, 0, 0:TP], 0.0, ALU.mult, ALU.max))
                link(v.tensor_tensor(rows[:, TP + 24:], rows[:, 0:TP], r4[:, 1, 0:TP], ALU.add))
                a, ms, its = r4[:, 2, 0:8], r4[:, 2, 8:16], gi[:, TP:T]
                link(v.tensor_tensor(a, gf[:, TP:T], lp4[:, 2:10], ALU.add))
                link(v.tensor_tensor(ms, a, its, ALU.max))
                v.tensor_tensor(rows[:, TP:TP + 8], its, ms, ALU.subtract)
                v.tensor_tensor(rows[:, TP + 8:TP + 16], a, ms, ALU.subtract)
                v.tensor_scalar_mul(rows[:, TP + 16:TP + 24], ms, -1.0).then_inc(S.rw2, 1)
                dve.wait_ge(S.sufs, 1)
                v.tensor_tensor(zs, zs, ps[:, Z, :], ALU.subtract).then_inc(S.t2r, 1)
                dve.wait_ge(S.rw3, 1)
                v.tensor_tensor(bd, rows.unsqueeze(1).broadcast_to([4, 4, nrow]),
                                consts[0:4, 0, 0:4].unsqueeze(2).broadcast_to([4, 4, nrow]), ALU.mult).then_inc(S.bdr, 1)
                dve.wait_ge(S.gcp, 1)
                v.tensor_copy(gcol[:], ps[:, M0, 0:8].rearrange("p (t h) -> p t h", t=2)).then_inc(S.gcr, 1)
                dve.wait_ge(S.gcr, 1)

                at, products.pos = slots.pos, 0
                before_b = products.count.n
                with dve.Fori(0, HEADS) as i, slots.loop(i, HEADS, [2], at), products.count.loop(i, HEADS, 2), \
                        link.loop(i, HEADS, 14):
                    slots.take(2, at)
                    products.take(2)
                    products.take(2)
                    dve.wait_ge(S.trb, i + 1)
                    link(v.tensor_copy(vk, ps[:, M0, :].rearrange("p (n t) -> p n t", n=4)))
                    dve.wait_ge(S.kqr, i + 1)
                    v.tensor_scalar(dm[:, 0:TP], ps[:, M2, 0:TP], gcol[:, 0, bds(i, 1)], 0.0, ALU.subtract, ALU.max)
                    v.tensor_scalar(dm[:, TP:TP + P], ps[:, M2, P:TP], gcol[:, 1, bds(i, 1)], 0.0, ALU.subtract, ALU.max)
                    link(v.tensor_copy(sw[:], ps[:, M2, TP:TP + 24]))
                    d = dm.rearrange("p (n t) -> p n t", t=P)[:, 0:3:2, :]
                    v.tensor_tensor(d, d, over2(causalpos), ALU.add).then_inc(S.exr, 1)
                    smp = slice(TP, T)
                    wv, dec = sw[:, 0:8], sw[:, 8:16]
                    link(v.tensor_tensor(s8a[:], vs[:, smp], wv, ALU.mult))
                    link(v.tensor_tensor(s8c[:], lp[:, bds(i * NB + N0, NB)], dec, ALU.mult))
                    link(v.tensor_tensor(s8b[:], ks[:, smp], wv, ALU.mult))
                    v.tensor_tensor(s8c[:], s8c[:], s8b[:], ALU.add).then_inc(S.nnr, 1)
                    dve.wait_ge(S.nnr, i + 1)
                    v.tensor_tensor(s8b[:], s8c[:], qs[:, smp], ALU.mult).then_inc(S.nqr, 1)
                    dve.wait_ge(S.dmr, i + 1)
                    v.tensor_tensor(wt, dm, ps[:, M1, 0:384], ALU.mult)
                    v.tensor_scalar(vw2[:, 0, :], vk[:, 0, :], dm[:, TP - 1:TP], None, ALU.mult)
                    v.tensor_scalar(vw2[:, 1, :], vk[:, 1, :], dm[:, TP + P - 1:TP + P], None, ALU.mult)\
                        .then_inc(S.vwr, 1)
                    dve.wait_ge(S.adr, i + 1)
                    link(v.tensor_tensor(w1[:, 0:TP], w1[:, 0:TP], w3[:, 0:TP], ALU.max))
                    link(v.reciprocal(w1[:, 0:TP], w1[:, 0:TP]))
                    v.tensor_tensor(ot[:, 0:TP], ps[:, M0, 0:TP], w1[:, 0:TP], ALU.mult).then_inc(S.htr, 1)
                    dve.wait_ge(S.kbr, i + 1)
                    bank2 = ps[:, M1:M1 + 2, :].rearrange("p a (b k) -> p (a b) k", k=P)
                    link(v.tensor_tensor(tt8, bank2, s8a[:].unsqueeze(2).broadcast_to([P, NB, P]), ALU.mult))
                    dve.wait_ge(S.cnp, i + 1)
                    v.tensor_tensor(sn8[:], sn8[:], tt8, ALU.add).then_inc(S.cnr, 1)
                    dve.wait_ge(S.cnr, i + 1)
                    dve.wait_ge(S.qbr, i + 1)
                    link(v.tensor_tensor(tt8, sn8[:], bank2, ALU.mult))
                    link(v.tensor_reduce(w3[:, smp], tt8, AX.X, ALU.add))
                    dve.wait_ge(S.dna, i + 1)
                    link(v.tensor_tensor(w1[:, smp], w1[:, smp], sw[:, 16:24], ALU.max))
                    link(v.reciprocal(w1[:, smp], w1[:, smp]))
                    v.tensor_tensor(ot[:, smp], w3[:, smp], w1[:, smp], ALU.mult).then_inc(S.otr, 1)
                    dve.wait_ge(S.evac, i * 2 + (before_b + 2 + 4))
                    g2 = gates[:, bds(i * 2 + 16, 2), :]
                    link(v.tensor_scalar_add(g2, g2, 1.0))
                    apart(dve)
                    v.reciprocal(g2, g2)
                    dve.wait_ge(S.rsb, i + 1)
                    link(v.scalar_tensor_tensor(ot[:], ot[:], lp[:, bds(i + MLG, 1)], rs[:], ALU.mult, ALU.mult))
                    v.tensor_tensor(oc[:, i, :], ot[:], mo[:, i, :], ALU.mult).then_inc(S.dve_it, 1)
                    dve.wait_ge(S.dve_it, i + HEADS + 2)

                dve.wait_ge(page_free[PAGES - 1], 2 * NB + 1)
                for h in range(2):
                    a, e = 64 * h, 64 * h + 64
                    last = v.tensor_copy(ob[a:e, :, TP:T],
                                         ps[a:e, 3, 0:64].rearrange("p (b c h) -> p c b h", c=HEADS, h=2)[:, :, :, h])
                last.then_inc(S.dve_it, 1)
                products.pos = 0
                for s in range(4):
                    r, _, before = slots.take(6)
                    for n in range(2):
                        c = s * 2 + n
                        for br in range(3):
                            b, count = products.take()
                            dve.wait_ge(slot_done[r], before + n * 3 + br + 2)
                            dst = merged[:, c, :] if br == 0 else ft[:, br - 1, :]
                            v.tensor_tensor(dst, ps[:, b, 0:T], gates[:, br * KC + c, :], ALU.mult).then_inc(S.evac, 1)
                            dve.wait_ge(S.evac, count + 5)
                            if br:
                                ins_ = v.tensor_tensor(merged[:, c, :], merged[:, c, :], dst, ALU.add)
                                if br == 2:
                                    ins_.then_inc(S.mg, 1)
                                    dve.wait_ge(S.mg, c + 1)
                                else:
                                    link(ins_)
                clear_sum()
                for s in range(4):
                    slots.take(2)
                    for n in range(2):
                        sum_squares()
                residual(2)
                tables(2)
                normalise(3)
                with dve.Fori(0, 5) as i, slots.loop(i, 5, [2] * 4), products.count.loop(i, 5, 8), exps.loop(i, 5, 4), \
                        link.loop(i, 5, 12):
                    for k in range(4):
                        ffn_slot(k, i * 4 + k)
                for k in range(2):
                    ffn_slot(k, 20 + k)
                down()
                residual(3)

            @block.scalar
            def _(act):
                slots, products, exps, sums = Slots(), Products(), Count(), Count()
                link = Chain(act, S.achain)
                A = nc.scalar.activation
                act.sem_inc(S.rsh, 1)
                act.sem_inc(S.store, 16)

                def squares(n):
                    for c in range(KC):
                        if n > 1:
                            act.wait_ge(S.x_fin, (n - 2) * KC + c + 1)
                        A(xn[:, c, :], x[:, c, :], ACT.Square).then_inc(S.x2_ready, 1)

                def rsqrt(bank, width):
                    link(A(lnt[:], ps[:, bank, 0:T], ACT.Ln, scale=1.0 / width, bias=eps[:]))
                    return A(rs[:], lnt[:], ACT.Exp, scale=-0.5)

                def pre(n):
                    squares(n)
                    act.wait_ge(S.ss_ready, n)
                    rsqrt(Z, D).then_inc(S.rs_ready, 1)

                def post(n):
                    act.wait_ge(S.yss_ready, n)
                    rsqrt(Z, D).then_inc(S.yrs_ready, 1)

                def ffn_slot(k):
                    r, _, before = slots.take(2)
                    b, _ = products.take()
                    products.take()
                    exps()
                    act.wait_ge(slot_done[r], before + 2)
                    A(fe[:, k % 2, :], ps[:, b, 0:T], ACT.Exp, scale=-1.0).then_inc(S.e_ready, 1)

                def y_chunk(r, done, c):
                    n = sums()
                    b, _ = products.take()
                    act.wait_ge(slot_done[r], done)
                    act.wait_ge(S.accd, n + 1)
                    A(y[:, c, :], ps[:, b, 0:T], ACT.Copy)
                    A(sq[:, sums.n % 2, :], ps[:, b, 0:T], ACT.Square).then_inc(S.evac, 1)

                def down():
                    with act.Fori(0, 2) as i, slots.loop(i, 2, [1] * 4), products.count.loop(i, 2, 4), sums.loop(i, 2, 4):
                        for k in range(4):
                            r, _, before = slots.take(1)
                            y_chunk(r, before + 2, i * 4 + k)

                for k in range(14):
                    slots.take(1)
                pre(1)
                with act.Fori(0, FC // 2) as i, slots.loop(i, FC // 2, [2, 1] * 2), products.count.loop(i, FC // 2, 4), \
                        exps.loop(i, FC // 2, 2):
                    for k in range(2):
                        ffn_slot(k)
                        slots.take(1)
                down()
                post(1)
                pre(2)

                def evac(r, done, dst, exp=False):
                    b, _ = products.take()
                    act.wait_ge(slot_done[r], done)
                    A(dst, ps[:, b, 0:T], ACT.Exp if exp else ACT.Copy, scale=-1.0 if exp else 1.0).then_inc(S.evac, 1)

                for s in range(2):
                    r, _, before = slots.take(2)
                    for n in range(2):
                        evac(r, before + 2 + n, ob[:, s * 2 + n, :])

                def softplus_tail(t, src):
                    link(A(t, src, ACT.Abs))
                    link(A(t, t, ACT.Exp, scale=-1.0))
                    return A(t, t, ACT.Ln, bias=1.0)

                before_a = products.count.n
                with act.Fori(0, HEADS) as i, slots.loop(i, HEADS, [3] * 4), products.count.loop(i, HEADS, 12), \
                        link.loop(i, HEADS, 10):
                    act.wait_ge(S.dve_it, i + 1)
                    act.wait_ge(S.pool_it, i + 1)
                    act.dma_start(hp[:], ins.head_par[layer, i]).then_inc(S.hpar, 16)
                    act.dma_start(st8[:], ins.hgrn[layer, i]).then_inc(S.hpar, 16)
                    dests = [pj[:, SK_, :], pj[:, SV_, :], xp[:, 3:3 + T], pj[:, HQ_, :], pj[:, HF_, :], pj[:, HI_, :],
                             pj[:, HG_, :], sgt[:, 1, :], gates[:, i * 4, :]]
                    for k in range(3):
                        r, _, before = slots.take(3)
                        for n in range(3):
                            evac(r, before + 2 + n, dests[3 * k + n], exp=3 * k + n >= 7)
                    act.wait_ge(S.evac, i * 12 + (before_a + 7 + 4))
                    act.dma_start(outs.k[layer, :, i, :], pj[:, SK_, :]).then_inc(S.store, 16)
                    act.dma_start(outs.v[layer, :, i, :], pj[:, SV_, :]).then_inc(S.store, 16)
                    act.dma_start(outs.conv_p[layer, i], xp[:, TP:TP + 3]).then_inc(S.store, 16)
                    softplus_tail(w1, pj[:, HF_, :]).then_inc(S.l1r, 1)
                    act.wait_ge(S.pchain, i + 1)
                    act.dma_start(outs.conv_s[layer, i], nbs[:].rearrange("p j b -> p (j b)")).then_inc(S.store, 16)
                    act.wait_ge(S.zpr, i + 1)
                    softplus_tail(sbt, zp).then_inc(S.lnr, 1)
                    act.wait_ge(S.evac, i * 12 + (before_a + 8 + 4))
                    A(sgt[:, 0, :], pj[:, HG_, :], ACT.Exp, scale=-1.0).then_inc(S.sge, 1)
                    act.wait_ge(S.accr, i + 1)
                    A(fe[:, 0, :], xc[:], ACT.Exp, scale=-1.0).then_inc(S.xer, 1)
                    act.wait_ge(S.ur, i + 1)
                    softplus_tail(w3, w3).then_inc(S.l2r, 1)
                    r, _, before = slots.take(3)
                    evac(r, before + 2, gates[:, i * 4 + 1, :], exp=True)
                    act.wait_ge(S.tzr, i + 1)
                    A(w4, w4, ACT.Exp).then_inc(S.khr, 1)
                    act.wait_ge(S.t_ready, i + 1)
                    A(sbt, zp, ACT.Exp).then_inc(S.ar, 1)
                    evac(r, before + 3, gates[:, i * 4 + 2, :], exp=True)
                    act.wait_ge(S.qkv_ps, i + 1)
                    for j, b in enumerate((M1, M2, M0)):
                        last = A(qkv[:, j, i, :], ps[:, b, 0:T], ACT.Copy)
                    last.then_inc(S.qkv_sb, 1)
                    act.wait_ge(S.dlr, i + 1)
                    link(A(e8, e8, ACT.Abs))
                    A(e8, e8, ACT.Exp, scale=-1.0).then_inc(S.elr, 1)
                    A(w6[:, 0:TP], w6[:, 0:TP], ACT.Exp, scale=-1.0).then_inc(S.kder, 1)
                    A(s8a[:], w5[:, TP:T], ACT.Exp).then_inc(S.fsr, 1)
                    evac(r, before + 4, gates[:, i * 4 + 3, :], exp=True)
                    act.wait_ge(S.ho, i + 1)
                    A(ot[:, 0:TP], ps[:, M0, 0:TP], ACT.Copy)
                    link(A(hsp[:], ps[:, M0, 384:512], ACT.Copy))
                    act.dma_start(outs.hgrn_p[layer, i], hsp[:]).then_inc(S.store, 16)
                    act.wait_ge(S.snr, i + 1)
                    act.dma_start(outs.hgrn_s[layer, i], sn8[:].rearrange("p b k -> p (b k)")).then_inc(S.store, 16)
                    act.wait_ge(S.hos, i + 1)
                    link(A(ot[:, TP:T], ps[:, M1, 0:NB], ACT.Copy))
                    A(w2, ot[:], ACT.Square).then_inc(S.osq, 1)
                    act.wait_ge(S.hss, i + 1)
                    rsqrt(M2, P).then_inc(S.rsh, 1)
                    act.wait_ge(S.store, i * (16 * STORES_A) + 16 * (STORES_A + 1))

                act.wait_ge(S.zpsr, 1)
                softplus_tail(zt, zs).then_inc(S.lnsr, 1)
                act.wait_ge(S.rl1, 1)
                softplus_tail(r4[:, 1, :], gf[:]).then_inc(S.rl1, 1)
                act.wait_ge(S.rw2, 1)
                A(rows[:, TP:TP + 24], rows[:, TP:TP + 24], ACT.Exp).then_inc(S.rw3, 1)
                act.dma_start(outs.m_p[layer], rows[:, 2 * TP + 23:2 * TP + 24]).then_inc(S.store, 16)
                act.dma_start(outs.m_s[layer], r4[:, 2, 8:16]).then_inc(S.store, 16)
                act.wait_ge(S.t2r, 1)
                A(as_[:], zs, ACT.Exp).then_inc(S.asr, 1)
                act.wait_ge(S.store, 16 * (STORES_A * HEADS + 3))

                at, products.pos = slots.pos, 0
                with act.Fori(0, HEADS) as i, slots.loop(i, HEADS, [2], at), products.count.loop(i, HEADS, 2), \
                        link.loop(i, HEADS, 1):
                    act.wait_ge(S.dve_it, i + HEADS + 1)
                    act.dma_start(st8[:], ins.ml_c[layer, i]).then_inc(S.hpar, 16)
                    A(ks, qkv[:, 1, i, :], ACT.Copy, scale=ML_SCALE).then_inc(S.stg, 1)
                    act.wait_ge(S.exr, i + 1)
                    A(dm, dm, ACT.Exp, scale=-1.0).then_inc(S.dmr, 1)
                    r, _, before = slots.take(2, at)
                    for n in range(2):
                        b, _ = products.take(2)
                        act.wait_ge(slot_done[r], before + 2 + n)
                        A(gates[:, i * 2 + (16 + n), :], ps[:, b, 0:T], ACT.Exp, scale=-1.0).then_inc(S.evac, 1)
                    act.wait_ge(S.nnr, i + 1)
                    act.dma_start(outs.n_s[layer, :, i, :], s8c[:]).then_inc(S.store, 16)
                    act.wait_ge(S.ndr, i + 1)
                    A(w1[:, 0:TP], ps[:, M1, 0:TP], ACT.Abs)
                    A(w3[:, 0:TP], ps[:, Z, 0:TP], ACT.Exp, scale=-1.0).then_inc(S.adr, 1)
                    act.wait_ge(S.cst, i + 1)
                    A(hsp[:], ps[:, M2, 0:P], ACT.Copy)
                    A(nst[:], ps[:, M2, P:P + 1], ACT.Copy).then_inc(S.cev, 1)
                    act.wait_ge(S.cev, i + 1)
                    act.dma_start(outs.c_p[layer, i], hsp[:]).then_inc(S.store, 16)
                    act.dma_start(outs.n_p[layer, i], nst[:]).then_inc(S.store, 16)
                    act.wait_ge(S.dns, i + 1)
                    A(w1[:, TP:T], ps[:, M0, 0:NB], ACT.Abs).then_inc(S.dna, 1)
                    act.wait_ge(S.cnr, i + 1)
                    act.dma_start(outs.c_s[layer, i], sn8[:].rearrange("p b k -> p (b k)")).then_inc(S.store, 16)
                    act.wait_ge(S.otr, i + 1)
                    A(w2, ot[:], ACT.Square).then_inc(S.sqh, 1)
                    act.wait_ge(S.hbs, i + 1)
                    rsqrt(M0, P).then_inc(S.rsb, 1)
                    act.wait_ge(S.store, i * (16 * STORES_B) + 16 * (STORES_A * HEADS + 3 + STORES_B))

                products.pos = 0
                for s in range(4):
                    slots.take(6)
                    for n in range(6):
                        products.take()
                for s in range(4):
                    r, _, before = slots.take(2)
                    for n in range(2):
                        y_chunk(r, before + 2 + n, s * 2 + n)
                post(2)
                pre(3)
                with act.Fori(0, 5) as i, slots.loop(i, 5, [2] * 4), products.count.loop(i, 5, 8), exps.loop(i, 5, 4):
                    for k in range(4):
                        ffn_slot(k)
                for k in range(2):
                    ffn_slot(k)
                down()
                post(3)

            @block.gpsimd
            def _(pool):
                g = nc.gpsimd
                pool.sem_inc(S.pool_it, 1)
                identb = consts[:, 0:1, :].broadcast_to([P, NB, P])
                before_a = 2 * FC + KC + HEADS

                def diagonal(src):
                    return g.tensor_tensor(dg8, identb, src.unsqueeze(2).broadcast_to([P, NB, P]), ALU.mult)

                with pool.Fori(0, HEADS) as i:
                    pool.wait_ge(S.dve_it, i + 1)
                    pool.wait_ge(S.store, i * (16 * STORES_A) + 16)
                    pool.wait_ge(S.evac, i * 12 + (before_a + 4))
                    apart(pool)
                    g.tensor_copy(pj[:, SQ_, :], ob[:, i, :]).then_inc(S.sqc, 1)
                    pool.wait_ge(S.hpar, i * 32 + 32)
                    pool.wait_ge(S.evac, i * 12 + (before_a + 3 + 4))
                    apart(pool)
                    g.tensor_copy(nbs[:, 0:2, :], hp[:, CST + 8:CST + 24].rearrange("p (j b) -> p j b", j=2))
                    g.tensor_copy(nbs[:, 2, :], xp[:, 3 + TP:3 + T]).then_inc(S.pchain, 1)
                    pool.wait_ge(S.fsr, i + 1)
                    g.tensor_tensor(sn8[:], st8[:], s8a[:].unsqueeze(2).broadcast_to([P, NB, P]), ALU.mult)\
                        .then_inc(S.snm, 1)
                    pool.wait_ge(S.khr, i + 1)
                    pool.wait_ge(S.qlr, i + 1)
                    g.tensor_tensor(kl, e8, w4[:, 0:TP].unsqueeze(1).broadcast_to([P, LEVELS, TP]), ALU.mult)\
                        .then_inc(S.klr, 1)
                    pool.wait_ge(S.lvc, i * 5 + 5)
                    diagonal(pj[:, HI_, TP:T]).then_inc(S.snp, 1)
                    pool.wait_ge(S.snp, i + 1)
                    pool.sem_inc(S.pool_it, 1)

                with pool.Fori(0, HEADS) as i:
                    pool.wait_ge(S.dve_it, i + (HEADS + 1))
                    pool.wait_ge(S.store, i * (16 * STORES_B) + 16 * (STORES_A * HEADS + 3))
                    g.tensor_copy(vs, qkv[:, 2, i, :]).then_inc(S.stg, 1)
                    g.tensor_copy(qs, qkv[:, 0, i, :]).then_inc(S.stg, 1)
                    pool.wait_ge(S.stg, i * 3 + 3)
                    diagonal(ks[:, TP:T]).then_inc(S.snp, 1)
                    pool.wait_ge(S.hpar, i * 16 + (32 * HEADS + 16))
                    pool.wait_ge(S.exr, i + 1)
                    g.tensor_tensor(sn8[:], st8[:], sw[:, 8:16].unsqueeze(2).broadcast_to([P, NB, P]), ALU.mult)\
                        .then_inc(S.cnp, 1)
                    pool.wait_ge(S.kbr, i + 1)
                    diagonal(qs[:, TP:T]).then_inc(S.snp, 1)

        with nc.Fori(0, DEPTH) as layer:
            with nc.Block() as block:
                one_layer(block, layer)
            clear_all()

        with nc.Block() as block:
            @block.sync
            def _(sp):
                sp.dma_start(outs.y, x[:]).then_inc(S.store, 16)
                sp.wait_ge(S.store, 16)


def over2(mask):
    return mask.unsqueeze(1).broadcast_to([P, 2, P])


def diag_blocks(t, h):
    return t[:, h, :].rearrange("p (n t) -> p n t", t=P)[:, 0:3:2, :]


def kernel(**inputs):
    import numpy as np
    import concourse.bacc as bacc
    from concourse.bass_utils import run_bass_kernel_spmd

    a = {k: np.asarray(v) for k, v in inputs.items()}

    def tokens(prompt, sample):
        t = np.concatenate([prompt.reshape(-1, D), sample.reshape(-1, D)], 0)
        return t.T.reshape(KC, P, -1).transpose(1, 0, 2)

    def tiles(w, per_slot):
        *lead, k, n = w.shape
        n_lead = len(lead)
        t = w.reshape(*lead, k // P, P, n // P // per_slot, per_slot, P)
        ax = list(range(n_lead))
        t = t.transpose(*ax, n_lead + 2, n_lead + 1, n_lead + 3, n_lead, n_lead + 4)
        return t.reshape(*lead, n // P // per_slot, P, per_slot * (k // P) * P)

    def chunk_cols(v, last=False):
        return v.reshape(DEPTH, -1, P).transpose(0, 2, 1)

    w_in = a["w_in"].reshape(DEPTH, D, -1, P)
    first = dict(hq=0, hf=4, hi=8, hg=12, sq=16, sk=20, sv=24, mx=28, mo=32, ga=36)
    g0 = first["ga"]
    order_a, order_b = [], []
    for i in range(HEADS):
        order_a += [first[k] + i for k in ("sk", "sv", "mx", "hq", "hf", "hi", "hg", "mo")] + \
                   [g0 + 4 * i + j for j in range(4)]
        order_b += [g0 + 16 + 2 * i + j for j in range(2)]

    def in_cols(order):
        return w_in[:, :, order, :].reshape(DEPTH, D, len(order) * P)

    ffn = a["w_ffn_in"].reshape(DEPTH, 2, D, 2, FC, P).transpose(0, 1, 2, 4, 3, 5).reshape(DEPTH, 2, D, 2 * DFF)
    proj = np.stack([a["w_hg_proj"], a["w_sb_proj"], a["w_ml_proj"]], 1)
    proj = proj.reshape(DEPTH, 3, HEADS, P, 4, 2, P).transpose(0, 4, 3, 5, 1, 2, 6).reshape(DEPTH, 4, P, 24 * P)

    layer_par = np.zeros((DEPTH, P, LPN), np.float32)
    layer_par[:, :, BADA:BADA + ADA_N] = chunk_cols(a["b_ada"])
    layer_par[:, :, GPRE:GPRE + 24] = chunk_cols(a["g_pre"].reshape(DEPTH, -1))
    layer_par[:, :, GPOST:GPOST + 24] = chunk_cols(a["g_post"].reshape(DEPTH, -1))
    layer_par[:, :, SBB:SBB + SBH] = a["sb_bias"][:, None, :]
    layer_par[:, :, N0:N0 + 32] = a["state_mlstm_n"].transpose(1, 3, 2, 0).reshape(DEPTH, P, 32)
    layer_par[:, :, MLG:MLG + 4] = chunk_cols(a["ml_gain"])
    layer_par4 = np.zeros((DEPTH, 4, 2 + NB), np.float32)
    layer_par4[:, :, 0] = a["ml_b_if"][:, 0:4]
    layer_par4[:, :, 1] = a["ml_b_if"][:, 4:8]
    layer_par4[:, :, 2:] = a["state_mlstm_m"].transpose(1, 2, 0)
    head_par = np.zeros((DEPTH, HEADS, P, HPN), np.float32)
    for j, k in enumerate(("ml_wq", "ml_wk", "ml_wv")):
        head_par[:, :, :, WQ + j * P:WQ + (j + 1) * P] = a[k]
    head_par[:, :, :, WIF:WIF + 24] = a["ml_w_if"].reshape(DEPTH, 3, HEADS, P, 8).transpose(0, 2, 3, 1, 4)\
        .reshape(DEPTH, HEADS, P, 24)
    head_par[:, :, :, CW:CW + 4] = a["ml_conv_w"].reshape(DEPTH, 4, HEADS, P).transpose(0, 2, 3, 1)
    head_par[:, :, :, CBIAS] = a["ml_conv_b"].reshape(DEPTH, HEADS, P)
    head_par[:, :, :, HGG] = a["hg_gain"].reshape(DEPTH, HEADS, P)
    head_par[:, :, :, CST:CST + 24] = a["state_mlstm_conv"].reshape(NB, DEPTH, 3, HEADS, P)\
        .transpose(1, 3, 4, 2, 0).reshape(DEPTH, HEADS, P, 24)
    head_par[:, :, :, SBB2:SBB2 + 2] = a["sb_bias"].reshape(DEPTH, HEADS, 1, 2)

    r = np.arange(P)
    k, q = r[:, None], r[None, :]
    consts = np.stack([k == q, k + q >= 0, k >= q, k < q], 1).astype(np.float32)
    consts = np.concatenate([consts, np.where(k < q, 0.0, NEVER)[:, None], np.where(k > q, -NEVER, 0.0)[:, None]], 1)
    masks = [k == q]
    for lv in range(LEVELS - 1):
        half = 1 << lv
        masks.append((k // (2 * half) == q // (2 * half)) & (k % (2 * half) < half) & (q % (2 * half) >= half))
    masks = np.stack(masks, 1)

    feeds = dict(
        consts=consts.astype(np.float32), masks=masks.astype(np.float32),
        x=tokens(a["x_prompt"], a["x_sample"]), c=tokens(a["c_prompt"], a["c_sample"]),
        lb=a["hg_lb_logits"].reshape(DEPTH, HEADS, P).transpose(2, 0, 1),
        page_table=a["page_table"].reshape(1, NB * PAGES),
        w_ada=tiles(a["w_ada"], 2), w_ffn_in=tiles(ffn, 2), w_ffn_down=tiles(a["w_ffn_down"], 1),
        w_sq=tiles(in_cols([first["sq"] + i for i in range(4)]), 2),
        w_a=tiles(in_cols(order_a), 3), w_b=tiles(in_cols(order_b), 2), w_proj=proj, w_out=tiles(a["w_out"], 2),
        k_pages=a["cache_sb_k"].reshape(PHYS, DEPTH, P, HEADS, P).transpose(1, 0, 4, 3, 2).reshape(DEPTH, PHYS, P, 512),
        v_pages=a["cache_sb_v"].reshape(PHYS, DEPTH, P, 512).transpose(1, 0, 2, 3),
        layer_par=layer_par, layer_par4=layer_par4, head_par=head_par,
        hgrn=a["state_hgrn"].transpose(1, 2, 3, 0, 4).reshape(DEPTH, HEADS, P, NB * P),
        ml_c=a["state_mlstm_c"].transpose(1, 2, 3, 0, 4).reshape(DEPTH, HEADS, P, NB * P),
    )
    results = dict(
        y=(P, KC, T), k=(DEPTH, P, HEADS, T), v=(DEPTH, P, HEADS, T), hgrn_p=(DEPTH, HEADS, P, P),
        hgrn_s=(DEPTH, HEADS, P, NB * P), c_p=(DEPTH, HEADS, P, P), c_s=(DEPTH, HEADS, P, NB * P),
        n_p=(DEPTH, HEADS, P, 1), n_s=(DEPTH, P, HEADS, NB), m_p=(DEPTH, HEADS, 1), m_s=(DEPTH, HEADS, NB),
        conv_p=(DEPTH, HEADS, P, 3), conv_s=(DEPTH, HEADS, P, 3 * NB),
    )
    nc = bacc.Bacc("TRN2", target_bir_lowering=False, num_devices=1)
    arrays, ins, outs = {}, {}, {}
    for name, v in feeds.items():
        v = np.ascontiguousarray(v)
        arrays["in_" + name] = v
        ins[name] = nc.dram_tensor("in_" + name, v.shape, mybir.dt.from_np(v.dtype), kind="ExternalInput").ap()
    for name, shape in results.items():
        outs[name] = nc.dram_tensor("out_" + name, shape, F32, kind="ExternalOutput").ap()
    build(nc, namedtuple("Inputs", ins)(**ins), namedtuple("Outputs", outs)(**outs))
    got = run_bass_kernel_spmd(nc, [arrays], core_ids=[0]).results[0]
    o = {name: np.asarray(got["out_" + name]) for name in results}

    yt = o["y"].transpose(2, 1, 0).reshape(T, D)
    kk, vv = (o[n].transpose(0, 3, 2, 1).reshape(DEPTH, T, SBH, 64) for n in ("k", "v"))
    hs = o["hgrn_s"].reshape(DEPTH, HEADS, P, NB, P).transpose(3, 0, 1, 2, 4)
    cs = o["c_s"].reshape(DEPTH, HEADS, P, NB, P).transpose(3, 0, 1, 2, 4)
    conv_s = o["conv_s"].reshape(DEPTH, HEADS, P, 3, NB).transpose(4, 0, 3, 1, 2).reshape(NB, DEPTH, 3, 512)
    conv_p = o["conv_p"].transpose(0, 3, 1, 2).reshape(1, DEPTH, 3, 512)
    c = np.ascontiguousarray
    return (c(yt[None, 0:TP]), c(yt[TP:, None]), c(kk[None, :, 0:TP]), c(vv[None, :, 0:TP]),
            c(kk[:, TP:].transpose(1, 0, 2, 3)[:, :, None]), c(vv[:, TP:].transpose(1, 0, 2, 3)[:, :, None]),
            c(o["hgrn_p"][None]), c(hs), c(o["c_p"][None]), c(cs), c(o["n_p"][None, :, :, :, 0]),
            c(o["n_s"].transpose(3, 0, 2, 1)), c(o["m_p"].transpose(2, 0, 1)), c(o["m_s"].transpose(2, 0, 1)),
            conv_p, c(conv_s))
```

```python
from collections import namedtuple
from contextlib import ExitStack, contextmanager

import concourse.bass as bass
from concourse import mybir

F32 = mybir.dt.float32
I32 = mybir.dt.int32
ALU = mybir.AluOpType
ACT = mybir.ActivationFunctionType
AX = mybir.AxisListType

P = 128
D = 1024
KC = D // P
TP = 256
NB = 8
T = TP + NB
DEPTH = 2
DFF = 2816
FC = DFF // P
HEADS = 4
SBH = 8
PAGES = 8
PHYS = 80
ADA_N = 9 * KC
ADA_G = 12
ADA_COLS = 3 * P
EPS = 1e-6
SB_SCALE = 64 ** -0.5
ML_SCALE = P ** -0.5
NEVER = -30000.0
SLOT = 24
SLOTS = 4
SQ_, SK_, SV_, MX_, HQ_, HF_, HI_, HG_ = range(KC)
WQ, WIF, CW, CBIAS, HGG, CST, SBB2, HPN = 0, 384, 408, 412, 413, 414, 438, 440
BADA, GPRE, GPOST, SBB, N0, MLG, LPN = 0, 72, 96, 120, 128, 160, 164
STORES_A, STORES_B = 6, 4
LEVELS = 8


class Count:

    def __init__(self):
        self.n, self.i, self.per = 0, None, 0

    @contextmanager
    def loop(self, i, times, per):
        before, self.i, self.per = self.n, i, per
        yield
        assert self.n - before == per, f"{self.n - before} in a round, not {per}"
        self.i, self.n = None, before + per * times

    def __call__(self, k=1):
        now = self.n if self.i is None or not self.per else self.i * self.per + self.n
        self.last = now
        self.n += k
        return now


class Slots:

    def __init__(self):
        self.pos = 0
        self.loads, self.parts = [Count() for _ in range(SLOTS)], [Count() for _ in range(SLOTS)]

    @contextmanager
    def loop(self, i, times, parts, at=None):
        with ExitStack() as stack:
            for r in range(SLOTS):
                mine = [p for j, p in enumerate(parts) if (self.pos + j) % SLOTS == r] if at is None \
                    else (parts if r == at else [])
                stack.enter_context(self.loads[r].loop(i, times, len(mine)))
                stack.enter_context(self.parts[r].loop(i, times, sum(mine)))
            yield

    def take(self, parts, at=None):
        r = self.pos if at is None else at
        if at is None:
            self.pos = (self.pos + 1) % SLOTS
        return r, self.loads[r](), self.parts[r](parts)


class Products:

    def __init__(self):
        self.count, self.pos = Count(), 0

    def take(self, banks=4):
        b = self.pos
        self.pos = (self.pos + 1) % banks
        return b, self.count()


class Chain:

    def __init__(self, eng, sem):
        self.eng, self.sem, self.n, self.i, self.per = eng, sem, 0, None, 0

    def __call__(self, ins):
        self.n += 1
        ins.then_inc(self.sem, 1)
        self.eng.wait_ge(self.sem, self.n if self.i is None else self.i * self.per + self.n)

    @contextmanager
    def loop(self, i, times, per):
        before = self.n
        self.i, self.per = i, per
        yield
        assert self.n - before == per, f"{self.n - before} links a round, not {per}"
        self.i, self.n = None, before + per * times


def build(nc, ins, outs):
    ctx = ExitStack()
    with ctx:
        def sb(name, shape, dt=F32):
            return ctx.enter_context(nc.sbuf_tensor(name, shape, dt))

        def sems(names):
            return namedtuple("Semaphores", names)(*(ctx.enter_context(nc.semaphore(n)) for n in names.split()))

        x = sb("x", [P, KC, T])
        xn = sb("xn", [P, KC, T])
        ring = sb("ring", [P, SLOTS, SLOT * P])
        pages = sb("pages", [P, PAGES, 4 * P])
        consts = sb("consts", [P, 6, P])
        ident, ones, tri = consts[:, 0, :], consts[:, 1, :], consts[:, 2, :]
        strict01, strictneg, causalpos = consts[:, 3, :], consts[:, 4, :], consts[:, 5, :]
        hmask = sb("hmask", [P, LEVELS, P], mybir.dt.uint8)
        onerow = ones[:, 0:1].broadcast_to([P, TP])
        eps = sb("eps", [P, 1])
        ctok = sb("ctok", [P, KC, NB + 1])
        sel = sb("sel", [P, SBH])
        rbuf = sb("rbuf", [P, 512])
        csil = sb("csil", [P, KC, NB + 1])
        lbl = sb("lbl", [P, DEPTH, HEADS])
        lbt = sb("lbt", [P, DEPTH * HEADS, 2])
        lbx = sb("lbx", [P, 4, HEADS])
        lbh = sb("lbh", [P, 2])
        ptab = sb("ptab", [1, NB * PAGES], I32)
        lp = sb("lp", [P, LPN])
        lp4 = sb("lp4", [4, 2 + NB])
        ada = sb("ada", [P, ADA_N, NB + 1])
        atab = sb("atab", [P, KC, NB + 1])
        gtab = sb("gtab", [P, KC, NB + 1])
        ctmp = gtab
        rs = sb("rs", [P, T])
        smpt = sb("smpt", [P, KC, NB])
        wbuf = sb("wbuf", [P, 6, T])
        w1, w2, w3, w4, w5, w6 = (wbuf[:, n, :] for n in range(6))
        sq, acc = wbuf[:, 4:6, :], w1
        fe = sb("fe", [P, 2, T])
        ft = sb("ft", [P, 2, T])
        big = sb("big", [P, 28, T])
        qkv = big[:, 0:12, :].rearrange("p (j h) t -> p j h t", j=3)
        oa, ob, oc = big[:, 12:16, :], big[:, 16:20, :], big[:, 20:24, :]
        mo = big[:, 24:28, :]
        hid = big[:, 0:FC, :]
        merged = big[:, 0:KC, :]
        gates = sb("gates", [P, 3 * KC, T])
        pj = sb("pj", [P, 9, T])
        y = pj[:, 0:KC, :]
        xp = sb("xp", [P, 3 + T])
        hp = sb("hp", [P, HPN])
        arena = sb("arena", [P, 2 * LEVELS * TP])
        e8 = arena[:, 0:LEVELS * TP].rearrange("p (v t) -> p v t", v=LEVELS)
        ql = arena[:, LEVELS * TP:2 * LEVELS * TP].rearrange("p (v t) -> p v t", v=LEVELS)
        kl = e8

        def part(at, n, *shape):
            v = arena[:, at:at + n]
            return v.rearrange("p (a b) -> p a b", a=shape[0]) if shape else v

        zp, sbt, spt = part(0, 768, 2), part(768, 768, 2), part(1536, 768, 2)
        tt8 = part(0, NB * P, NB)
        dg8 = part(NB * P, NB * P, NB)
        st8 = sb("st8", [P, NB, P])
        sn8 = sb("sn8", [P, NB, P])
        vi = sb("vi", [P, 4, P])
        sct = sb("sct", [P, 3, P])
        kdt = sb("kdt", [P, 2, P])
        hsp = sb("hsp", [P, P])
        sgt = sb("sgt", [P, 2, T])
        xc = sb("xc", [P, T])
        nbs = sb("nbs", [P, 3, NB])
        s8a, s8b, s8c = sb("s8a", [P, NB]), sb("s8b", [P, NB]), sb("s8c", [P, NB])
        ot = sb("ot", [P, T])
        gi = sb("gi", [4, T])
        gf = sb("gf", [4, T])
        r4 = arena[0:4, 3072:3072 + 3 * T].rearrange("p (a t) -> p a t", a=3)
        rows = arena[0:4, 0:TP + 3 * NB + TP]
        nrow = TP + 3 * NB + TP
        bd = pj[0:4, :, :].rearrange("p c t -> p (c t)")[:, 0:4 * nrow].rearrange("p (h n) -> p h n", h=4)
        gcol = sb("gcol", [P, 2, 4])
        qm = sb("qm", [P, NB, HEADS, SBH])
        zt = part(2560, 512)
        zs = sb("zs", [P, 512])
        ast = sb("ast", [P, 2, PAGES * SBH])
        qst = ast[:, 0, :].rearrange("p (e c h) -> p e c h", e=2, c=HEADS)
        ks, vs, qs = fe[:, 0, :], fe[:, 1, :], sgt[:, 0, :]
        vk, dm, wt = part(2048, 512, 4), part(2560, 384), part(2944, 384)
        vw2 = xc[:, 0:TP].rearrange("p (t k) -> p t k", t=2)
        nst = sb("nst", [P, 1])
        sw = sb("sw", [P, 3 * NB])
        ps = ctx.enter_context(nc.psum_tensor("ps", [P, 8, 512], F32))
        M0, M1, M2, Z = 4, 5, 6, 7

        slot_full = [ctx.enter_context(nc.semaphore(f"slot_full{r}")) for r in range(SLOTS)]
        slot_done = [ctx.enter_context(nc.semaphore(f"slot_done{r}")) for r in range(SLOTS)]
        page_full = [ctx.enter_context(nc.semaphore(f"page_full{r}")) for r in range(PAGES // 2)]
        page_free = [ctx.enter_context(nc.semaphore(f"page_free{r}")) for r in range(PAGES // 2)]
        S = sems(
            "evac ada_evac ada_row ada_tr qstr zrow ztr zev astr vrow vrd lpar dchain achain pchain store hpar "
            "x2_ready ss_ready rs_ready xn_ready y_ready yss_ready yrs_ready e_ready "
            "sqc qmr tr zz spr suf t_ready ar av obr xcr qkv_ps qkv_sb gt gir kdr kdtp kdtr accd nnr nqr lfr ibr ho hos osq hss "
            "lvl lvc klr qlr snr pe_it act_it dve_it pool_it vir zpr l1r lnr accr xer tzr ur l2r khr "
            "dlr elr kder fsr sge rsh ger snp snm otr "
            "zpsr lnsr spsr sufs t2r asr rw1 rl1 rw2 rw3 bdr gcp gcr "
            "stg trb kqr exr dmr vwr ndr adr htr cst cev kbr cnr cnp qbr qcr dns dna sqh hbs rsb mg x_fin "
        )

        with nc.Block() as block:
            @block.sync
            def _(sp):
                for dst, src in ((consts[:], ins.consts), (tt8, ins.masks), (x[:], ins.x),
                                 (ctok[:], ins.c), (sel[:], ins.sel), (lbl[:], ins.lb), (ptab[:], ins.page_table)):
                    sp.dma_start(dst, src).then_inc(S.lpar, 16)
                sp.wait_ge(S.lpar, 112)

            @block.gpsimd
            def _(pool):
                nc.gpsimd.memset(eps[:], EPS)
                nc.gpsimd.memset(qm[:], 0.0)
                nc.gpsimd.memset(xp[:], 0.0)

            @block.scalar
            def _(act):
                act.wait_ge(S.lpar, 112)
                nc.scalar.activation(ctmp[:], ctok[:], ACT.Exp, scale=-1.0).then_inc(S.achain, 1)
                act.wait_ge(S.dchain, 3)
                nc.scalar.activation(lbx[:, 1:3, :], lbx[:, 1:3, :], ACT.Exp).then_inc(S.achain, 1)
                act.wait_ge(S.x_fin, 1)
                nc.scalar.activation(lbx[:, 3, :], lbx[:, 3, :], ACT.Ln).then_inc(S.achain, 1)

            @block.vector
            def _(dve):
                link = Chain(dve, S.dchain)
                dve.wait_ge(S.lpar, 112)
                nc.vector.tensor_copy(hmask[:], tt8)
                for bank in (M0, Z):
                    nc.vector.memset(ps[:, bank, :], 0.0)
                link(nc.vector.tensor_tensor(lbx[:, 0, :], lbl[:, 0, :], lbl[:, 1, :], ALU.max))
                for j in range(2):
                    link(nc.vector.tensor_tensor(lbx[:, 1 + j, :], lbl[:, j, :], lbx[:, 0, :], ALU.subtract))
                link(nc.vector.memset(lbt[:, 0:HEADS, 0:1], -1e30))
                link(nc.vector.memset(lbt[:, 0:HEADS, 1:2], 0.0))
                dve.wait_ge(S.achain, 2)
                nc.vector.tensor_tensor(lbx[:, 3, :], lbx[:, 1, :], lbx[:, 2, :], ALU.add).then_inc(S.x_fin, 1)
                dve.wait_ge(S.x_fin, 1)
                dve.wait_ge(S.achain, 3)
                link(nc.vector.tensor_tensor(lbx[:, 0, :], lbx[:, 0, :], lbx[:, 3, :], ALU.add))
                for j in range(2):
                    link(nc.vector.tensor_tensor(lbt[:, HEADS:2 * HEADS, j], lbl[:, 1 - j, :],
                                                 lbx[:, 0, :], ALU.subtract))
                link(nc.vector.tensor_scalar_add(ctmp[:], ctmp[:], 1.0))
                link(nc.vector.reciprocal(ctmp[:], ctmp[:]))
                link(nc.vector.tensor_tensor(csil[:], ctmp[:], ctok[:], ALU.mult))

        clear = list(S) + slot_full + slot_done + page_full + page_free

        def clear_all():
            nc.all_engine_barrier()
            for s in clear:
                nc.sync.sem_clear(s)
            nc.all_engine_barrier()

        clear_all()

        def one_layer(block, layer):
            bds = bass.ds

            def apart(eng):
                eng.nop(nofuse=True)

            @block.sync
            def _(sp):
                slots, page_loads = Slots(), Count()
                nc.sync.dma_start(lp[:], ins.layer_par[layer]).then_inc(S.lpar, 16)
                nc.sync.dma_start(lp4[:], ins.layer_par4[layer]).then_inc(S.lpar, 16)

                def load(src, parts, at=None):
                    tiles = src.shape[-1] // P
                    r, _, before = slots.take(parts, at)
                    sp.wait_ge(slot_done[r], before + 1)
                    sp.dma_start(ring[:, r, 0:tiles * P], src).then_inc(slot_full[r], 16)

                def load_pages(pool_of_pages, b):
                    before = page_loads()
                    for j in range(PAGES):
                        page = sp.value_load(ptab[0:1, bds(b * PAGES + j, 1)], min_val=0, max_val=PHYS - 1)
                        sp.wait_ge(page_free[j // 2], before + 1)
                        sp.dma_start(pages[:, j, :], pool_of_pages[layer, page]).then_inc(page_full[j // 2], 16)

                with sp.Fori(0, 2) as i, slots.loop(i, 2, [1] * 4):
                    for k in range(4):
                        load(ins.w_ada[layer, i * 4 + k], 1)
                with sp.Fori(0, 4) as i, slots.loop(i, 4, [1, 2] * 4):
                    for k in range(4):
                        load(ins.w_ada[layer, i * 4 + (8 + k)], 1)
                        load(ins.w_ffn_in[layer, 0, i * 4 + k], 2)
                for k in range(16, FC):
                    load(ins.w_ffn_in[layer, 0, k], 2)
                with sp.Fori(0, 2) as i, slots.loop(i, 2, [1] * 4):
                    for k in range(4):
                        load(ins.w_ffn_down[layer, 0, i * 4 + k], 1)
                for s in range(2):
                    load(ins.w_sq[layer, s], 2)
                with sp.Fori(0, HEADS) as i, slots.loop(i, HEADS, [3] * 4), page_loads.loop(i, HEADS, 2):
                    for k in range(3):
                        load(ins.w_a[layer, i * 4 + k], 3)
                    load_pages(ins.k_pages, i * 2)
                    load(ins.w_a[layer, i * 4 + 3], 3)
                    load_pages(ins.k_pages, i * 2 + 1)
                at = slots.pos
                with sp.Fori(0, HEADS) as i, slots.loop(i, HEADS, [2], at), page_loads.loop(i, HEADS, 2):
                    load_pages(ins.v_pages, i * 2)
                    load(ins.w_b[layer, i], 2, at)
                    load_pages(ins.v_pages, i * 2 + 1)
                for s in range(4):
                    load(ins.w_proj[layer, s], 6)
                for s in range(4):
                    load(ins.w_out[layer, s], 2)
                with sp.Fori(0, 5) as i, slots.loop(i, 5, [2] * 4):
                    for k in range(4):
                        load(ins.w_ffn_in[layer, 1, i * 4 + k], 2)
                for s in (20, 21):
                    load(ins.w_ffn_in[layer, 1, s], 2)
                with sp.Fori(0, 2) as i, slots.loop(i, 2, [1] * 4):
                    for k in range(4):
                        load(ins.w_ffn_down[layer, 1, i * 4 + k], 1)

            @block.tensor
            def _(pe):
                slots, products, adas, page_uses = Slots(), Products(), Count(), Count()
                for s in slot_done + page_free:
                    pe.sem_inc(s, 1)
                mm = nc.tensor.matmul

                def open_slot(parts, at=None):
                    r, loads, _ = slots.take(parts, at)
                    pe.wait_ge(slot_full[r], loads * 16 + 16)
                    return r

                def tile_of(r, k):
                    return ring[:, r, k * P:(k + 1) * P]

                def product(r, first, rhs, depth, banks=4):
                    b, n = products.take(banks)
                    pe.wait_ge(S.evac, n + (1 + 4 - banks))
                    for k in range(depth):
                        last = mm(ps[:, b, 0:T], tile_of(r, first + k), rhs(k), start=(k == 0), stop=(k == depth - 1))
                    last.then_inc(slot_done[r], 1)

                def ada_slot(q):
                    r = open_slot(1)
                    if q == 0:
                        pe.wait_ge(S.ada_evac, adas() + 1)
                    for u in range(2):
                        k = 2 * q + u
                        for j in range(4):
                            last = mm(ps[32 * j:32 * j + NB + 1, M0, 0:ADA_COLS], csil[:, k, :],
                                      ring[:, r, (u * 4 + j) * ADA_COLS:(u * 4 + j + 1) * ADA_COLS],
                                      start=(k == 0), stop=(k == KC - 1))
                    last.then_inc(slot_done[r], 1)

                def ada_columns(n):
                    pe.wait_ge(S.ada_row, n + 1)
                    for k in range(3):
                        last = nc.tensor.transpose(ps[:, M1, k * P:(k + 1) * P], rbuf[:, k * P:(k + 1) * P], ident)
                    last.then_inc(S.ada_tr, 1)

                def xn_of(k):
                    return xn[:, k, :]

                def ffn_slot():
                    r = open_slot(2)
                    product(r, 0, xn_of, KC)
                    product(r, KC, xn_of, KC)

                def pre_sums(n):
                    for k in range(KC):
                        pe.wait_ge(S.x2_ready, (n - 1) * KC + k + 1)
                        last = mm(ps[:, Z, 0:T], ones, xn[:, k, :], start=(k == 0), stop=(k == KC - 1))
                    last.then_inc(S.ss_ready, 1)

                def post_sum(n):
                    pe.wait_ge(S.accd, n * KC + 2)
                    mm(ps[:, Z, 0:T], ones, acc, start=True, stop=True).then_inc(S.yss_ready, 1)

                def down():
                    pe.wait_ge(S.evac, products.count.n + 4)
                    with pe.Fori(0, 2) as i, slots.loop(i, 2, [1] * 4), products.count.loop(i, 2, 4):
                        for k in range(4):
                            r = open_slot(1)
                            product(r, 0, lambda k: hid[:, k, :], FC)

                with pe.Fori(0, 2) as i, slots.loop(i, 2, [1] * 4), adas.loop(i, 2, 1):
                    for k in range(4):
                        ada_slot(k)
                    ada_columns(i)
                pre_sums(1)
                pe.wait_ge(S.xn_ready, 1)
                with pe.Fori(0, 4) as i, slots.loop(i, 4, [1, 2] * 4), products.count.loop(i, 4, 8), \
                        adas.loop(i, 4, 1):
                    for k in range(4):
                        ada_slot(k)
                        ffn_slot()
                    ada_columns(i + 2)
                for k in range(16, FC):
                    ffn_slot()
                down()
                post_sum(1)
                pre_sums(2)
                pe.wait_ge(S.xn_ready, 2)

                for s in range(2):
                    r = open_slot(2)
                    product(r, 0, xn_of, KC)
                    product(r, KC, xn_of, KC)

                def key_pages(e):
                    loads = page_uses()
                    for j in range(4):
                        pe.wait_ge(page_full[j], loads * 32 + 32)
                    for c in range(HEADS):
                        for j in range(4):
                            last = mm(ps[32 * j:32 * j + SBH, Z, e * 256:(e + 1) * 256], qst[:, e, c, :],
                                      pages[:, 2 * j:2 * j + 2, c * P:(c + 1) * P],
                                      start=(c == 0), stop=(c == HEADS - 1))
                            if c == HEADS - 1:
                                last.then_inc(page_free[j], 1)

                def value_pages(e, n):
                    loads = page_uses()
                    for j in range(4):
                        pe.wait_ge(page_full[j], loads * 32 + 32)
                    pe.wait_ge(S.vrow, n + 1)
                    for u in range(2):
                        for j in range(4):
                            last = mm(ps[32 * j:32 * j + SBH, 3, :], ast[:, e, (2 * j + u) * SBH:(2 * j + u + 1) * SBH],
                                      pages[:, 2 * j + u, :], start=(u == 0), stop=(u == 1))
                            if u == 1:
                                last.then_inc(page_free[j], 1)

                def value_columns(b, n):
                    pe.wait_ge(S.vrow, n + 2)
                    for c in range(HEADS):
                        last = mm(ps[:, 2, bds(b * 8 + 2 * c, 2)], rbuf[:, c * P:(c + 1) * P],
                                  sel[:, 2 * c:2 * c + 2], start=True, stop=True)
                    last.then_inc(S.vrd, 1)

                before_a = products.count.n
                with pe.Fori(0, HEADS) as i:
                    with slots.loop(i, HEADS, [3] * 4), products.count.loop(i, HEADS, 12), page_uses.loop(i, HEADS, 2):
                        for k in range(3):
                            r = open_slot(3)
                            for n in range(3):
                                product(r, n * KC, xn_of, KC)
                        pe.wait_ge(S.dve_it, i + 1)
                        pe.wait_ge(S.rsh, i + 1)
                        pe.wait_ge(S.sqc, i + 1)
                        pe.wait_ge(S.evac, i * 12 + (before_a + 6 + 4))
                        for n, (c, t) in enumerate(((SV_, 0), (SV_, 1), (HI_, 0), (HI_, 1))):
                            last = nc.tensor.transpose(ps[:, M0, n * P:(n + 1) * P], pj[:, c, t * P:(t + 1) * P], ident)
                        last.then_inc(S.tr, 1)
                        for h in range(2):
                            a, e = 64 * h, 64 * h + 64
                            mm(ps[:, M1 + h, 0:TP], pj[a:e, SK_, 0:P], pj[a:e, SQ_, 0:TP], start=True, stop=True)
                            last = mm(ps[:, M1 + h, TP:TP + P], pj[a:e, SK_, P:TP], pj[a:e, SQ_, P:TP],
                                      start=True, stop=True)
                        last.then_inc(S.zz, 1)
                        gslot = open_slot(3)
                        product(gslot, 0, xn_of, KC)
                        pe.wait_ge(S.spr, i + 1)
                        for h in range(2):
                            mm(ps[:, M1 + h, 0:TP], tri, spt[:, h, 0:TP], start=True, stop=False)
                            mm(ps[:, M1 + h, P:TP], ones, spt[:, h, TP:TP + P], start=False, stop=True)
                            last = mm(ps[:, M1 + h, TP:TP + P], tri, spt[:, h, TP:TP + P], start=True, stop=True)
                        last.then_inc(S.suf, 1)
                        product(gslot, KC, xn_of, KC)
                        pe.wait_ge(S.vir, i + 1)
                        pe.wait_ge(S.ar, i + 1)
                        for h in range(2):
                            a, e = 64 * h, 64 * h + 64
                            mm(ps[a:e, M0, 0:TP], vi[:, 0, a:e], sbt[:, h, 0:TP], start=True, stop=False)
                            last = mm(ps[a:e, M0, P:TP], vi[:, 1, a:e], sbt[:, h, TP:TP + P], start=False, stop=True)
                        last.then_inc(S.av, 1)
                        pe.wait_ge(S.xcr, i + 1)
                        pe.wait_ge(S.hpar, i * 32 + 32)
                        mm(ps[:, M1, 0:T], hp[:, WQ:WQ + P], xc[:], start=True, stop=True)
                        mm(ps[:, M2, 0:T], hp[:, WQ + P:WQ + 2 * P], xc[:], start=True, stop=True)
                        pe.wait_ge(S.obr, i + 1)
                        mm(ps[:, M0, 0:T], hp[:, WQ + 2 * P:WQ + 3 * P], xp[:, 3:3 + T], start=True, stop=True)\
                            .then_inc(S.qkv_ps, 1)
                        product(gslot, 2 * KC, xn_of, KC)
                        pe.wait_ge(S.qkv_sb, i + 1)
                        for g in range(2):
                            for j in range(3):
                                last = mm(ps[0:4, M1 + g, 0:T], hp[:, WIF + j * 8 + 4 * g:WIF + j * 8 + 4 * g + 4],
                                          qkv[:, j, i, :], start=(j == 0), stop=(j == 2))
                        last.then_inc(S.gt, 1)
                        pe.wait_ge(S.qstr, i + 1)
                        key_pages(0)
                        pe.wait_ge(S.qlr, i + 1)
                        pe.wait_ge(S.klr, i + 1)
                        pe.wait_ge(S.gir, i + 1)

                        def level(b, at, v):
                            for t in range(2):
                                lhs = w4[:, t * P:(t + 1) * P] if v < 0 else kl[:, v, t * P:(t + 1) * P]
                                rhs = pj[:, HQ_, t * P:(t + 1) * P] if v < 0 else ql[:, v, t * P:(t + 1) * P]
                                last = mm(ps[:, b, at + t * P:at + (t + 1) * P], lhs, rhs, start=True, stop=True)
                            return last

                        level(M1, 0, -1)
                        level(M1, TP, 0).then_inc(S.lvl, 1)
                        level(M2, 0, 1)
                        level(M2, TP, 2).then_inc(S.lvl, 1)
                        mm(ps[:, M0, 0:P], kl[:, 7, 0:P], ql[:, 7, P:TP], start=True, stop=True).then_inc(S.lvl, 1)
                        pe.wait_ge(S.lvc, i * 5 + 1)
                        level(M1, 0, 3)
                        level(M1, TP, 4).then_inc(S.lvl, 1)
                        pe.wait_ge(S.lvc, i * 5 + 2)
                        level(M2, 0, 5)
                        level(M2, TP, 6).then_inc(S.lvl, 1)
                        pe.wait_ge(S.lvc, i * 5 + 3)
                        pe.wait_ge(S.kdr, i + 1)
                        for t in range(2):
                            last = nc.tensor.transpose(ps[:, M0, t * P:(t + 1) * P], w6[:, t * P:(t + 1) * P], ident)
                        last.then_inc(S.kdtp, 1)
                        key_pages(1)
                        pe.wait_ge(S.lvc, i * 5 + 5)
                        pe.wait_ge(S.kdtr, i + 1)
                        pe.wait_ge(S.snp, i + 1)
                        for n in range(2):
                            last = mm(ps[:, M1 + n, 0:512], ones, dg8[:, 4 * n:4 * n + 4, :], start=True, stop=True)
                        last.then_inc(S.ibr, 1)
                        mm(ps[:, M0, 0:TP], vi[:, 2, :], sct[:, 0:2, :], start=True, stop=False)
                        mm(ps[:, M0, P:TP], vi[:, 3, :], sct[:, 2, :], start=False, stop=True)
                        mm(ps[:, M0, 384:512], kdt[:, 0, :], vi[:, 2, :], start=True, stop=False)
                        mm(ps[:, M0, 384:512], kdt[:, 1, :], vi[:, 3, :], start=False, stop=True).then_inc(S.ho, 1)
                        pe.wait_ge(S.snr, i + 1)
                        for b in range(NB):
                            last = mm(ps[:, M1, b:b + 1], sn8[:, b, :], pj[:, HQ_, TP + b:TP + b + 1],
                                      start=True, stop=True)
                        last.then_inc(S.hos, 1)
                        pe.wait_ge(S.osq, i + 1)
                        mm(ps[:, M2, 0:T], ones, w2, start=True, stop=True).then_inc(S.hss, 1)
                        pe.wait_ge(S.zrow, i + 1)
                        for n in range(4):
                            last = nc.tensor.transpose(ps[:, Z, n * P:(n + 1) * P], rbuf[:, n * P:(n + 1) * P], ident)
                        last.then_inc(S.ztr, 1)

                pe.wait_ge(S.spsr, 1)
                mm(ps[:, Z, 0:512], tri, zt, start=True, stop=False)
                out4 = ps[:, Z, :].rearrange("p (b j h) -> p b j h", b=NB, j=PAGES)
                in4 = zt.rearrange("p (b j h) -> p b j h", b=NB, j=PAGES)
                for j in range(1, PAGES):
                    last = mm(out4[:, :, 0:PAGES - j, :], ones, in4[:, :, j:PAGES, :], start=False, stop=(j == PAGES - 1))
                last.then_inc(S.sufs, 1)
                pe.wait_ge(S.rw1, 1)
                pe.wait_ge(S.dve_it, HEADS + 1)
                pe.wait_ge(S.rsh, HEADS + 1)
                for t in range(2):
                    last = nc.tensor.transpose(ps[:, M0, t * 4:t * 4 + 4], r4[:, 0, t * P:(t + 1) * P], ident[0:4, 0:4])
                last.then_inc(S.gcp, 1)
                pe.wait_ge(S.gcr, 1)
                gate_slot, products.pos = slots.pos, 0

                with pe.Fori(0, HEADS) as i:
                    with slots.loop(i, HEADS, [2], gate_slot), products.count.loop(i, HEADS, 2), \
                            page_uses.loop(i, HEADS, 2):
                        pe.wait_ge(S.stg, i * 3 + 3)
                        pe.wait_ge(S.dve_it, i + HEADS + 1)
                        for n, src in enumerate((vs, vs, ks, ks)):
                            t = n % 2
                            last = nc.tensor.transpose(ps[:, M0, n * P:(n + 1) * P], src[:, t * P:(t + 1) * P], ident)
                        last.then_inc(S.trb, 1)
                        mm(ps[:, M1, 0:TP], ks[:, 0:P], qs[:, 0:TP], start=True, stop=True)
                        mm(ps[:, M1, TP:TP + P], ks[:, P:TP], qs[:, P:TP], start=True, stop=True)
                        pe.wait_ge(S.bdr, 1)
                        mm(ps[:, M2, 0:TP + 24], ones[0:4, :], bd[:, i, 0:TP + 24], start=True, stop=True)
                        mm(ps[:, Z, 0:TP], ones[0:4, :], bd[:, i, TP + 24:], start=True, stop=True).then_inc(S.kqr, 1)
                        pe.wait_ge(S.astr, i + 1)
                        value_pages(0, i * 2)
                        r = open_slot(2, gate_slot)
                        for n in range(2):
                            product(r, n * KC, xn_of, KC, banks=2)
                        value_columns(i * 2, i * 2)
                        pe.wait_ge(S.vwr, i + 1)
                        for b, lhs in ((M0, None), (M1, ones)):
                            mm(ps[:, b, 0:TP], lhs if lhs is not None else vk[:, 0, :], wt[:, 0:TP], start=True, stop=False)
                            last = mm(ps[:, b, P:TP], lhs if lhs is not None else vk[:, 1, :], wt[:, TP:TP + P],
                                      start=False, stop=True)
                        last.then_inc(S.ndr, 1)
                        for t in range(2):
                            mm(ps[:, M2, 0:P], vw2[:, t, :], vk[:, 2 + t, :], start=(t == 0), stop=(t == 1))
                        for t in range(2):
                            col = (TP - 1, TP + P - 1)[t]
                            last = mm(ps[:, M2, P:P + 1], vk[:, 2 + t, :], dm[:, col:col + 1],
                                      start=(t == 0), stop=(t == 1))
                        last.then_inc(S.cst, 1)
                        pe.wait_ge(S.htr, i + 1)
                        pe.wait_ge(S.cev, i + 1)
                        pe.wait_ge(S.snp, HEADS + 2 * i + 1)
                        for n in range(2):
                            last = mm(ps[:, M1 + n, 0:512], ones, dg8[:, 4 * n:4 * n + 4, :], start=True, stop=True)
                        last.then_inc(S.kbr, 1)
                        pe.wait_ge(S.nqr, i + 1)
                        mm(ps[:, M0, 0:NB], ones, s8b[:], start=True, stop=True).then_inc(S.dns, 1)
                        pe.wait_ge(S.cnr, i + 1)
                        pe.wait_ge(S.snp, HEADS + 2 * i + 2)
                        for n in range(2):
                            last = mm(ps[:, M1 + n, 0:512], ones, dg8[:, 4 * n:4 * n + 4, :], start=True, stop=True)
                        last.then_inc(S.qbr, 1)
                        value_pages(1, i * 2 + 1)
                        pe.wait_ge(S.sqh, i + 1)
                        mm(ps[:, M0, 0:T], ones, w2, start=True, stop=True).then_inc(S.hbs, 1)
                        value_columns(i * 2 + 1, i * 2 + 1)

                products.pos = 0
                pe.wait_ge(S.dve_it, 2 * HEADS + 2)
                for s in range(4):
                    r = open_slot(6)
                    for n in range(2):
                        for br, o in enumerate((oa, ob, oc)):
                            product(r, (n * 3 + br) * 4, (lambda o: lambda k: o[:, k, :])(o), HEADS)
                pe.wait_ge(S.mg, KC)
                for s in range(4):
                    r = open_slot(2)
                    for n in range(2):
                        product(r, n * KC, lambda k: merged[:, k, :], KC)
                post_sum(2)
                pre_sums(3)
                pe.wait_ge(S.xn_ready, 3)
                with pe.Fori(0, 5) as i, slots.loop(i, 5, [2] * 4), products.count.loop(i, 5, 8):
                    for k in range(4):
                        ffn_slot()
                for k in range(2):
                    ffn_slot()
                down()
                post_sum(3)

            @block.vector
            def _(dve):
                slots, products, exps, sums = Slots(), Products(), Count(), Count()
                v = nc.vector
                link = Chain(dve, S.dchain)
                dve.sem_inc(S.evac, 4)
                dve.sem_inc(S.ada_evac, 1)
                dve.sem_inc(S.accd, 2)
                dve.sem_inc(S.dve_it, 1)
                dve.wait_ge(S.lpar, 32)

                def ada_rows():
                    for q in range(4):
                        r, _, before = slots.take(1)
                        yield
                    dve.wait_ge(slot_done[r], before + 2)
                    v.tensor_copy(rbuf[:, 0:ADA_COLS], ps[:, M0, 0:ADA_COLS]).then_inc(S.ada_row, 1)
                    yield

                def ada_columns(n):
                    dve.wait_ge(S.ada_tr, n + 1)
                    v.tensor_tensor(
                        ada[:, bds(n * ADA_G, ADA_G), :].rearrange("p (j q) t -> p j q t", j=4),
                        ps[:, M1, 0:ADA_COLS].rearrange("p (q j t) -> p j q t", q=3, j=4)[:, :, :, 0:NB + 1],
                        lp[:, bds(n * ADA_G + BADA, ADA_G)].rearrange("p (j q) -> p j q", j=4).unsqueeze(3)
                        .broadcast_to([P, 4, 3, NB + 1]), ALU.add).then_inc(S.ada_evac, 1)

                def ffn_slot(k, chunk):
                    r, _, before = slots.take(2)
                    bg, _ = products.take()
                    bu, _ = products.take()
                    dve.wait_ge(S.e_ready, exps() + 1)
                    t = ft[:, k % 2, :]
                    link(v.tensor_scalar_add(t, fe[:, k % 2, :], 1.0))
                    link(v.reciprocal(t, t))
                    link(v.tensor_tensor(t, ps[:, bg, 0:T], t, ALU.mult))
                    dve.wait_ge(slot_done[r], before + 3)
                    v.tensor_tensor(hid[:, chunk, :], ps[:, bu, 0:T], t, ALU.mult).then_inc(S.evac, 2)

                def sum_squares():
                    n = sums()
                    products.take()
                    dve.wait_ge(S.evac, products.count.last + (1 + 4))
                    dve.wait_ge(S.accd, n + 2)
                    v.tensor_tensor(acc, acc, sq[:, sums.n % 2, :], ALU.add).then_inc(S.accd, 1)

                def clear_sum():
                    link(v.memset(acc, 0.0))

                def tables(sub):
                    at = sub * 3 * KC
                    gp = lp[:, GPRE + sub * KC:GPRE + (sub + 1) * KC].unsqueeze(2).broadcast_to([P, KC, NB + 1])
                    gq = lp[:, GPOST + sub * KC:GPOST + (sub + 1) * KC].unsqueeze(2).broadcast_to([P, KC, NB + 1])
                    link(v.scalar_tensor_tensor(atab[:], ada[:, at + KC:at + 2 * KC, :], 1.0, gp, ALU.add, ALU.mult))
                    link(v.scalar_tensor_tensor(gtab[:], ada[:, at + 2 * KC:at + 3 * KC, :], 1.0, gq, ALU.add, ALU.mult))
                    if sub != 1:
                        link(v.tensor_scalar_mul(gtab[:], gtab[:], 0.5))

                def normalise(n):
                    sub = n - 1
                    dve.wait_ge(S.rs_ready, n)
                    link(v.tensor_tensor(xn[:], x[:], rs[:].unsqueeze(1).broadcast_to([P, KC, T]), ALU.mult))
                    smp = xn[:, :, TP:T]
                    link(v.tensor_tensor(smp, smp, atab[:, :, 1:NB + 1], ALU.mult))
                    link(v.tensor_tensor(smp, smp, ada[:, sub * 3 * KC:sub * 3 * KC + KC, 1:NB + 1], ALU.add))
                    for c in range(KC):
                        last = v.tensor_scalar(xn[:, c, 0:TP], xn[:, c, 0:TP], atab[:, c, 0:1],
                                               ada[:, sub * 3 * KC + c, 0:1], ALU.mult, ALU.add)
                    last.then_inc(S.xn_ready, 1)

                def residual(n):
                    dve.wait_ge(S.yrs_ready, n)
                    rss = rs[:, TP:T].unsqueeze(1).broadcast_to([P, KC, NB])
                    link(v.tensor_tensor(smpt[:], y[:, :, TP:T], gtab[:, :, 1:NB + 1], ALU.mult))
                    link(v.tensor_tensor(smpt[:], smpt[:], rss, ALU.mult))
                    link(v.tensor_tensor(x[:, :, TP:T], x[:, :, TP:T], smpt[:], ALU.add))
                    for c in range(KC):
                        t = ft[:, c % 2, 0:TP]
                        link(v.scalar_tensor_tensor(t, y[:, c, 0:TP], gtab[:, c, 0:1], rs[:, 0:TP], ALU.mult, ALU.mult))
                        v.tensor_tensor(x[:, c, 0:TP], x[:, c, 0:TP], t, ALU.add).then_inc(S.x_fin, 1)
                    dve.wait_ge(S.x_fin, n * KC)

                def down():
                    clear_sum()
                    with dve.Fori(0, 2) as i, slots.loop(i, 2, [1] * 4), products.count.loop(i, 2, 4), sums.loop(i, 2, 4):
                        for k in range(4):
                            slots.take(1)
                            sum_squares()

                with dve.Fori(0, 2) as i, slots.loop(i, 2, [1] * 4):
                    for _ in ada_rows():
                        pass
                    ada_columns(i)
                dve.wait_ge(S.ada_evac, 3)
                tables(0)
                normalise(1)
                with dve.Fori(0, 4) as i, slots.loop(i, 4, [1, 2] * 4), products.count.loop(i, 4, 8), \
                        exps.loop(i, 4, 4), link.loop(i, 4, 12):
                    rows_of = ada_rows()
                    for k in range(4):
                        next(rows_of)
                        if k == 3:
                            next(rows_of)
                        ffn_slot(k, i * 4 + k)
                    ada_columns(i + 2)
                for k in range(16, FC):
                    ffn_slot(k, k)
                down()
                residual(1)
                dve.wait_ge(S.ada_evac, 7)
                tables(1)
                normalise(2)

                for s in range(2):
                    slots.take(2)
                    products.take()
                    products.take()
                dve.wait_ge(S.evac, products.count.n + 4)
                for h in range(2):
                    a, e = 64 * h, 64 * h + 64
                    for c in range(HEADS):
                        last = v.tensor_copy(qm[a:e, :, c, 2 * c + h], ob[a:e, c, TP:T])
                last.then_inc(S.qmr, 1)
                link(v.memset(gi[:], 0.0))
                link(v.memset(gf[:], 0.0))

                before_a = products.count.n
                with dve.Fori(0, HEADS) as i, slots.loop(i, HEADS, [3] * 4), products.count.loop(i, HEADS, 12), \
                        link.loop(i, HEADS, 31):
                    for k in range(4):
                        slots.take(3)
                        for n in range(3):
                            products.take()
                    link(v.tensor_copy(lbh[:], lbt[:, bds(layer * HEADS + i, 1), :].rearrange("p a b -> p (a b)")))
                    link(v.memset(sct[:], 0.0))
                    dve.wait_ge(S.tr, i + 1)
                    v.tensor_copy(vi[:], ps[:, M0, :].rearrange("p (n t) -> p n t", n=4)).then_inc(S.vir, 1)
                    dve.wait_ge(S.hpar, i * 32 + 32)
                    dve.wait_ge(S.zz, i + 1)
                    for h in range(2):
                        last = v.tensor_scalar(zp[:, h, :], ps[:, M1 + h, 0:384], SB_SCALE, hp[:, SBB2 + h:SBB2 + h + 1],
                                               ALU.mult, ALU.add)
                    last.then_inc(S.zpr, 1)
                    dve.wait_ge(S.l1r, i + 1)
                    link(v.scalar_tensor_tensor(w2, pj[:, HF_, :], 0.0, w1, ALU.min, ALU.subtract))
                    link(v.tensor_scalar(w2, w2, lbh[:, 1:2], None, ALU.add))
                    v.tensor_scalar(w3, w2, lbh[:, 0:1], None, ALU.subtract).then_inc(S.ur, 1)
                    v.tensor_tensor(w4, w2, pj[:, HF_, :], ALU.subtract).then_inc(S.tzr, 1)
                    def cw(j):
                        return hp[:, CW + j:CW + j + 1]
                    xcp, xcs = xc[:, 0:TP], xc[:, TP:T]
                    link(v.tensor_scalar(xcp, xp[:, 0:TP], cw(0), hp[:, CBIAS:CBIAS + 1], ALU.mult, ALU.add))
                    link(v.tensor_scalar(xcs, xp[:, 3 + TP:3 + T], cw(3), hp[:, CBIAS:CBIAS + 1], ALU.mult, ALU.add))
                    for j in range(1, 4):
                        link(v.scalar_tensor_tensor(xcp, xp[:, j:j + TP], cw(j), xcp, ALU.mult, ALU.add))
                    for j in range(3):
                        ins_ = v.scalar_tensor_tensor(xcs, hp[:, CST + 8 * j:CST + 8 * j + 8], cw(j), xcs, ALU.mult, ALU.add)
                        link(ins_) if j < 2 else ins_.then_inc(S.accr, 1)
                    dve.wait_ge(S.lnr, i + 1)
                    link(v.scalar_tensor_tensor(spt, zp, 0.0, sbt, ALU.max, ALU.add))
                    for h in range(2):
                        d = diag_blocks(spt, h)
                        last = v.tensor_tensor(d, d, over2(strict01), ALU.mult)
                    last.then_inc(S.spr, 1)
                    dve.wait_ge(S.xer, i + 1)
                    link(v.tensor_scalar_add(fe[:, 0, :], fe[:, 0, :], 1.0))
                    link(v.reciprocal(fe[:, 0, :], fe[:, 0, :]))
                    v.tensor_tensor(xc[:], xc[:], fe[:, 0, :], ALU.mult).then_inc(S.xcr, 1)
                    dve.wait_ge(S.l2r, i + 1)
                    link(v.scalar_tensor_tensor(w5, w2, lbh[:, 0:1], w3, ALU.max, ALU.add))
                    link(v.tensor_tensor_scan(w1[:, 0:TP], onerow, w5[:, 0:TP], 0.0, ALU.mult, ALU.add))
                    dve.wait_ge(S.suf, i + 1)
                    link(v.tensor_tensor(zp, zp, ps[:, M1:M1 + 2, 0:384], ALU.subtract))
                    for h in range(2):
                        d = diag_blocks(zp, h)
                        last = v.scalar_tensor_tensor(d, d, 0.0, over2(strictneg), ALU.min, ALU.add)
                    last.then_inc(S.t_ready, 1)
                    dve.wait_ge(S.sge, i + 1)
                    link(v.tensor_scalar_add(sgt[:], sgt[:], 1.0))
                    link(v.reciprocal(sgt[:], sgt[:]))
                    link(v.tensor_copy(mo[:, i, :], sgt[:, 1, :]))
                    link(v.tensor_tensor(sgt[:, 0, :], sgt[:, 0, :], pj[:, HG_, :], ALU.mult))
                    dve.wait_ge(S.av, i + 1)
                    v.tensor_copy(ob[:, i, 0:TP], ps[:, M0, 0:TP]).then_inc(S.obr, 1)
                    for lv in range(LEVELS):
                        half = 1 << lv
                        src = w1[:, 0:TP].rearrange("p (n w) -> p n w", w=2 * half)
                        v.tensor_tensor(e8[:, lv, :].rearrange("p (n w) -> p n w", w=2 * half), src,
                                        src[:, :, half - 1:half].broadcast_to([P, TP // (2 * half), 2 * half]), ALU.subtract)
                    v.tensor_scalar(w6[:, 0:TP], w1[:, 0:TP], w1[:, TP - 1:TP], None, ALU.subtract).then_inc(S.dlr, 1)
                    dve.wait_ge(S.gt, i + 1)
                    link(v.tensor_tensor(gi[:], gi[:], ps[0:4, M1, 0:T], ALU.add))
                    v.tensor_tensor(gf[:], gf[:], ps[0:4, M2, 0:T], ALU.add).then_inc(S.gir, 1)
                    dve.wait_ge(S.elr, i + 1)
                    v.tensor_tensor(ql, e8, pj[:, HQ_, 0:TP].unsqueeze(1).broadcast_to([P, LEVELS, TP]), ALU.mult)\
                        .then_inc(S.qlr, 1)
                    dve.wait_ge(S.kder, i + 1)
                    dve.wait_ge(S.khr, i + 1)
                    v.tensor_tensor(w6[:, 0:TP], w6[:, 0:TP], w4[:, 0:TP], ALU.mult).then_inc(S.kdr, 1)

                    def pick(bank, at, mask):
                        return v.copy_predicated(sct[:, 0:3:2, :], over2(hmask[:, mask, :]),
                                                 ps[:, bank, at:at + TP].rearrange("p (t q) -> p t q", t=2))

                    for n, (bank, first) in enumerate(((M1, 0), (M2, 2), (M0, None), (M1, 4), (M2, 6))):
                        dve.wait_ge(S.lvl, i * 5 + n + 1)
                        if first is None:
                            v.tensor_copy(sct[:, 1, :], ps[:, M0, 0:P]).then_inc(S.lvc, 1)
                        else:
                            apart(dve)
                            link(pick(bank, 0, first))
                            apart(dve)
                            pick(bank, TP, first + 1).then_inc(S.lvc, 1)
                        dve.wait_ge(S.lvc, i * 5 + n + 1)
                    dve.wait_ge(S.kdtp, i + 1)
                    v.tensor_copy(kdt[:], ps[:, M0, 0:TP].rearrange("p (t q) -> p t q", t=2)).then_inc(S.kdtr, 1)
                    dve.wait_ge(S.ibr, i + 1)
                    dve.wait_ge(S.klr, i + 1)
                    link(v.tensor_tensor(tt8, ps[:, M1:M1 + 2, :].rearrange("p a (b k) -> p (a b) k", k=P),
                                         w4[:, TP:T].unsqueeze(2).broadcast_to([P, NB, P]), ALU.mult))
                    dve.wait_ge(S.snm, i + 1)
                    v.tensor_tensor(sn8[:], sn8[:], tt8, ALU.add).then_inc(S.snr, 1)
                    dve.wait_ge(page_free[3], i * 2 + 3)
                    v.tensor_copy(rbuf[:], ps[:, Z, :]).then_inc(S.zrow, 1)
                    dve.wait_ge(S.evac, i * 12 + (before_a + 12 + 4))
                    g4 = gates[:, bds(i * 4, 4), :]
                    link(v.tensor_scalar_add(g4, g4, 1.0))
                    apart(dve)
                    link(v.reciprocal(g4, g4))
                    dve.wait_ge(S.rsh, i + 2)
                    link(v.scalar_tensor_tensor(ot[:], ot[:], hp[:, HGG:HGG + 1], rs[:], ALU.mult, ALU.mult))
                    link(v.tensor_tensor(oa[:, i, :], ot[:], sgt[:, 0, :], ALU.mult))
                    dve.wait_ge(S.ztr, i + 1)
                    for n in range(4):
                        e, u = n // 2, n % 2
                        last = v.scalar_tensor_tensor(
                            zs[:, bds(i * 128 + e * 64, 64)].rearrange("p (j u h) -> p j u h", j=4, u=2)[:, :, u, :],
                            ps[:, Z, n * P:(n + 1) * P].rearrange("p (j h) -> p j h", j=4)[:, :, 0:SBH], SB_SCALE,
                            lp[:, SBB:SBB + SBH].unsqueeze(1).broadcast_to([P, 4, SBH]), ALU.mult, ALU.add)
                    last.then_inc(S.dve_it, 1)
                    dve.wait_ge(S.dve_it, i + 2)

                link(v.tensor_scalar(gf[:], gf[:], lp4[:, 1:2], None, ALU.add))
                link(v.tensor_scalar(gi[:], gi[:], lp4[:, 0:1], None, ALU.add))
                v.nop().then_inc(S.rl1, 1)
                dve.wait_ge(S.lnsr, 1)
                v.scalar_tensor_tensor(zt, zs[:], 0.0, zt, ALU.max, ALU.add).then_inc(S.spsr, 1)
                dve.wait_ge(S.rl1, 2)
                link(v.scalar_tensor_tensor(gf[:], gf[:], 0.0, r4[:, 1, :], ALU.min, ALU.subtract))
                link(v.tensor_tensor_scan(r4[:, 1, 0:TP], onerow[0:4, :], gf[:, 0:TP], 0.0, ALU.mult, ALU.add))
                v.tensor_tensor(r4[:, 0, 0:TP], gi[:, 0:TP], r4[:, 1, 0:TP], ALU.subtract).then_inc(S.rw1, 1)
                dve.wait_ge(S.rw1, 1)
                link(v.tensor_tensor_scan(rows[:, 0:TP], onerow[0:4, :], r4[:, 0, 0:TP], 0.0, ALU.mult, ALU.max))
                link(v.tensor_tensor(rows[:, TP + 24:], rows[:, 0:TP], r4[:, 1, 0:TP], ALU.add))
                a, ms, its = r4[:, 2, 0:8], r4[:, 2, 8:16], gi[:, TP:T]
                link(v.tensor_tensor(a, gf[:, TP:T], lp4[:, 2:10], ALU.add))
                link(v.tensor_tensor(ms, a, its, ALU.max))
                v.tensor_tensor(rows[:, TP:TP + 8], its, ms, ALU.subtract)
                v.tensor_tensor(rows[:, TP + 8:TP + 16], a, ms, ALU.subtract)
                v.tensor_scalar_mul(rows[:, TP + 16:TP + 24], ms, -1.0).then_inc(S.rw2, 1)
                dve.wait_ge(S.sufs, 1)
                v.tensor_tensor(zs[:], zs[:], ps[:, Z, :], ALU.subtract).then_inc(S.t2r, 1)
                dve.wait_ge(S.rw3, 1)
                v.tensor_tensor(bd, rows.unsqueeze(1).broadcast_to([4, 4, nrow]),
                                consts[0:4, 0, 0:4].unsqueeze(2).broadcast_to([4, 4, nrow]), ALU.mult).then_inc(S.bdr, 1)
                dve.wait_ge(S.gcp, 1)
                v.tensor_copy(gcol[:], ps[:, M0, 0:8].rearrange("p (t h) -> p t h", t=2)).then_inc(S.gcr, 1)
                dve.wait_ge(S.gcr, 1)

                def value_rows(n):
                    dve.wait_ge(S.vrd, n + 1)
                    dve.wait_ge(page_free[3], n + (NB + 2))
                    v.tensor_copy(rbuf[:], ps[:, 3, :]).then_inc(S.vrow, 1)

                dve.sem_inc(S.vrd, 1)
                v.memset(ps[:, 3, :], 0.0).then_inc(S.vrow, 1)
                at, products.pos = slots.pos, 0
                before_b = products.count.n
                with dve.Fori(0, HEADS) as i, slots.loop(i, HEADS, [2], at), products.count.loop(i, HEADS, 2), \
                        link.loop(i, HEADS, 14):
                    slots.take(2, at)
                    products.take(2)
                    products.take(2)
                    dve.wait_ge(S.trb, i + 1)
                    link(v.tensor_copy(vk, ps[:, M0, :].rearrange("p (n t) -> p n t", n=4)))
                    dve.wait_ge(S.kqr, i + 1)
                    v.tensor_scalar(dm[:, 0:TP], ps[:, M2, 0:TP], gcol[:, 0, bds(i, 1)], 0.0, ALU.subtract, ALU.max)
                    v.tensor_scalar(dm[:, TP:TP + P], ps[:, M2, P:TP], gcol[:, 1, bds(i, 1)], 0.0, ALU.subtract, ALU.max)
                    link(v.tensor_copy(sw[:], ps[:, M2, TP:TP + 24]))
                    d = dm.rearrange("p (n t) -> p n t", t=P)[:, 0:3:2, :]
                    v.tensor_tensor(d, d, over2(causalpos), ALU.add).then_inc(S.exr, 1)
                    smp = slice(TP, T)
                    wv, dec = sw[:, 0:8], sw[:, 8:16]
                    link(v.tensor_tensor(s8a[:], vs[:, smp], wv, ALU.mult))
                    link(v.tensor_tensor(s8c[:], lp[:, bds(i * NB + N0, NB)], dec, ALU.mult))
                    link(v.tensor_tensor(s8b[:], ks[:, smp], wv, ALU.mult))
                    v.tensor_tensor(s8c[:], s8c[:], s8b[:], ALU.add).then_inc(S.nnr, 1)
                    dve.wait_ge(S.nnr, i + 1)
                    v.tensor_tensor(s8b[:], s8c[:], qs[:, smp], ALU.mult).then_inc(S.nqr, 1)
                    dve.wait_ge(S.dmr, i + 1)
                    v.tensor_tensor(wt, dm, ps[:, M1, 0:384], ALU.mult)
                    v.tensor_scalar(vw2[:, 0, :], vk[:, 0, :], dm[:, TP - 1:TP], None, ALU.mult)
                    v.tensor_scalar(vw2[:, 1, :], vk[:, 1, :], dm[:, TP + P - 1:TP + P], None, ALU.mult)\
                        .then_inc(S.vwr, 1)
                    value_rows(i * 2)
                    dve.wait_ge(S.adr, i + 1)
                    link(v.tensor_tensor(w1[:, 0:TP], w1[:, 0:TP], w3[:, 0:TP], ALU.max))
                    link(v.reciprocal(w1[:, 0:TP], w1[:, 0:TP]))
                    v.tensor_tensor(ot[:, 0:TP], ps[:, M0, 0:TP], w1[:, 0:TP], ALU.mult).then_inc(S.htr, 1)
                    dve.wait_ge(S.kbr, i + 1)
                    bank2 = ps[:, M1:M1 + 2, :].rearrange("p a (b k) -> p (a b) k", k=P)
                    link(v.tensor_tensor(tt8, bank2, s8a[:].unsqueeze(2).broadcast_to([P, NB, P]), ALU.mult))
                    dve.wait_ge(S.cnp, i + 1)
                    v.tensor_tensor(sn8[:], sn8[:], tt8, ALU.add).then_inc(S.cnr, 1)
                    dve.wait_ge(S.cnr, i + 1)
                    dve.wait_ge(S.qbr, i + 1)
                    link(v.tensor_tensor(tt8, sn8[:], bank2, ALU.mult))
                    link(v.tensor_reduce(w3[:, smp], tt8, AX.X, ALU.add))
                    dve.wait_ge(S.dna, i + 1)
                    link(v.tensor_tensor(w1[:, smp], w1[:, smp], sw[:, 16:24], ALU.max))
                    link(v.reciprocal(w1[:, smp], w1[:, smp]))
                    v.tensor_tensor(ot[:, smp], w3[:, smp], w1[:, smp], ALU.mult).then_inc(S.otr, 1)
                    value_rows(i * 2 + 1)
                    dve.wait_ge(S.evac, i * 2 + (before_b + 2 + 4))
                    g2 = gates[:, bds(i * 2 + 16, 2), :]
                    link(v.tensor_scalar_add(g2, g2, 1.0))
                    apart(dve)
                    v.reciprocal(g2, g2)
                    dve.wait_ge(S.rsb, i + 1)
                    link(v.scalar_tensor_tensor(ot[:], ot[:], lp[:, bds(i + MLG, 1)], rs[:], ALU.mult, ALU.mult))
                    v.tensor_tensor(oc[:, i, :], ot[:], mo[:, i, :], ALU.mult).then_inc(S.dve_it, 1)
                    dve.wait_ge(S.dve_it, i + HEADS + 2)

                dve.wait_ge(S.vrd, NB + 1)
                for h in range(2):
                    a, e = 64 * h, 64 * h + 64
                    last = v.tensor_copy(ob[a:e, :, TP:T],
                                         ps[a:e, 2, 0:64].rearrange("p (b c h) -> p c b h", c=HEADS, h=2)[:, :, :, h])
                last.then_inc(S.dve_it, 1)
                products.pos = 0
                for s in range(4):
                    r, _, before = slots.take(6)
                    for n in range(2):
                        c = s * 2 + n
                        for br in range(3):
                            b, count = products.take()
                            dve.wait_ge(slot_done[r], before + n * 3 + br + 2)
                            dst = merged[:, c, :] if br == 0 else ft[:, br - 1, :]
                            v.tensor_tensor(dst, ps[:, b, 0:T], gates[:, br * KC + c, :], ALU.mult).then_inc(S.evac, 1)
                            dve.wait_ge(S.evac, count + 5)
                            if br:
                                ins_ = v.tensor_tensor(merged[:, c, :], merged[:, c, :], dst, ALU.add)
                                if br == 2:
                                    ins_.then_inc(S.mg, 1)
                                    dve.wait_ge(S.mg, c + 1)
                                else:
                                    link(ins_)
                clear_sum()
                for s in range(4):
                    slots.take(2)
                    for n in range(2):
                        sum_squares()
                residual(2)
                tables(2)
                normalise(3)
                with dve.Fori(0, 5) as i, slots.loop(i, 5, [2] * 4), products.count.loop(i, 5, 8), exps.loop(i, 5, 4), \
                        link.loop(i, 5, 12):
                    for k in range(4):
                        ffn_slot(k, i * 4 + k)
                for k in range(2):
                    ffn_slot(k, 20 + k)
                down()
                residual(3)

            @block.scalar
            def _(act):
                slots, products, exps, sums = Slots(), Products(), Count(), Count()
                link = Chain(act, S.achain)
                A = nc.scalar.activation
                act.sem_inc(S.rsh, 1)
                act.sem_inc(S.store, 16)

                def squares(n):
                    for c in range(KC):
                        if n > 1:
                            act.wait_ge(S.x_fin, (n - 2) * KC + c + 1)
                        A(xn[:, c, :], x[:, c, :], ACT.Square).then_inc(S.x2_ready, 1)

                def rsqrt(bank, width):
                    link(A(rs[:], ps[:, bank, 0:T], ACT.Ln, scale=1.0 / width, bias=eps[:]))
                    return A(rs[:], rs[:], ACT.Exp, scale=-0.5)

                def pre(n):
                    squares(n)
                    act.wait_ge(S.ss_ready, n)
                    rsqrt(Z, D).then_inc(S.rs_ready, 1)

                def post(n):
                    act.wait_ge(S.yss_ready, n)
                    rsqrt(Z, D).then_inc(S.yrs_ready, 1)

                def ffn_slot(k):
                    r, _, before = slots.take(2)
                    b, _ = products.take()
                    products.take()
                    exps()
                    act.wait_ge(slot_done[r], before + 2)
                    A(fe[:, k % 2, :], ps[:, b, 0:T], ACT.Exp, scale=-1.0).then_inc(S.e_ready, 1)

                def y_chunk(r, done, c):
                    n = sums()
                    b, _ = products.take()
                    act.wait_ge(slot_done[r], done)
                    act.wait_ge(S.accd, n + 1)
                    A(y[:, c, :], ps[:, b, 0:T], ACT.Copy)
                    A(sq[:, sums.n % 2, :], ps[:, b, 0:T], ACT.Square).then_inc(S.evac, 1)

                def down():
                    with act.Fori(0, 2) as i, slots.loop(i, 2, [1] * 4), products.count.loop(i, 2, 4), sums.loop(i, 2, 4):
                        for k in range(4):
                            r, _, before = slots.take(1)
                            y_chunk(r, before + 2, i * 4 + k)

                for k in range(8):
                    slots.take(1)
                pre(1)
                with act.Fori(0, 4) as i, slots.loop(i, 4, [1, 2] * 4), products.count.loop(i, 4, 8), \
                        exps.loop(i, 4, 4):
                    for k in range(4):
                        slots.take(1)
                        ffn_slot(k)
                for k in range(16, FC):
                    ffn_slot(k)
                down()
                post(1)
                pre(2)

                def evac(r, done, dst, exp=False):
                    b, _ = products.take()
                    act.wait_ge(slot_done[r], done)
                    A(dst, ps[:, b, 0:T], ACT.Exp if exp else ACT.Copy, scale=-1.0 if exp else 1.0).then_inc(S.evac, 1)

                for s in range(2):
                    r, _, before = slots.take(2)
                    for n in range(2):
                        evac(r, before + 2 + n, ob[:, s * 2 + n, :])

                def softplus_tail(t, src):
                    link(A(t, src, ACT.Abs))
                    link(A(t, t, ACT.Exp, scale=-1.0))
                    return A(t, t, ACT.Ln, bias=1.0)

                before_a = products.count.n
                with act.Fori(0, HEADS) as i, slots.loop(i, HEADS, [3] * 4), products.count.loop(i, HEADS, 12), \
                        link.loop(i, HEADS, 10):
                    act.wait_ge(S.dve_it, i + 1)
                    act.wait_ge(S.pool_it, i + 1)
                    act.dma_start(hp[:], ins.head_par[layer, i]).then_inc(S.hpar, 16)
                    act.dma_start(st8[:], ins.hgrn[layer, i]).then_inc(S.hpar, 16)
                    dests = [pj[:, SK_, :], pj[:, SV_, :], xp[:, 3:3 + T], pj[:, HQ_, :], pj[:, HF_, :], pj[:, HI_, :],
                             pj[:, HG_, :], sgt[:, 1, :], gates[:, i * 4, :]]
                    for k in range(3):
                        r, _, before = slots.take(3)
                        for n in range(3):
                            evac(r, before + 2 + n, dests[3 * k + n], exp=3 * k + n >= 7)
                    act.wait_ge(S.evac, i * 12 + (before_a + 7 + 4))
                    act.dma_start(outs.k[layer, :, i, :], pj[:, SK_, :]).then_inc(S.store, 16)
                    act.dma_start(outs.v[layer, :, i, :], pj[:, SV_, :]).then_inc(S.store, 16)
                    act.dma_start(outs.conv_p[layer, i], xp[:, TP:TP + 3]).then_inc(S.store, 16)
                    softplus_tail(w1, pj[:, HF_, :]).then_inc(S.l1r, 1)
                    act.wait_ge(S.pchain, i + 1)
                    act.dma_start(outs.conv_s[layer, i], nbs[:].rearrange("p j b -> p (j b)")).then_inc(S.store, 16)
                    act.wait_ge(S.zpr, i + 1)
                    softplus_tail(sbt, zp).then_inc(S.lnr, 1)
                    act.wait_ge(S.evac, i * 12 + (before_a + 8 + 4))
                    A(sgt[:, 0, :], pj[:, HG_, :], ACT.Exp, scale=-1.0).then_inc(S.sge, 1)
                    act.wait_ge(S.accr, i + 1)
                    A(fe[:, 0, :], xc[:], ACT.Exp, scale=-1.0).then_inc(S.xer, 1)
                    act.wait_ge(S.ur, i + 1)
                    softplus_tail(w3, w3).then_inc(S.l2r, 1)
                    r, _, before = slots.take(3)
                    evac(r, before + 2, gates[:, i * 4 + 1, :], exp=True)
                    act.wait_ge(S.tzr, i + 1)
                    A(w4, w4, ACT.Exp).then_inc(S.khr, 1)
                    act.wait_ge(S.t_ready, i + 1)
                    A(sbt, zp, ACT.Exp).then_inc(S.ar, 1)
                    evac(r, before + 3, gates[:, i * 4 + 2, :], exp=True)
                    act.wait_ge(S.qkv_ps, i + 1)
                    for j, b in enumerate((M1, M2, M0)):
                        last = A(qkv[:, j, i, :], ps[:, b, 0:T], ACT.Copy)
                    last.then_inc(S.qkv_sb, 1)
                    act.wait_ge(S.dlr, i + 1)
                    link(A(e8, e8, ACT.Abs))
                    A(e8, e8, ACT.Exp, scale=-1.0).then_inc(S.elr, 1)
                    A(w6[:, 0:TP], w6[:, 0:TP], ACT.Exp, scale=-1.0).then_inc(S.kder, 1)
                    A(s8a[:], w5[:, TP:T], ACT.Exp).then_inc(S.fsr, 1)
                    evac(r, before + 4, gates[:, i * 4 + 3, :], exp=True)
                    act.wait_ge(S.ho, i + 1)
                    A(ot[:, 0:TP], ps[:, M0, 0:TP], ACT.Copy)
                    link(A(hsp[:], ps[:, M0, 384:512], ACT.Copy))
                    act.dma_start(outs.hgrn_p[layer, i], hsp[:]).then_inc(S.store, 16)
                    act.wait_ge(S.snr, i + 1)
                    act.dma_start(outs.hgrn_s[layer, i], sn8[:].rearrange("p b k -> p (b k)")).then_inc(S.store, 16)
                    act.wait_ge(S.hos, i + 1)
                    link(A(ot[:, TP:T], ps[:, M1, 0:NB], ACT.Copy))
                    A(w2, ot[:], ACT.Square).then_inc(S.osq, 1)
                    act.wait_ge(S.hss, i + 1)
                    rsqrt(M2, P).then_inc(S.rsh, 1)
                    act.wait_ge(S.store, i * (16 * STORES_A) + 16 * (STORES_A + 1))

                act.wait_ge(S.dve_it, HEADS + 1)
                softplus_tail(zt, zs[:]).then_inc(S.lnsr, 1)
                act.wait_ge(S.rl1, 1)
                softplus_tail(r4[:, 1, :], gf[:]).then_inc(S.rl1, 1)
                act.wait_ge(S.rw2, 1)
                A(rows[:, TP:TP + 24], rows[:, TP:TP + 24], ACT.Exp).then_inc(S.rw3, 1)
                act.dma_start(outs.m_p[layer], rows[:, 2 * TP + 23:2 * TP + 24]).then_inc(S.store, 16)
                act.dma_start(outs.m_s[layer], r4[:, 2, 8:16]).then_inc(S.store, 16)
                act.wait_ge(S.t2r, 1)
                A(zs[:], zs[:], ACT.Exp).then_inc(S.asr, 1)
                act.wait_ge(S.store, 16 * (STORES_A * HEADS + 3))

                at, products.pos = slots.pos, 0
                with act.Fori(0, HEADS) as i, slots.loop(i, HEADS, [2], at), products.count.loop(i, HEADS, 2), \
                        link.loop(i, HEADS, 1):
                    act.wait_ge(S.dve_it, i + HEADS + 1)
                    act.dma_start(st8[:], ins.ml_c[layer, i]).then_inc(S.hpar, 16)
                    A(ks, qkv[:, 1, i, :], ACT.Copy, scale=ML_SCALE).then_inc(S.stg, 1)
                    act.wait_ge(S.exr, i + 1)
                    A(dm, dm, ACT.Exp, scale=-1.0).then_inc(S.dmr, 1)
                    r, _, before = slots.take(2, at)
                    for n in range(2):
                        b, _ = products.take(2)
                        act.wait_ge(slot_done[r], before + 2 + n)
                        A(gates[:, i * 2 + (16 + n), :], ps[:, b, 0:T], ACT.Exp, scale=-1.0).then_inc(S.evac, 1)
                    act.wait_ge(S.nnr, i + 1)
                    act.dma_start(outs.n_s[layer, :, i, :], s8c[:]).then_inc(S.store, 16)
                    act.wait_ge(S.ndr, i + 1)
                    A(w1[:, 0:TP], ps[:, M1, 0:TP], ACT.Abs)
                    A(w3[:, 0:TP], ps[:, Z, 0:TP], ACT.Exp, scale=-1.0).then_inc(S.adr, 1)
                    act.wait_ge(S.cst, i + 1)
                    A(hsp[:], ps[:, M2, 0:P], ACT.Copy)
                    A(nst[:], ps[:, M2, P:P + 1], ACT.Copy).then_inc(S.cev, 1)
                    act.wait_ge(S.cev, i + 1)
                    act.dma_start(outs.c_p[layer, i], hsp[:]).then_inc(S.store, 16)
                    act.dma_start(outs.n_p[layer, i], nst[:]).then_inc(S.store, 16)
                    act.wait_ge(S.dns, i + 1)
                    A(w1[:, TP:T], ps[:, M0, 0:NB], ACT.Abs).then_inc(S.dna, 1)
                    act.wait_ge(S.cnr, i + 1)
                    act.dma_start(outs.c_s[layer, i], sn8[:].rearrange("p b k -> p (b k)")).then_inc(S.store, 16)
                    act.wait_ge(S.otr, i + 1)
                    A(w2, ot[:], ACT.Square).then_inc(S.sqh, 1)
                    act.wait_ge(S.hbs, i + 1)
                    rsqrt(M0, P).then_inc(S.rsb, 1)
                    act.wait_ge(S.store, i * (16 * STORES_B) + 16 * (STORES_A * HEADS + 3 + STORES_B))

                products.pos = 0
                for s in range(4):
                    slots.take(6)
                    for n in range(6):
                        products.take()
                for s in range(4):
                    r, _, before = slots.take(2)
                    for n in range(2):
                        y_chunk(r, before + 2 + n, s * 2 + n)
                post(2)
                pre(3)
                with act.Fori(0, 5) as i, slots.loop(i, 5, [2] * 4), products.count.loop(i, 5, 8), exps.loop(i, 5, 4):
                    for k in range(4):
                        ffn_slot(k)
                for k in range(2):
                    ffn_slot(k)
                down()
                post(3)

            @block.gpsimd
            def _(pool):
                g = nc.gpsimd
                pool.sem_inc(S.pool_it, 1)
                identb = consts[:, 0:1, :].broadcast_to([P, NB, P])
                before_a = 2 * FC + KC + HEADS

                def diagonal(src):
                    return g.tensor_tensor(dg8, identb, src.unsqueeze(2).broadcast_to([P, NB, P]), ALU.mult)

                with pool.Fori(0, HEADS) as i:
                    pool.wait_ge(S.dve_it, i + 1)
                    pool.wait_ge(S.store, i * (16 * STORES_A) + 16)
                    pool.wait_ge(S.evac, i * 12 + (before_a + 4))
                    apart(pool)
                    g.tensor_copy(pj[:, SQ_, :], ob[:, i, :]).then_inc(S.sqc, 1)
                    pool.wait_ge(S.hpar, i * 32 + 32)
                    pool.wait_ge(S.evac, i * 12 + (before_a + 3 + 4))
                    apart(pool)
                    g.tensor_copy(nbs[:, 0:2, :], hp[:, CST + 8:CST + 24].rearrange("p (j b) -> p j b", j=2))
                    g.tensor_copy(nbs[:, 2, :], xp[:, 3 + TP:3 + T]).then_inc(S.pchain, 1)
                    pool.wait_ge(S.qmr, 1)
                    for e in range(2):
                        last = g.tensor_copy(qst[:, e, :, :], qm[:, i * 2 + e, :, :])
                    last.then_inc(S.qstr, 1)
                    pool.wait_ge(S.fsr, i + 1)
                    g.tensor_tensor(sn8[:], st8[:], s8a[:].unsqueeze(2).broadcast_to([P, NB, P]), ALU.mult)\
                        .then_inc(S.snm, 1)
                    pool.wait_ge(S.khr, i + 1)
                    pool.wait_ge(S.qlr, i + 1)
                    g.tensor_tensor(kl, e8, w4[:, 0:TP].unsqueeze(1).broadcast_to([P, LEVELS, TP]), ALU.mult)\
                        .then_inc(S.klr, 1)
                    pool.wait_ge(S.lvc, i * 5 + 5)
                    diagonal(pj[:, HI_, TP:T]).then_inc(S.snp, 1)
                    pool.wait_ge(S.snp, i + 1)
                    pool.sem_inc(S.pool_it, 1)

                with pool.Fori(0, HEADS) as i:
                    pool.wait_ge(S.dve_it, i + (HEADS + 1))
                    pool.wait_ge(S.store, i * (16 * STORES_B) + 16 * (STORES_A * HEADS + 3))
                    pool.wait_ge(S.vrd, i * 2 + 1)
                    pool.wait_ge(S.asr, 1)
                    for e in range(2):
                        last = g.tensor_copy(ast[:, e, :], zs[:, bds(i * 128 + e * 64, 64)])
                    last.then_inc(S.astr, 1)
                    g.tensor_copy(vs, qkv[:, 2, i, :]).then_inc(S.stg, 1)
                    g.tensor_copy(qs, qkv[:, 0, i, :]).then_inc(S.stg, 1)
                    pool.wait_ge(S.stg, i * 3 + 3)
                    diagonal(ks[:, TP:T]).then_inc(S.snp, 1)
                    pool.wait_ge(S.hpar, i * 16 + (32 * HEADS + 16))
                    pool.wait_ge(S.exr, i + 1)
                    g.tensor_tensor(sn8[:], st8[:], sw[:, 8:16].unsqueeze(2).broadcast_to([P, NB, P]), ALU.mult)\
                        .then_inc(S.cnp, 1)
                    pool.wait_ge(S.kbr, i + 1)
                    diagonal(qs[:, TP:T]).then_inc(S.snp, 1)

        with nc.Fori(0, DEPTH) as layer:
            with nc.Block() as block:
                one_layer(block, layer)
            clear_all()

        with nc.Block() as block:
            @block.sync
            def _(sp):
                sp.dma_start(outs.y, x[:]).then_inc(S.store, 16)
                sp.wait_ge(S.store, 16)


def over2(mask):
    return mask.unsqueeze(1).broadcast_to([P, 2, P])


def diag_blocks(t, h):
    return t[:, h, :].rearrange("p (n t) -> p n t", t=P)[:, 0:3:2, :]


def kernel(**inputs):
    import numpy as np
    import concourse.bacc as bacc
    from concourse.bass_utils import run_bass_kernel_spmd

    a = {k: np.asarray(v) for k, v in inputs.items()}

    def tokens(prompt, sample):
        t = np.concatenate([prompt.reshape(-1, D), sample.reshape(-1, D)], 0)
        return t.T.reshape(KC, P, -1).transpose(1, 0, 2)

    def tiles(w, per_slot):
        *lead, k, n = w.shape
        n_lead = len(lead)
        t = w.reshape(*lead, k // P, P, n // P // per_slot, per_slot, P)
        ax = list(range(n_lead))
        t = t.transpose(*ax, n_lead + 2, n_lead + 1, n_lead + 3, n_lead, n_lead + 4)
        return t.reshape(*lead, n // P // per_slot, P, per_slot * (k // P) * P)

    def chunk_cols(v, last=False):
        return v.reshape(DEPTH, -1, P).transpose(0, 2, 1)

    w_in = a["w_in"].reshape(DEPTH, D, -1, P)
    first = dict(hq=0, hf=4, hi=8, hg=12, sq=16, sk=20, sv=24, mx=28, mo=32, ga=36)
    g0 = first["ga"]
    order_a, order_b = [], []
    for i in range(HEADS):
        order_a += [first[k] + i for k in ("sk", "sv", "mx", "hq", "hf", "hi", "hg", "mo")] + \
                   [g0 + 4 * i + j for j in range(4)]
        order_b += [g0 + 16 + 2 * i + j for j in range(2)]

    def in_cols(order):
        return w_in[:, :, order, :].reshape(DEPTH, D, len(order) * P)

    ffn = a["w_ffn_in"].reshape(DEPTH, 2, D, 2, FC, P).transpose(0, 1, 2, 4, 3, 5).reshape(DEPTH, 2, D, 2 * DFF)
    proj = np.stack([a["w_hg_proj"], a["w_sb_proj"], a["w_ml_proj"]], 1)
    proj = proj.reshape(DEPTH, 3, HEADS, P, 4, 2, P).transpose(0, 4, 3, 5, 1, 2, 6).reshape(DEPTH, 4, P, 24 * P)

    layer_par = np.zeros((DEPTH, P, LPN), np.float32)
    layer_par[:, :, BADA:BADA + ADA_N] = chunk_cols(a["b_ada"])
    layer_par[:, :, GPRE:GPRE + 24] = chunk_cols(a["g_pre"].reshape(DEPTH, -1))
    layer_par[:, :, GPOST:GPOST + 24] = chunk_cols(a["g_post"].reshape(DEPTH, -1))
    layer_par[:, :, SBB:SBB + SBH] = a["sb_bias"][:, None, :]
    layer_par[:, :, N0:N0 + 32] = a["state_mlstm_n"].transpose(1, 3, 2, 0).reshape(DEPTH, P, 32)
    layer_par[:, :, MLG:MLG + 4] = chunk_cols(a["ml_gain"])
    layer_par4 = np.zeros((DEPTH, 4, 2 + NB), np.float32)
    layer_par4[:, :, 0] = a["ml_b_if"][:, 0:4]
    layer_par4[:, :, 1] = a["ml_b_if"][:, 4:8]
    layer_par4[:, :, 2:] = a["state_mlstm_m"].transpose(1, 2, 0)
    head_par = np.zeros((DEPTH, HEADS, P, HPN), np.float32)
    for j, k in enumerate(("ml_wq", "ml_wk", "ml_wv")):
        head_par[:, :, :, WQ + j * P:WQ + (j + 1) * P] = a[k]
    head_par[:, :, :, WIF:WIF + 24] = a["ml_w_if"].reshape(DEPTH, 3, HEADS, P, 8).transpose(0, 2, 3, 1, 4)\
        .reshape(DEPTH, HEADS, P, 24)
    head_par[:, :, :, CW:CW + 4] = a["ml_conv_w"].reshape(DEPTH, 4, HEADS, P).transpose(0, 2, 3, 1)
    head_par[:, :, :, CBIAS] = a["ml_conv_b"].reshape(DEPTH, HEADS, P)
    head_par[:, :, :, HGG] = a["hg_gain"].reshape(DEPTH, HEADS, P)
    head_par[:, :, :, CST:CST + 24] = a["state_mlstm_conv"].reshape(NB, DEPTH, 3, HEADS, P)\
        .transpose(1, 3, 4, 2, 0).reshape(DEPTH, HEADS, P, 24)
    head_par[:, :, :, SBB2:SBB2 + 2] = a["sb_bias"].reshape(DEPTH, HEADS, 1, 2)

    r = np.arange(P)
    k, q = r[:, None], r[None, :]
    consts = np.stack([k == q, k + q >= 0, k >= q, k < q], 1).astype(np.float32)
    consts = np.concatenate([consts, np.where(k < q, 0.0, NEVER)[:, None], np.where(k > q, -NEVER, 0.0)[:, None]], 1)
    masks = [k == q]
    for lv in range(LEVELS - 1):
        half = 1 << lv
        masks.append((k // (2 * half) == q // (2 * half)) & (k % (2 * half) < half) & (q % (2 * half) >= half))
    masks = np.stack(masks, 1)

    w_ada = a["w_ada"].reshape(DEPTH, KC // 2, 2, P, ADA_N // ADA_G, 4, ADA_COLS).transpose(0, 4, 1, 3, 2, 5, 6)
    w_ada = w_ada.reshape(DEPTH, -1, P, 8 * ADA_COLS)
    feeds = dict(
        consts=consts.astype(np.float32), masks=masks.astype(np.float32),
        x=tokens(a["x_prompt"], a["x_sample"]), c=tokens(a["c_prompt"], a["c_sample"]),
        lb=a["hg_lb_logits"].reshape(DEPTH, HEADS, P).transpose(2, 0, 1),
        page_table=a["page_table"].reshape(1, NB * PAGES),
        w_ada=w_ada, sel=np.equal(r[:, None] % 32, np.arange(SBH)).astype(np.float32), w_ffn_in=tiles(ffn, 2), w_ffn_down=tiles(a["w_ffn_down"], 1),
        w_sq=tiles(in_cols([first["sq"] + i for i in range(4)]), 2),
        w_a=tiles(in_cols(order_a), 3), w_b=tiles(in_cols(order_b), 2), w_proj=proj, w_out=tiles(a["w_out"], 2),
        k_pages=a["cache_sb_k"].reshape(PHYS, DEPTH, P, HEADS, P).transpose(1, 0, 4, 3, 2).reshape(DEPTH, PHYS, P, 512),
        v_pages=a["cache_sb_v"].reshape(PHYS, DEPTH, P, 512).transpose(1, 0, 2, 3),
        layer_par=layer_par, layer_par4=layer_par4, head_par=head_par,
        hgrn=a["state_hgrn"].transpose(1, 2, 3, 0, 4).reshape(DEPTH, HEADS, P, NB * P),
        ml_c=a["state_mlstm_c"].transpose(1, 2, 3, 0, 4).reshape(DEPTH, HEADS, P, NB * P),
    )
    results = dict(
        y=(P, KC, T), k=(DEPTH, P, HEADS, T), v=(DEPTH, P, HEADS, T), hgrn_p=(DEPTH, HEADS, P, P),
        hgrn_s=(DEPTH, HEADS, P, NB * P), c_p=(DEPTH, HEADS, P, P), c_s=(DEPTH, HEADS, P, NB * P),
        n_p=(DEPTH, HEADS, P, 1), n_s=(DEPTH, P, HEADS, NB), m_p=(DEPTH, HEADS, 1), m_s=(DEPTH, HEADS, NB),
        conv_p=(DEPTH, HEADS, P, 3), conv_s=(DEPTH, HEADS, P, 3 * NB),
    )
    nc = bacc.Bacc("TRN2", target_bir_lowering=False, num_devices=1)
    arrays, ins, outs = {}, {}, {}
    for name, v in feeds.items():
        v = np.ascontiguousarray(v)
        arrays["in_" + name] = v
        ins[name] = nc.dram_tensor("in_" + name, v.shape, mybir.dt.from_np(v.dtype), kind="ExternalInput").ap()
    for name, shape in results.items():
        outs[name] = nc.dram_tensor("out_" + name, shape, F32, kind="ExternalOutput").ap()
    build(nc, namedtuple("Inputs", ins)(**ins), namedtuple("Outputs", outs)(**outs))
    got = run_bass_kernel_spmd(nc, [arrays], core_ids=[0]).results[0]
    o = {name: np.asarray(got["out_" + name]) for name in results}

    yt = o["y"].transpose(2, 1, 0).reshape(T, D)
    kk, vv = (o[n].transpose(0, 3, 2, 1).reshape(DEPTH, T, SBH, 64) for n in ("k", "v"))
    hs = o["hgrn_s"].reshape(DEPTH, HEADS, P, NB, P).transpose(3, 0, 1, 2, 4)
    cs = o["c_s"].reshape(DEPTH, HEADS, P, NB, P).transpose(3, 0, 1, 2, 4)
    conv_s = o["conv_s"].reshape(DEPTH, HEADS, P, 3, NB).transpose(4, 0, 3, 1, 2).reshape(NB, DEPTH, 3, 512)
    conv_p = o["conv_p"].transpose(0, 3, 1, 2).reshape(1, DEPTH, 3, 512)
    c = np.ascontiguousarray
    return (c(yt[None, 0:TP]), c(yt[TP:, None]), c(kk[None, :, 0:TP]), c(vv[None, :, 0:TP]),
            c(kk[:, TP:].transpose(1, 0, 2, 3)[:, :, None]), c(vv[:, TP:].transpose(1, 0, 2, 3)[:, :, None]),
            c(o["hgrn_p"][None]), c(hs), c(o["c_p"][None]), c(cs), c(o["n_p"][None, :, :, :, 0]),
            c(o["n_s"].transpose(3, 0, 2, 1)), c(o["m_p"].transpose(2, 0, 1)), c(o["m_s"].transpose(2, 0, 1)),
            conv_p, c(conv_s))
```

```python
from collections import namedtuple
from contextlib import ExitStack, contextmanager

import concourse.bass as bass
from concourse import mybir

F32 = mybir.dt.float32
I32 = mybir.dt.int32
F32R = mybir.dt.float32r
ALU = mybir.AluOpType
ACT = mybir.ActivationFunctionType
AX = mybir.AxisListType

P = 128
D = 1024
KC = D // P
TP = 256
NB = 8
T = TP + NB
DEPTH = 2
DFF = 2816
FC = DFF // P
HEADS = 4
SBH = 8
PAGES = 8
PHYS = 80
ADA_N = 9 * KC
ADA_GROUPS = 7
ADA_LOOP = 2 * 8
EPS = 1e-6
SB_SCALE = 64 ** -0.5
ML_SCALE = P ** -0.5
NEVER = -30000.0
SLOT = 24
SLOTS = 4
PIECE = KC
SQ_, SK_, SV_, MX_, HQ_, HF_, HI_, HG_ = range(KC)
WQ, WIF, CW, CBIAS, HGG, CST, SBB2, HPN = 0, 384, 408, 412, 413, 414, 438, 440
BADA, GPRE, GPOST, SBB, N0, MLG, LPN = 0, 72, 96, 120, 128, 160, 164
STORES_A, STORES_B = 6, 4
KL_DVE = 4
LEVELS = 8


class Count:

    def __init__(self):
        self.n, self.i, self.per = 0, None, 0

    @contextmanager
    def loop(self, i, times, per):
        before, self.i, self.per = self.n, i, per
        yield
        assert self.n - before == per, f"{self.n - before} in a round, not {per}"
        self.i, self.n = None, before + per * times

    def __call__(self, k=1):
        now = self.n if self.i is None or not self.per else self.i * self.per + self.n
        self.last = now
        self.n += k
        return now


class Slots:

    def __init__(self):
        self.pos = 0
        self.loads, self.parts = [Count() for _ in range(SLOTS)], [Count() for _ in range(SLOTS)]

    @contextmanager
    def loop(self, i, times, parts, at=None):
        with ExitStack() as stack:
            for r in range(SLOTS):
                mine = [p for j, p in enumerate(parts) if (self.pos + j) % SLOTS == r] if at is None \
                    else (parts if r == at else [])
                stack.enter_context(self.loads[r].loop(i, times, len(mine)))
                stack.enter_context(self.parts[r].loop(i, times, sum(mine)))
            yield

    def take(self, parts, at=None):
        r = self.pos if at is None else at
        if at is None:
            self.pos = (self.pos + 1) % SLOTS
        return r, self.loads[r](), self.parts[r](parts)

    def follow(self, other):
        self.pos = other.pos
        for mine, theirs in zip(self.loads + self.parts, other.loads + other.parts):
            mine.n = theirs.n


class Products:

    def __init__(self):
        self.count, self.pos = Count(), 0

    def take(self, banks=4):
        b = self.pos
        self.pos = (self.pos + 1) % banks
        return b, self.count()


class Chain:

    def __init__(self, eng, sem):
        self.eng, self.sem, self.n, self.i, self.per = eng, sem, 0, None, 0

    def __call__(self, ins):
        self.n += 1
        ins.then_inc(self.sem, 1)
        self.eng.wait_ge(self.sem, self.n if self.i is None else self.i * self.per + self.n)

    @contextmanager
    def loop(self, i, times, per):
        before = self.n
        self.i, self.per = i, per
        yield
        assert self.n - before == per, f"{self.n - before} links a round, not {per}"
        self.i, self.n = None, before + per * times


def build(nc, ins, outs):
    ctx = ExitStack()
    with ctx:
        def sb(name, shape, dt=F32):
            return ctx.enter_context(nc.sbuf_tensor(name, shape, dt))

        def twins(name, shape):
            with nc.sbuf_tensor(name + "_parts", shape, F32R) as parts:
                pass
            return sb(name, shape), parts

        def sems(names):
            return namedtuple("Semaphores", names)(*(ctx.enter_context(nc.semaphore(n)) for n in names.split()))

        x = sb("x", [P, KC, T])
        xn, xlo = twins("xn", [P, KC, T])
        ring, ring_lo = twins("ring", [P, SLOTS, SLOT * P])
        pages, page_parts = twins("pages", [P, PAGES, 4 * P])
        consts = sb("consts", [P, 6, P])
        ident, ones, tri = consts[:, 0, :], consts[:, 1, :], consts[:, 2, :]
        strict01, strictneg, causalpos = consts[:, 3, :], consts[:, 4, :], consts[:, 5, :]
        hmask = sb("hmask", [P, LEVELS, P], mybir.dt.uint8)
        onerow = ones[:, 0:1].broadcast_to([P, TP])
        eps = sb("eps", [P, 1])
        ctok = sb("ctok", [P, KC, NB + 1])
        sel = sb("sel", [P, SBH])
        rbuf = sb("rbuf", [P, 512])
        csil = sb("csil", [P, KC, NB + 1])
        lbl = sb("lbl", [P, DEPTH, HEADS])
        lbt = sb("lbt", [P, DEPTH * HEADS, 2])
        lbx = sb("lbx", [P, 4, HEADS])
        lbh = sb("lbh", [P, 2])
        ptab = sb("ptab", [1, NB * PAGES], I32)
        lp = sb("lp", [P, LPN])
        lp4 = sb("lp4", [4, 2 + NB])
        ada = sb("ada", [P, ADA_N, NB + 1])
        atab = sb("atab", [P, KC, NB + 1])
        gtab = sb("gtab", [P, KC, NB + 1])
        ctmp = gtab
        rs = sb("rs", [P, T])
        smpt = sb("smpt", [P, KC, NB])
        wbuf = sb("wbuf", [P, 6, T])
        w1, w2, w3, w4, w5, w6 = (wbuf[:, n, :] for n in range(6))
        sq, acc = wbuf[:, 4:6, :], w1
        fe = sb("fe", [P, 2, T])
        ft = sb("ft", [P, 2, T])
        big, big_parts = twins("big", [P, 28, T])
        qkv = big[:, 0:12, :].rearrange("p (j h) t -> p j h t", j=3)
        oa, ob, oc = big[:, 12:16, :], big[:, 16:20, :], big[:, 20:24, :]
        mo = big[:, 24:28, :]
        whi = page_parts[:].rearrange("p (j a) k -> p j (a k)", a=PIECE // 4)
        hid = big_parts[:, 0:FC, :]
        merged = big[:, 0:KC, :]
        gates, gate_parts = twins("gates", [P, 3 * KC, T])
        hid_lo = gate_parts[:, 0:FC, :]
        pj = sb("pj", [P, 9, T])
        y = pj[:, 0:KC, :]
        xp = sb("xp", [P, 3 + T])
        hp = sb("hp", [P, HPN])
        arena, arena_parts = twins("arena", [P, 2 * LEVELS * TP])
        e8 = arena[:, 0:LEVELS * TP].rearrange("p (v t) -> p v t", v=LEVELS)
        ql = arena[:, LEVELS * TP:2 * LEVELS * TP].rearrange("p (v t) -> p v t", v=LEVELS)
        xhi = arena_parts[:, 0:KC * T].rearrange("p (c t) -> p c t", c=KC)
        kl = e8

        def part(at, n, *shape):
            v = arena[:, at:at + n]
            return v.rearrange("p (a b) -> p a b", a=shape[0]) if shape else v

        zp, sbt, spt = part(0, 768, 2), part(768, 768, 2), part(1536, 768, 2)
        tt8 = part(0, NB * P, NB)
        dg8 = part(NB * P, NB * P, NB)
        st8 = sb("st8", [P, NB, P])
        sn8 = sb("sn8", [P, NB, P])
        vi = sb("vi", [P, 4, P])
        sct = sb("sct", [P, 3, P])
        kdt = sb("kdt", [P, 2, P])
        hsp = sb("hsp", [P, P])
        sgt = sb("sgt", [P, 2, T])
        xc = sb("xc", [P, T])
        nbs = sb("nbs", [P, 3, NB])
        s8a, s8b, s8c = sb("s8a", [P, NB]), sb("s8b", [P, NB]), sb("s8c", [P, NB])
        ot = sb("ot", [P, T])
        gi = sb("gi", [4, T])
        gf = sb("gf", [4, T])
        r4 = arena[0:4, 3072:3072 + 3 * T].rearrange("p (a t) -> p a t", a=3)
        rows = arena[0:4, 0:TP + 3 * NB + TP]
        nrow = TP + 3 * NB + TP
        bd = pj[0:4, :, :].rearrange("p c t -> p (c t)")[:, 0:4 * nrow].rearrange("p (h n) -> p h n", h=4)
        gcol = sb("gcol", [P, 2, 4])
        qm = sb("qm", [P, NB, HEADS, SBH])
        zt = part(2560, 512)
        zs = sb("zs", [P, 512])
        ast = sb("ast", [P, 2, PAGES * SBH])
        qst = ast[:, 0, :].rearrange("p (e c h) -> p e c h", e=2, c=HEADS)
        ks, vs, qs = fe[:, 0, :], fe[:, 1, :], sgt[:, 0, :]
        vk, dm, wt = part(2048, 512, 4), part(2560, 384), part(2944, 384)
        vw2 = xc[:, 0:TP].rearrange("p (t k) -> p t k", t=2)
        nst = sb("nst", [P, 1])
        sw = sb("sw", [P, 3 * NB])
        ps = ctx.enter_context(nc.psum_tensor("ps", [P, 8, 512], F32))
        M0, M1, M2, Z = 4, 5, 6, 7

        slot_full = [ctx.enter_context(nc.semaphore(f"slot_full{r}")) for r in range(SLOTS)]
        slot_done = [ctx.enter_context(nc.semaphore(f"slot_done{r}")) for r in range(SLOTS)]
        page_full = [ctx.enter_context(nc.semaphore(f"page_full{r}")) for r in range(PAGES // 2)]
        page_free = [ctx.enter_context(nc.semaphore(f"page_free{r}")) for r in range(PAGES // 2)]
        S = sems(
            "xs_ready xp_ready xsmp res xsum sig whi_done whi_ready wlo_ready xmod xhi_ready hhi_ready "
            "hlo_ready evac ada_evac ada_row ada_tr qstr zrow ztr astr vrow vrd lpar dchain achain pchain "
            "store hpar x2_ready ss_ready rs_ready xn_ready yss_ready yrs_ready e_ready sqc qmr tr zz spr "
            "suf t_ready ar av obr xcr qkv_ps qkv_sb gt gir kdr kdtp kdtr accd nnr nqr ibr ho hos osq hss "
            "lvl lvc klr qlr snr dve_it pool_it vir zpr l1r lnr accr xer tzr ur l2r khr dlr elr kder fsr sge "
            "rsh snp snm otr lnsr spsr sufs t2r asr rw1 rl1 rw2 rw3 bdr gcp gcr stg trb kqr exr dmr vwr ndr "
            "adr htr cst cev kbr cnr cnp qbr dns dna sqh hbs rsb mg x_fin "
        )

        with nc.Block() as block:
            @block.sync
            def _(sp):
                for dst, src in ((consts[:], ins.consts), (tt8, ins.masks), (x[:], ins.x),
                                 (ctok[:], ins.c), (sel[:], ins.sel), (lbl[:], ins.lb), (ptab[:], ins.page_table)):
                    sp.dma_start(dst, src).then_inc(S.lpar, 16)
                sp.wait_ge(S.lpar, 112)

            @block.gpsimd
            def _(pool):
                nc.gpsimd.memset(eps[:], EPS)
                nc.gpsimd.memset(qm[:], 0.0)
                nc.gpsimd.memset(xp[:], 0.0)

            @block.scalar
            def _(act):
                act.wait_ge(S.lpar, 112)
                nc.scalar.activation(ctmp[:], ctok[:], ACT.Exp, scale=-1.0).then_inc(S.achain, 1)
                act.wait_ge(S.dchain, 3)
                nc.scalar.activation(lbx[:, 1:3, :], lbx[:, 1:3, :], ACT.Exp).then_inc(S.achain, 1)
                act.wait_ge(S.x_fin, 1)
                nc.scalar.activation(lbx[:, 3, :], lbx[:, 3, :], ACT.Ln).then_inc(S.achain, 1)

            @block.vector
            def _(dve):
                link = Chain(dve, S.dchain)
                dve.wait_ge(S.lpar, 112)
                nc.vector.tensor_copy(hmask[:], tt8)
                for bank in (M0, Z):
                    nc.vector.memset(ps[:, bank, :], 0.0)
                link(nc.vector.tensor_tensor(lbx[:, 0, :], lbl[:, 0, :], lbl[:, 1, :], ALU.max))
                for j in range(2):
                    link(nc.vector.tensor_tensor(lbx[:, 1 + j, :], lbl[:, j, :], lbx[:, 0, :], ALU.subtract))
                link(nc.vector.memset(lbt[:, 0:HEADS, 0:1], -1e30))
                link(nc.vector.memset(lbt[:, 0:HEADS, 1:2], 0.0))
                dve.wait_ge(S.achain, 2)
                nc.vector.tensor_tensor(lbx[:, 3, :], lbx[:, 1, :], lbx[:, 2, :], ALU.add).then_inc(S.x_fin, 1)
                dve.wait_ge(S.x_fin, 1)
                dve.wait_ge(S.achain, 3)
                link(nc.vector.tensor_tensor(lbx[:, 0, :], lbx[:, 0, :], lbx[:, 3, :], ALU.add))
                for j in range(2):
                    link(nc.vector.tensor_tensor(lbt[:, HEADS:2 * HEADS, j], lbl[:, 1 - j, :],
                                                 lbx[:, 0, :], ALU.subtract))
                link(nc.vector.tensor_scalar_add(ctmp[:], ctmp[:], 1.0))
                link(nc.vector.reciprocal(ctmp[:], ctmp[:]))
                link(nc.vector.tensor_tensor(csil[:], ctmp[:], ctok[:], ALU.mult))

        numbers = sorted(s.num for s in list(S) + slot_full + slot_done + page_full + page_free)
        assert numbers == list(range(numbers[0], numbers[-1] + 1))

        def clear_all():
            nc.all_engine_barrier()
            nc.sync.sem_clear(range(numbers[0], numbers[-1] + 1))
            nc.all_engine_barrier()

        clear_all()

        def one_layer(block, layer):
            bds = bass.ds

            def residual_part(c):
                return (ft if c % 4 < 2 else fe)[:, c % 2, 0:TP]

            def apart(eng):
                eng.nop(nofuse=True)

            @block.sync
            def _(sp):
                slots, page_loads = Slots(), Count()
                nc.sync.dma_start(lp[:], ins.layer_par[layer]).then_inc(S.lpar, 16)
                nc.sync.dma_start(lp4[:], ins.layer_par4[layer]).then_inc(S.lpar, 16)

                def load(src, parts, at=None):
                    tiles = src.shape[-1] // P
                    r, _, before = slots.take(parts, at)
                    sp.wait_ge(slot_done[r], before + 1)
                    sp.dma_start(ring[:, r, 0:tiles * P], src).then_inc(slot_full[r], 16)

                def load_pages(pool_of_pages, b):
                    before = page_loads()
                    for j in range(PAGES):
                        page = sp.value_load(ptab[0:1, bds(b * PAGES + j, 1)], min_val=0, max_val=PHYS - 1)
                        sp.wait_ge(page_free[j // 2], before + 1)
                        sp.dma_start(pages[:, j, :], pool_of_pages[layer, page]).then_inc(page_full[j // 2], 16)

                with sp.Fori(0, 2) as i, slots.loop(i, 2, [1] * 4):
                    for k in range(4):
                        load(ins.w_ada8[layer, i * 4 + k], 1)
                with sp.Fori(0, 4) as i, slots.loop(i, 4, [2, 1] * 4):
                    for k in range(4):
                        load(ins.w_ffn_in[layer, 0, i * 4 + k], 2)
                        load(ins.w_ada12[layer, i * 4 + k], 1)
                for k in range(16, FC):
                    load(ins.w_ffn_in[layer, 0, k], 2)
                    if k < 20:
                        load(ins.w_ada8[layer, k - 8], 1)
                with sp.Fori(0, 2) as i, slots.loop(i, 2, [1] * 4):
                    for k in range(4):
                        load(ins.w_ffn_down[layer, 0, i * 4 + k], 1)
                for s in range(2):
                    load(ins.w_sq[layer, s], 2)
                with sp.Fori(0, HEADS) as i, slots.loop(i, HEADS, [3] * 4), page_loads.loop(i, HEADS, 2):
                    for k in range(3):
                        load(ins.w_a[layer, i * 4 + k], 3)
                    sp.wait_ge(S.yss_ready, 1)
                    load_pages(ins.k_pages, i * 2)
                    load(ins.w_a[layer, i * 4 + 3], 3)
                    load_pages(ins.k_pages, i * 2 + 1)
                at = slots.pos
                with sp.Fori(0, HEADS) as i, slots.loop(i, HEADS, [2], at), page_loads.loop(i, HEADS, 2):
                    load(ins.w_b[layer, i], 2, at)
                    load_pages(ins.v_pages, i * 2)
                    load_pages(ins.v_pages, i * 2 + 1)
                for s in range(4):
                    load(ins.w_proj[layer, s], 6)
                for s in range(4):
                    load(ins.w_out[layer, s], 2)
                with sp.Fori(0, 5) as i, slots.loop(i, 5, [2] * 4):
                    for k in range(4):
                        load(ins.w_ffn_in[layer, 1, i * 4 + k], 2)
                for s in (20, 21):
                    load(ins.w_ffn_in[layer, 1, s], 2)
                with sp.Fori(0, 2) as i, slots.loop(i, 2, [1] * 4):
                    for k in range(4):
                        load(ins.w_ffn_down[layer, 1, i * 4 + k], 1)

            @block.tensor
            def _(pe):
                slots, products, adas, page_uses = Slots(), Products(), Count(), Count()
                pieces = Products()
                pe.sem_inc(S.whi_done, 4)
                for s in slot_done + page_free:
                    pe.sem_inc(s, 1)
                mm = nc.tensor.matmul

                def open_slot(parts, at=None):
                    r, loads, _ = slots.take(parts, at)
                    pe.wait_ge(slot_full[r], loads * 16 + 16)
                    return r

                def tile_of(r, k):
                    return ring[:, r, k * P:(k + 1) * P]

                def product(r, first, rhs, depth, banks=4):
                    b, n = products.take(banks)
                    pe.wait_ge(S.evac, n + (1 + 4 - banks))
                    for k in range(depth):
                        last = mm(ps[:, b, 0:T], tile_of(r, first + k), rhs(k), start=(k == 0), stop=(k == depth - 1))
                    last.then_inc(slot_done[r], 1)

                def ada_slot(q, group):
                    cols = group // 4 * P
                    r = open_slot(1)
                    if q == 0:
                        pe.wait_ge(S.ada_row, adas() + 1)
                    for u in range(2):
                        k = 2 * q + u
                        for j in range(4):
                            last = mm(ps[32 * j:32 * j + NB + 1, M0, 0:cols], csil[:, k, :],
                                      ring[:, r, (u * 4 + j) * cols:(u * 4 + j + 1) * cols],
                                      start=(k == 0), stop=(k == KC - 1))
                    last.then_inc(slot_done[r], 1)

                def ada_columns(n, group):
                    pe.wait_ge(S.ada_row, n + 2)
                    pe.wait_ge(S.ada_evac, n + 1)
                    for k in range(group // 4):
                        last = nc.tensor.transpose(ps[:, M1, k * P:(k + 1) * P], rbuf[:, k * P:(k + 1) * P], ident)
                    last.then_inc(S.ada_tr, 1)

                def xn_of(k):
                    return xn[:, k, :]

                def upper(b, place, k, hi, lo, start):
                    tile = whi[:, place, k % PIECE * P:(k % PIECE + 1) * P]
                    mm(ps[:, b, 0:T], tile, hi[:, k, :], start=start, stop=False)
                    return mm(ps[:, b, 0:T], tile, lo[:, k, :], start=False, stop=False)

                def lower(b, r, tile, k, hi, stop):
                    return mm(ps[:, b, 0:T], ring_lo[:, r, tile * P:(tile + 1) * P], hi[:, k, :], start=False, stop=stop)

                def split_product(r, first, hi, lo, depth):
                    b, n = products.take()
                    pe.wait_ge(S.evac, n + 1)
                    for at in range(0, depth, PIECE):
                        place, m = pieces.take()
                        ks = range(at, min(at + PIECE, depth))
                        pe.wait_ge(S.wlo_ready, m + 1)
                        for k in ks:
                            last = upper(b, place, k, hi, lo, k == 0)
                        last.then_inc(S.whi_done, 1)
                        for k in ks:
                            last = lower(b, r, first + k, k, hi, k == depth - 1)
                    last.then_inc(slot_done[r], 1)

                def ffn_products(r):
                    split_product(r, 0, xhi, xlo, KC)
                    split_product(r, KC, xhi, xlo, KC)

                def ffn_slot():
                    ffn_products(open_slot(2))

                def first_ffn_slot(before):
                    r = open_slot(2)
                    places = []
                    for _ in range(2):
                        b, n = products.take()
                        place, m = pieces.take()
                        places.append((b, place))
                    pe.wait_ge(S.evac, n + 1)
                    pe.wait_ge(S.wlo_ready, m + 1)
                    for k in range(KC):
                        pe.wait_ge(S.xn_ready, before + k + 1)
                        for j, (b, place) in enumerate(places):
                            if k:
                                lower(b, r, j * KC + k, k, xhi, False)
                            last = upper(b, place, k, xhi, xlo, k == 0)
                            if k == KC - 1:
                                last.then_inc(S.whi_done, 1)
                    for j, (b, place) in enumerate(places):
                        lower(b, r, j * KC, 0, xhi, True).then_inc(slot_done[r], 1)

                def pre_sums(n):
                    for k in range(KC):
                        pe.wait_ge(S.x2_ready, (n - 1) * KC + k + 1)
                        last = mm(ps[:, Z, 0:T], ones, xn[:, k, :], start=(k == 0), stop=(k == KC - 1))
                    last.then_inc(S.ss_ready, 1)

                def post_sum(n):
                    pe.wait_ge(S.accd, n * KC + 2)
                    mm(ps[:, Z, 0:T], ones, acc, start=True, stop=True).then_inc(S.yss_ready, 1)

                def down(n):
                    pe.wait_ge(S.hlo_ready, n * FC)
                    with pe.Fori(0, 2) as i, slots.loop(i, 2, [1] * 4), products.count.loop(i, 2, 4), \
                            pieces.count.loop(i, 2, 12):
                        for k in range(4):
                            split_product(open_slot(1), 0, hid, hid_lo, FC)

                pre_sums(1)
                with pe.Fori(0, 2) as i, slots.loop(i, 2, [1] * 4), adas.loop(i, 2, 1):
                    for k in range(4):
                        ada_slot(k, 8)
                    ada_columns(i, 8)
                with pe.Fori(0, 4) as i, slots.loop(i, 4, [2, 1] * 4), products.count.loop(i, 4, 8), \
                        pieces.count.loop(i, 4, 8), adas.loop(i, 4, 1):
                    first_ffn_slot(0)
                    ada_slot(0, 12)
                    for k in (1, 2):
                        ffn_slot()
                        ada_slot(k, 12)
                    r = open_slot(2)
                    ada_slot(3, 12)
                    ffn_products(r)
                    ada_columns(i + 2, 12)
                for k in range(16, FC):
                    ffn_slot()
                    if k < 20:
                        ada_slot(k - 16, 8)
                    if k == 20:
                        ada_columns(6, 8)
                down(1)
                post_sum(1)
                pre_sums(2)

                def xn_as_it_comes(k):
                    pe.wait_ge(S.xmod, KC + k + 1)
                    return xn[:, k, :]

                for s in range(2):
                    r = open_slot(2)
                    product(r, 0, xn_of if s else xn_as_it_comes, KC)
                    product(r, KC, xn_of, KC)

                def key_pages(e):
                    loads = page_uses()
                    for j in range(4):
                        pe.wait_ge(page_full[j], loads * 32 + 32)
                    for c in range(HEADS):
                        for j in range(4):
                            last = mm(ps[32 * j:32 * j + SBH, Z, e * 256:(e + 1) * 256], qst[:, e, c, :],
                                      pages[:, 2 * j:2 * j + 2, c * P:(c + 1) * P],
                                      start=(c == 0), stop=(c == HEADS - 1))
                            if c == HEADS - 1:
                                last.then_inc(page_free[j], 1)

                def value_pages(e, n):
                    loads = page_uses()
                    for j in range(4):
                        pe.wait_ge(page_full[j], loads * 32 + 32)
                    pe.wait_ge(S.vrow, n + 1)
                    for u in range(2):
                        for j in range(4):
                            last = mm(ps[32 * j:32 * j + SBH, 3, :], ast[:, e, (2 * j + u) * SBH:(2 * j + u + 1) * SBH],
                                      pages[:, 2 * j + u, :], start=(u == 0), stop=(u == 1))
                            if u == 1:
                                last.then_inc(page_free[j], 1)

                def value_columns(b, n):
                    pe.wait_ge(S.vrow, n + 2)
                    for c in range(HEADS):
                        last = mm(ps[:, 2, bds(b * 8 + 2 * c, 2)], rbuf[:, c * P:(c + 1) * P],
                                  sel[:, 2 * c:2 * c + 2], start=True, stop=True)
                    last.then_inc(S.vrd, 1)

                before_a = products.count.n
                with pe.Fori(0, HEADS) as i:
                    with slots.loop(i, HEADS, [3] * 4), products.count.loop(i, HEADS, 12), page_uses.loop(i, HEADS, 2):
                        for k in range(2):
                            r = open_slot(3)
                            for n in range(3):
                                product(r, n * KC, xn_of, KC)
                        pe.wait_ge(S.dve_it, i + 1)
                        pe.wait_ge(S.rsh, i + 1)
                        pe.wait_ge(S.sqc, i + 1)
                        pe.wait_ge(S.evac, i * 12 + (before_a + 6 + 4))
                        for n, (c, t) in enumerate(((SV_, 0), (SV_, 1), (HI_, 0), (HI_, 1))):
                            last = nc.tensor.transpose(ps[:, M0, n * P:(n + 1) * P], pj[:, c, t * P:(t + 1) * P], ident)
                        last.then_inc(S.tr, 1)
                        for h in range(2):
                            a, e = 64 * h, 64 * h + 64
                            mm(ps[:, M1 + h, 0:TP], pj[a:e, SK_, 0:P], pj[a:e, SQ_, 0:TP], start=True, stop=True)
                            last = mm(ps[:, M1 + h, TP:TP + P], pj[a:e, SK_, P:TP], pj[a:e, SQ_, P:TP],
                                      start=True, stop=True)
                        last.then_inc(S.zz, 1)
                        oslot = open_slot(3)
                        product(oslot, 0, xn_of, KC)
                        product(oslot, KC, xn_of, KC)
                        pe.wait_ge(S.spr, i + 1)
                        for h in range(2):
                            mm(ps[:, M1 + h, 0:TP], tri, spt[:, h, 0:TP], start=True, stop=False)
                            mm(ps[:, M1 + h, P:TP], ones, spt[:, h, TP:TP + P], start=False, stop=True)
                            last = mm(ps[:, M1 + h, TP:TP + P], tri, spt[:, h, TP:TP + P], start=True, stop=True)
                        last.then_inc(S.suf, 1)
                        product(oslot, 2 * KC, xn_of, KC)
                        pe.wait_ge(S.vir, i + 1)
                        pe.wait_ge(S.ar, i + 1)
                        for h in range(2):
                            a, e = 64 * h, 64 * h + 64
                            mm(ps[a:e, M0, 0:TP], vi[:, 0, a:e], sbt[:, h, 0:TP], start=True, stop=False)
                            last = mm(ps[a:e, M0, P:TP], vi[:, 1, a:e], sbt[:, h, TP:TP + P], start=False, stop=True)
                        last.then_inc(S.av, 1)
                        pe.wait_ge(S.xcr, i + 1)
                        pe.wait_ge(S.hpar, i * 32 + 32)
                        mm(ps[:, M1, 0:T], hp[:, WQ:WQ + P], xc[:], start=True, stop=True)
                        mm(ps[:, M2, 0:T], hp[:, WQ + P:WQ + 2 * P], xc[:], start=True, stop=True)
                        pe.wait_ge(S.obr, i + 1)
                        mm(ps[:, M0, 0:T], hp[:, WQ + 2 * P:WQ + 3 * P], xp[:, 3:3 + T], start=True, stop=True)\
                            .then_inc(S.qkv_ps, 1)
                        gslot = open_slot(3)
                        product(gslot, 0, xn_of, KC)
                        pe.wait_ge(S.qkv_sb, i + 1)
                        for g in range(2):
                            for j in range(3):
                                last = mm(ps[0:4, M1 + g, 0:T], hp[:, WIF + j * 8 + 4 * g:WIF + j * 8 + 4 * g + 4],
                                          qkv[:, j, i, :], start=(j == 0), stop=(j == 2))
                        last.then_inc(S.gt, 1)
                        pe.wait_ge(S.qstr, i + 1)
                        key_pages(0)
                        product(gslot, KC, xn_of, KC)
                        pe.wait_ge(S.qlr, i + 1)
                        pe.wait_ge(S.klr, i * 2 + 2)
                        pe.wait_ge(S.gir, i + 1)

                        def level(b, at, v):
                            for t in range(2):
                                lhs = w4[:, t * P:(t + 1) * P] if v < 0 else kl[:, v, t * P:(t + 1) * P]
                                rhs = pj[:, HQ_, t * P:(t + 1) * P] if v < 0 else ql[:, v, t * P:(t + 1) * P]
                                last = mm(ps[:, b, at + t * P:at + (t + 1) * P], lhs, rhs, start=True, stop=True)
                            return last

                        level(M1, 0, -1)
                        level(M1, TP, 0).then_inc(S.lvl, 1)
                        level(M2, 0, 1)
                        level(M2, TP, 2).then_inc(S.lvl, 1)
                        mm(ps[:, M0, 0:P], kl[:, 7, 0:P], ql[:, 7, P:TP], start=True, stop=True).then_inc(S.lvl, 1)
                        pe.wait_ge(S.lvc, i * 5 + 1)
                        level(M1, 0, 3)
                        level(M1, TP, 4).then_inc(S.lvl, 1)
                        pe.wait_ge(S.lvc, i * 5 + 2)
                        level(M2, 0, 5)
                        level(M2, TP, 6).then_inc(S.lvl, 1)
                        pe.wait_ge(S.lvc, i * 5 + 3)
                        pe.wait_ge(S.kdr, i + 1)
                        for t in range(2):
                            last = nc.tensor.transpose(ps[:, M0, t * P:(t + 1) * P], w6[:, t * P:(t + 1) * P], ident)
                        last.then_inc(S.kdtp, 1)
                        key_pages(1)
                        pe.wait_ge(S.lvc, i * 5 + 5)
                        pe.wait_ge(S.kdtr, i + 1)
                        pe.wait_ge(S.snp, i + 1)
                        for n in range(2):
                            last = mm(ps[:, M1 + n, 0:512], ones, dg8[:, 4 * n:4 * n + 4, :], start=True, stop=True)
                        last.then_inc(S.ibr, 1)
                        mm(ps[:, M0, 0:TP], vi[:, 2, :], sct[:, 0:2, :], start=True, stop=False)
                        mm(ps[:, M0, P:TP], vi[:, 3, :], sct[:, 2, :], start=False, stop=True)
                        mm(ps[:, M0, 384:512], kdt[:, 0, :], vi[:, 2, :], start=True, stop=False)
                        mm(ps[:, M0, 384:512], kdt[:, 1, :], vi[:, 3, :], start=False, stop=True).then_inc(S.ho, 1)
                        product(gslot, 2 * KC, xn_of, KC)
                        pe.wait_ge(S.snr, i + 1)
                        for b in range(NB):
                            last = mm(ps[:, M1, b:b + 1], sn8[:, b, :], pj[:, HQ_, TP + b:TP + b + 1],
                                      start=True, stop=True)
                        last.then_inc(S.hos, 1)
                        pe.wait_ge(S.osq, i + 1)
                        mm(ps[:, M2, 0:T], ones, w2, start=True, stop=True).then_inc(S.hss, 1)
                        pe.wait_ge(S.zrow, i + 1)
                        for n in range(4):
                            last = nc.tensor.transpose(ps[:, Z, n * P:(n + 1) * P], rbuf[:, n * P:(n + 1) * P], ident)
                        last.then_inc(S.ztr, 1)

                pe.wait_ge(S.spsr, 1)
                mm(ps[:, Z, 0:512], tri, zt, start=True, stop=False)
                out4 = ps[:, Z, :].rearrange("p (b j h) -> p b j h", b=NB, j=PAGES)
                in4 = zt.rearrange("p (b j h) -> p b j h", b=NB, j=PAGES)
                for j in range(1, PAGES):
                    last = mm(out4[:, :, 0:PAGES - j, :], ones, in4[:, :, j:PAGES, :], start=False, stop=(j == PAGES - 1))
                last.then_inc(S.sufs, 1)
                pe.wait_ge(S.rw1, 1)
                pe.wait_ge(S.dve_it, HEADS + 1)
                pe.wait_ge(S.rsh, HEADS + 1)
                for t in range(2):
                    last = nc.tensor.transpose(ps[:, M0, t * 4:t * 4 + 4], r4[:, 0, t * P:(t + 1) * P], ident[0:4, 0:4])
                last.then_inc(S.gcp, 1)
                gate_slot, products.pos = slots.pos, 0

                with pe.Fori(0, HEADS) as i:
                    with slots.loop(i, HEADS, [2], gate_slot), products.count.loop(i, HEADS, 2), \
                            page_uses.loop(i, HEADS, 2):
                        r = open_slot(2, gate_slot)
                        product(r, 0, xn_of, KC, banks=2)
                        pe.wait_ge(S.gcr, 1)
                        pe.wait_ge(S.stg, i * 3 + 3)
                        pe.wait_ge(S.dve_it, i + HEADS + 1)
                        for n, src in enumerate((vs, vs, ks, ks)):
                            t = n % 2
                            last = nc.tensor.transpose(ps[:, M0, n * P:(n + 1) * P], src[:, t * P:(t + 1) * P], ident)
                        last.then_inc(S.trb, 1)
                        mm(ps[:, M1, 0:TP], ks[:, 0:P], qs[:, 0:TP], start=True, stop=True)
                        mm(ps[:, M1, TP:TP + P], ks[:, P:TP], qs[:, P:TP], start=True, stop=True)
                        pe.wait_ge(S.bdr, 1)
                        mm(ps[:, M2, 0:TP + 24], ones[0:4, :], bd[:, i, 0:TP + 24], start=True, stop=True)
                        mm(ps[:, Z, 0:TP], ones[0:4, :], bd[:, i, TP + 24:], start=True, stop=True).then_inc(S.kqr, 1)
                        pe.wait_ge(S.astr, i + 1)
                        value_pages(0, i * 2)
                        pe.wait_ge(S.vwr, i + 1)
                        for b, lhs in ((M0, None), (M1, ones)):
                            mm(ps[:, b, 0:TP], lhs if lhs is not None else vk[:, 0, :], wt[:, 0:TP], start=True, stop=False)
                            last = mm(ps[:, b, P:TP], lhs if lhs is not None else vk[:, 1, :], wt[:, TP:TP + P],
                                      start=False, stop=True)
                        last.then_inc(S.ndr, 1)
                        for t in range(2):
                            mm(ps[:, M2, 0:P], vw2[:, t, :], vk[:, 2 + t, :], start=(t == 0), stop=(t == 1))
                        for t in range(2):
                            col = (TP - 1, TP + P - 1)[t]
                            last = mm(ps[:, M2, P:P + 1], vk[:, 2 + t, :], dm[:, col:col + 1],
                                      start=(t == 0), stop=(t == 1))
                        last.then_inc(S.cst, 1)
                        product(r, KC, xn_of, KC, banks=2)
                        value_columns(i * 2, i * 2)
                        pe.wait_ge(S.htr, i + 1)
                        pe.wait_ge(S.cev, i + 1)
                        pe.wait_ge(S.snp, HEADS + 2 * i + 1)
                        for n in range(2):
                            last = mm(ps[:, M1 + n, 0:512], ones, dg8[:, 4 * n:4 * n + 4, :], start=True, stop=True)
                        last.then_inc(S.kbr, 1)
                        pe.wait_ge(S.nqr, i + 1)
                        mm(ps[:, M0, 0:NB], ones, s8b[:], start=True, stop=True).then_inc(S.dns, 1)
                        value_pages(1, i * 2 + 1)
                        pe.wait_ge(S.cnr, i + 1)
                        pe.wait_ge(S.snp, HEADS + 2 * i + 2)
                        for n in range(2):
                            last = mm(ps[:, M1 + n, 0:512], ones, dg8[:, 4 * n:4 * n + 4, :], start=True, stop=True)
                        last.then_inc(S.qbr, 1)
                        pe.wait_ge(S.sqh, i + 1)
                        mm(ps[:, M0, 0:T], ones, w2, start=True, stop=True).then_inc(S.hbs, 1)
                        value_columns(i * 2 + 1, i * 2 + 1)

                products.pos = 0
                pe.wait_ge(S.dve_it, 2 * HEADS + 2)
                for s in range(4):
                    r = open_slot(6)
                    for n in range(2):
                        for br, o in enumerate((oa, ob, oc)):
                            product(r, (n * 3 + br) * 4, (lambda o: lambda k: o[:, k, :])(o), HEADS)
                pe.wait_ge(S.mg, KC)
                for s in range(4):
                    r = open_slot(2)
                    for n in range(2):
                        product(r, n * KC, lambda k: merged[:, k, :], KC)
                post_sum(2)
                pre_sums(3)
                with pe.Fori(0, 5) as i, slots.loop(i, 5, [2] * 4), products.count.loop(i, 5, 8), \
                        pieces.count.loop(i, 5, 8):
                    first_ffn_slot(KC)
                    for k in (1, 2, 3):
                        ffn_slot()
                for k in range(2):
                    ffn_slot()
                down(2)
                post_sum(3)

            @block.vector
            def _(dve):
                slots, products, exps, sums = Slots(), Products(), Count(), Count()
                pieces, hids = Products(), Count()
                v = nc.vector
                link = Chain(dve, S.dchain)
                dve.sem_inc(S.evac, 4)
                dve.sem_inc(S.ada_evac, 1)
                dve.sem_inc(S.ada_row, 1)
                dve.sem_inc(S.accd, 2)
                dve.sem_inc(S.dve_it, 1)
                dve.wait_ge(S.lpar, 32)

                def ada_rows(group):
                    for q in range(4):
                        r, _, before = slots.take(1)
                        yield
                    dve.wait_ge(slot_done[r], before + 2)
                    cols = group // 4 * P
                    v.tensor_copy(rbuf[:, 0:cols], ps[:, M0, 0:cols]).then_inc(S.ada_row, 1)
                    yield

                def ada_columns(n, group, first):
                    dve.wait_ge(S.ada_tr, n + 1)
                    q = group // 4
                    v.tensor_tensor(
                        ada[:, bds(first, group), :].rearrange("p (j q) t -> p j q t", j=4),
                        ps[:, M1, 0:q * P].rearrange("p (q j t) -> p j q t", q=q, j=4)[:, :, :, 0:NB + 1],
                        lp[:, bds(first + BADA, group)].rearrange("p (j q) -> p j q", j=4).unsqueeze(3)
                        .broadcast_to([P, 4, q, NB + 1]), ALU.add).then_inc(S.ada_evac, 1)

                ahead = Slots()

                def split(tiles):
                    r, _, _ = ahead.take(2 if tiles == 2 * KC else 1)
                    for at in range(0, tiles, PIECE):
                        place, m = pieces.take()
                        n = min(PIECE, tiles - at)
                        w = ring[:, r, at * P:(at + n) * P]
                        dve.wait_ge(S.whi_ready, m + 1)
                        v.tensor_tensor(ring_lo[:, r, at * P:(at + n) * P], w, whi[:, place, 0:n * P].bitcast(F32), ALU.subtract)\
                            .then_inc(S.wlo_ready, 1)

                def ffn_slot(k, chunk, slot):
                    r, _, before = slot
                    bg, _ = products.take()
                    bu, _ = products.take()
                    dve.wait_ge(S.e_ready, exps() + 1)
                    t = ft[:, k % 2, :]
                    link(v.tensor_tensor(t, ps[:, bg, 0:T], fe[:, k % 2, :], ALU.mult))
                    dve.wait_ge(slot_done[r], before + 3)
                    v.tensor_tensor(t, ps[:, bu, 0:T], t, ALU.mult).then_inc(S.evac, 2)
                    dve.wait_ge(S.hhi_ready, hids() + 1)
                    v.tensor_tensor(hid_lo[:, chunk, :], t, hid[:, chunk, :].bitcast(F32), ALU.subtract)\
                        .then_inc(S.hlo_ready, 1)

                def sum_squares():
                    n = sums()
                    products.take()
                    dve.wait_ge(S.evac, products.count.last + (1 + 4))
                    dve.wait_ge(S.accd, n + 2)
                    v.tensor_tensor(acc, acc, sq[:, sums.n % 2, :], ALU.add).then_inc(S.accd, 1)

                def clear_sum():
                    link(v.memset(acc, 0.0))

                def scale_table(sub):
                    at = sub * 3 * KC
                    gp = lp[:, GPRE + sub * KC:GPRE + (sub + 1) * KC].unsqueeze(2).broadcast_to([P, KC, NB + 1])
                    link(v.scalar_tensor_tensor(atab[:], ada[:, at + KC:at + 2 * KC, :], 1.0, gp, ALU.add, ALU.mult))

                def gate_table(sub):
                    at = sub * 3 * KC
                    gq = lp[:, GPOST + sub * KC:GPOST + (sub + 1) * KC].unsqueeze(2).broadcast_to([P, KC, NB + 1])
                    link(v.scalar_tensor_tensor(gtab[:], ada[:, at + 2 * KC:at + 3 * KC, :], 1.0, gq, ALU.add, ALU.mult))
                    if sub != 1:
                        link(v.tensor_scalar_mul(gtab[:], gtab[:], 0.5))

                def scale_samples(n):
                    dve.wait_ge(S.rs_ready, n)
                    v.tensor_tensor(xn[:, :, TP:T], x[:, :, TP:T], rs[:, TP:T].unsqueeze(1).broadcast_to([P, KC, NB]),
                                    ALU.mult).then_inc(S.xs_ready, 1)

                def scale_prompt():
                    for c in range(KC):
                        v.tensor_tensor(xn[:, c, 0:TP], x[:, c, 0:TP], rs[:, 0:TP], ALU.mult).then_inc(S.xp_ready, 1)

                def modulate_samples(n):
                    shift = (n - 1) * 3 * KC
                    smp = xn[:, :, TP:T]
                    dve.wait_ge(S.xs_ready, n)
                    link(v.tensor_tensor(smp, smp, atab[:, :, 1:NB + 1], ALU.mult))
                    v.tensor_tensor(smp, smp, ada[:, shift:shift + KC, 1:NB + 1], ALU.add).then_inc(S.xsmp, 1)

                def split_input(n):
                    for c in range(KC + 1):
                        if c < KC:
                            dve.wait_ge(S.xmod, (n - 1) * KC + c + 1)
                            v.tensor_copy(xhi[:, c, :], xn[:, c, :]).then_inc(S.xhi_ready, 1)
                        if c:
                            dve.wait_ge(S.xhi_ready, n // 2 * KC + c)
                            v.tensor_tensor(xlo[:, c - 1, :], xn[:, c - 1, :], xhi[:, c - 1, :].bitcast(F32),
                                            ALU.subtract).then_inc(S.xn_ready, 1)

                def residual(n):
                    dve.wait_ge(S.yrs_ready, n)
                    rss = rs[:, TP:T].unsqueeze(1).broadcast_to([P, KC, NB])
                    link(v.tensor_tensor(smpt[:], y[:, :, TP:T], gtab[:, :, 1:NB + 1], ALU.mult))
                    link(v.tensor_tensor(smpt[:], smpt[:], rss, ALU.mult))
                    v.tensor_tensor(x[:, :, TP:T], x[:, :, TP:T], smpt[:], ALU.add).then_inc(S.xsum, 1)
                    for c in range(KC):
                        if c >= 4:
                            dve.wait_ge(S.x_fin, (n - 1) * KC + c - 3)
                        v.scalar_tensor_tensor(residual_part(c), y[:, c, 0:TP], gtab[:, c, 0:1], rs[:, 0:TP],
                                               ALU.mult, ALU.mult).then_inc(S.res, 1)
                    dve.wait_ge(S.x_fin, n * KC)

                def down():
                    clear_sum()
                    for c in range(KC):
                        if c < KC - 1:
                            split(FC)
                        slots.take(1)
                        sum_squares()

                scale_samples(1)
                scale_prompt()
                with dve.Fori(0, 2) as i, slots.loop(i, 2, [1] * 4):
                    for _ in ada_rows(8):
                        pass
                    ada_columns(i, 8, i * 8)
                dve.wait_ge(S.ada_evac, 3)
                scale_table(0)
                ahead.follow(slots)
                modulate_samples(1)
                split_input(1)
                split(2 * KC)
                with dve.Fori(0, 4) as i, slots.loop(i, 4, [2, 1] * 4), ahead.loop(i, 4, [1, 2] * 4), \
                        products.count.loop(i, 4, 8), pieces.count.loop(i, 4, 8), hids.loop(i, 4, 4), \
                        exps.loop(i, 4, 4), link.loop(i, 4, 4):
                    rows_of = ada_rows(12)
                    for k in range(4):
                        ahead.take(1)
                        split(2 * KC)
                        slot = slots.take(2)
                        next(rows_of)
                        if k == 3:
                            next(rows_of)
                        ffn_slot(k, i * 4 + k, slot)
                    ada_columns(i + 2, 12, i * 12 + ADA_LOOP)
                rows_of = ada_rows(8)
                for k in range(16, FC):
                    if k < 20:
                        ahead.take(1)
                    split(2 * KC if k < FC - 1 else FC)
                    if k == 20:
                        next(rows_of)
                    ffn_slot(k, k, slots.take(2))
                    if k < 20:
                        next(rows_of)
                    if k == 20:
                        ada_columns(6, 8, ADA_N - 8)
                down()
                dve.wait_ge(S.ada_evac, ADA_GROUPS + 1)
                gate_table(0)
                residual(1)
                scale_table(1)
                gate_table(1)
                scale_samples(2)
                modulate_samples(2)
                scale_prompt()

                for s in range(2):
                    slots.take(2)
                    products.take()
                    products.take()
                dve.wait_ge(S.evac, products.count.n + 4)
                for h in range(2):
                    a, e = 64 * h, 64 * h + 64
                    for c in range(HEADS):
                        last = v.tensor_copy(qm[a:e, :, c, 2 * c + h], ob[a:e, c, TP:T])
                last.then_inc(S.qmr, 1)
                link(v.memset(gi[:], 0.0))
                link(v.memset(gf[:], 0.0))

                before_a = products.count.n
                with dve.Fori(0, HEADS) as i, slots.loop(i, HEADS, [3] * 4), products.count.loop(i, HEADS, 12), \
                        link.loop(i, HEADS, 25):
                    for k in range(4):
                        slots.take(3)
                        for n in range(3):
                            products.take()
                    link(v.tensor_copy(lbh[:], lbt[:, bds(layer * HEADS + i, 1), :].rearrange("p a b -> p (a b)")))
                    link(v.memset(sct[:], 0.0))
                    dve.wait_ge(S.tr, i + 1)
                    v.tensor_copy(vi[:], ps[:, M0, :].rearrange("p (n t) -> p n t", n=4)).then_inc(S.vir, 1)
                    dve.wait_ge(S.hpar, i * 32 + 32)
                    dve.wait_ge(S.zz, i + 1)
                    for h in range(2):
                        last = v.tensor_scalar(zp[:, h, :], ps[:, M1 + h, 0:384], SB_SCALE, hp[:, SBB2 + h:SBB2 + h + 1],
                                               ALU.mult, ALU.add)
                    last.then_inc(S.zpr, 1)
                    dve.wait_ge(S.l1r, i + 1)
                    link(v.scalar_tensor_tensor(w2, pj[:, HF_, :], 0.0, w1, ALU.min, ALU.subtract))
                    link(v.tensor_scalar(w2, w2, lbh[:, 1:2], None, ALU.add))
                    v.tensor_scalar(w3, w2, lbh[:, 0:1], None, ALU.subtract).then_inc(S.ur, 1)
                    v.tensor_tensor(w4, w2, pj[:, HF_, :], ALU.subtract).then_inc(S.tzr, 1)
                    def cw(j):
                        return hp[:, CW + j:CW + j + 1]
                    xcp, xcs = xc[:, 0:TP], xc[:, TP:T]
                    link(v.tensor_scalar(xcp, xp[:, 0:TP], cw(0), hp[:, CBIAS:CBIAS + 1], ALU.mult, ALU.add))
                    link(v.tensor_scalar(xcs, xp[:, 3 + TP:3 + T], cw(3), hp[:, CBIAS:CBIAS + 1], ALU.mult, ALU.add))
                    for j in range(1, 4):
                        link(v.scalar_tensor_tensor(xcp, xp[:, j:j + TP], cw(j), xcp, ALU.mult, ALU.add))
                    for j in range(3):
                        ins_ = v.scalar_tensor_tensor(xcs, hp[:, CST + 8 * j:CST + 8 * j + 8], cw(j), xcs, ALU.mult, ALU.add)
                        link(ins_) if j < 2 else ins_.then_inc(S.accr, 1)
                    dve.wait_ge(S.lnr, i + 1)
                    link(v.scalar_tensor_tensor(spt, zp, 0.0, sbt, ALU.max, ALU.add))
                    for h in range(2):
                        d = diag_blocks(spt, h)
                        last = v.tensor_tensor(d, d, over2(strict01), ALU.mult)
                    last.then_inc(S.spr, 1)
                    dve.wait_ge(S.suf, i + 1)
                    link(v.tensor_tensor(zp, zp, ps[:, M1:M1 + 2, 0:384], ALU.subtract))
                    for h in range(2):
                        d = diag_blocks(zp, h)
                        last = v.scalar_tensor_tensor(d, d, 0.0, over2(strictneg), ALU.min, ALU.add)
                    last.then_inc(S.t_ready, 1)
                    dve.wait_ge(S.xer, i + 1)
                    v.tensor_tensor(xc[:], xc[:], fe[:, 0, :], ALU.mult).then_inc(S.xcr, 1)
                    dve.wait_ge(S.l2r, i + 1)
                    link(v.scalar_tensor_tensor(w5, w2, lbh[:, 0:1], w3, ALU.max, ALU.add))
                    link(v.tensor_tensor_scan(w1[:, 0:TP], onerow, w5[:, 0:TP], 0.0, ALU.mult, ALU.add))
                    dve.wait_ge(S.sge, i + 1)
                    link(v.tensor_copy(mo[:, i, :], sgt[:, 1, :]))
                    link(v.tensor_tensor(sgt[:, 0, :], sgt[:, 0, :], pj[:, HG_, :], ALU.mult))
                    dve.wait_ge(S.av, i + 1)
                    v.tensor_copy(ob[:, i, 0:TP], ps[:, M0, 0:TP]).then_inc(S.obr, 1)
                    for lv in range(LEVELS):
                        half = 1 << lv
                        src = w1[:, 0:TP].rearrange("p (n w) -> p n w", w=2 * half)
                        v.tensor_tensor(e8[:, lv, :].rearrange("p (n w) -> p n w", w=2 * half), src,
                                        src[:, :, half - 1:half].broadcast_to([P, TP // (2 * half), 2 * half]), ALU.subtract)
                    v.tensor_scalar(w6[:, 0:TP], w1[:, 0:TP], w1[:, TP - 1:TP], None, ALU.subtract).then_inc(S.dlr, 1)
                    dve.wait_ge(S.gt, i + 1)
                    link(v.tensor_tensor(gi[:], gi[:], ps[0:4, M1, 0:T], ALU.add))
                    v.tensor_tensor(gf[:], gf[:], ps[0:4, M2, 0:T], ALU.add).then_inc(S.gir, 1)
                    dve.wait_ge(S.elr, i + 1)
                    v.tensor_tensor(ql, e8, pj[:, HQ_, 0:TP].unsqueeze(1).broadcast_to([P, LEVELS, TP]), ALU.mult)\
                        .then_inc(S.qlr, 1)
                    dve.wait_ge(S.khr, i + 1)
                    dve.wait_ge(S.qlr, i + 1)
                    v.tensor_tensor(kl[:, 0:KL_DVE, :], e8[:, 0:KL_DVE, :],
                                    w4[:, 0:TP].unsqueeze(1).broadcast_to([P, KL_DVE, TP]), ALU.mult).then_inc(S.klr, 1)
                    dve.wait_ge(S.kder, i + 1)
                    v.tensor_tensor(w6[:, 0:TP], w6[:, 0:TP], w4[:, 0:TP], ALU.mult).then_inc(S.kdr, 1)

                    def pick(bank, at, mask):
                        return v.copy_predicated(sct[:, 0:3:2, :], over2(hmask[:, mask, :]),
                                                 ps[:, bank, at:at + TP].rearrange("p (t q) -> p t q", t=2))

                    for n, (bank, first) in enumerate(((M1, 0), (M2, 2), (M0, None), (M1, 4), (M2, 6))):
                        dve.wait_ge(S.lvl, i * 5 + n + 1)
                        if first is None:
                            v.tensor_copy(sct[:, 1, :], ps[:, M0, 0:P]).then_inc(S.lvc, 1)
                        else:
                            apart(dve)
                            link(pick(bank, 0, first))
                            apart(dve)
                            pick(bank, TP, first + 1).then_inc(S.lvc, 1)
                        dve.wait_ge(S.lvc, i * 5 + n + 1)
                    dve.wait_ge(S.kdtp, i + 1)
                    v.tensor_copy(kdt[:], ps[:, M0, 0:TP].rearrange("p (t q) -> p t q", t=2)).then_inc(S.kdtr, 1)
                    dve.wait_ge(S.ibr, i + 1)
                    dve.wait_ge(S.klr, i * 2 + 2)
                    link(v.tensor_tensor(tt8, ps[:, M1:M1 + 2, :].rearrange("p a (b k) -> p (a b) k", k=P),
                                         w4[:, TP:T].unsqueeze(2).broadcast_to([P, NB, P]), ALU.mult))
                    dve.wait_ge(S.snm, i + 1)
                    v.tensor_tensor(sn8[:], sn8[:], tt8, ALU.add).then_inc(S.snr, 1)
                    dve.wait_ge(page_free[3], i * 2 + 3)
                    v.tensor_copy(rbuf[:], ps[:, Z, :]).then_inc(S.zrow, 1)
                    dve.wait_ge(S.rsh, i + 2)
                    link(v.scalar_tensor_tensor(ot[:], ot[:], hp[:, HGG:HGG + 1], rs[:], ALU.mult, ALU.mult))
                    link(v.tensor_tensor(oa[:, i, :], ot[:], sgt[:, 0, :], ALU.mult))
                    dve.wait_ge(S.ztr, i + 1)
                    for n in range(4):
                        e, u = n // 2, n % 2
                        last = v.scalar_tensor_tensor(
                            zs[:, bds(i * 128 + e * 64, 64)].rearrange("p (j u h) -> p j u h", j=4, u=2)[:, :, u, :],
                            ps[:, Z, n * P:(n + 1) * P].rearrange("p (j h) -> p j h", j=4)[:, :, 0:SBH], SB_SCALE,
                            lp[:, SBB:SBB + SBH].unsqueeze(1).broadcast_to([P, 4, SBH]), ALU.mult, ALU.add)
                    last.then_inc(S.dve_it, 1)
                    dve.wait_ge(S.dve_it, i + 2)

                link(v.tensor_scalar(gf[:], gf[:], lp4[:, 1:2], None, ALU.add))
                link(v.tensor_scalar(gi[:], gi[:], lp4[:, 0:1], None, ALU.add))
                v.nop().then_inc(S.rl1, 1)
                dve.wait_ge(S.lnsr, 1)
                v.scalar_tensor_tensor(zt, zs[:], 0.0, zt, ALU.max, ALU.add).then_inc(S.spsr, 1)
                dve.wait_ge(S.rl1, 2)
                link(v.scalar_tensor_tensor(gf[:], gf[:], 0.0, r4[:, 1, :], ALU.min, ALU.subtract))
                link(v.tensor_tensor_scan(r4[:, 1, 0:TP], onerow[0:4, :], gf[:, 0:TP], 0.0, ALU.mult, ALU.add))
                v.tensor_tensor(r4[:, 0, 0:TP], gi[:, 0:TP], r4[:, 1, 0:TP], ALU.subtract).then_inc(S.rw1, 1)
                dve.wait_ge(S.rw1, 1)
                link(v.tensor_tensor_scan(rows[:, 0:TP], onerow[0:4, :], r4[:, 0, 0:TP], 0.0, ALU.mult, ALU.max))
                link(v.tensor_tensor(rows[:, TP + 24:], rows[:, 0:TP], r4[:, 1, 0:TP], ALU.add))
                a, ms, its = r4[:, 2, 0:8], r4[:, 2, 8:16], gi[:, TP:T]
                link(v.tensor_tensor(a, gf[:, TP:T], lp4[:, 2:10], ALU.add))
                link(v.tensor_tensor(ms, a, its, ALU.max))
                v.tensor_tensor(rows[:, TP:TP + 8], its, ms, ALU.subtract)
                v.tensor_tensor(rows[:, TP + 8:TP + 16], a, ms, ALU.subtract)
                v.tensor_scalar_mul(rows[:, TP + 16:TP + 24], ms, -1.0).then_inc(S.rw2, 1)
                dve.wait_ge(S.gcp, 1)
                v.tensor_copy(gcol[:], ps[:, M0, 0:8].rearrange("p (t h) -> p t h", t=2)).then_inc(S.gcr, 1)
                dve.wait_ge(S.gcr, 1)
                dve.wait_ge(S.sufs, 1)
                v.tensor_tensor(zs[:], zs[:], ps[:, Z, :], ALU.subtract).then_inc(S.t2r, 1)
                dve.wait_ge(S.rw3, 1)
                v.tensor_tensor(bd, rows.unsqueeze(1).broadcast_to([4, 4, nrow]),
                                consts[0:4, 0, 0:4].unsqueeze(2).broadcast_to([4, 4, nrow]), ALU.mult).then_inc(S.bdr, 1)

                def value_rows(n):
                    dve.wait_ge(S.vrd, n + 1)
                    dve.wait_ge(page_free[3], n + (NB + 2))
                    v.tensor_copy(rbuf[:], ps[:, 3, :]).then_inc(S.vrow, 1)

                dve.sem_inc(S.vrd, 1)
                v.memset(ps[:, 3, :], 0.0).then_inc(S.vrow, 1)
                at, products.pos = slots.pos, 0
                before_b = products.count.n
                with dve.Fori(0, HEADS) as i, slots.loop(i, HEADS, [2], at), products.count.loop(i, HEADS, 2), \
                        link.loop(i, HEADS, 13):
                    slots.take(2, at)
                    products.take(2)
                    products.take(2)
                    dve.wait_ge(S.trb, i + 1)
                    link(v.tensor_copy(vk, ps[:, M0, :].rearrange("p (n t) -> p n t", n=4)))
                    dve.wait_ge(S.kqr, i + 1)
                    v.tensor_scalar(dm[:, 0:TP], ps[:, M2, 0:TP], gcol[:, 0, bds(i, 1)], 0.0, ALU.subtract, ALU.max)
                    v.tensor_scalar(dm[:, TP:TP + P], ps[:, M2, P:TP], gcol[:, 1, bds(i, 1)], 0.0, ALU.subtract, ALU.max)
                    link(v.tensor_copy(sw[:], ps[:, M2, TP:TP + 24]))
                    d = dm.rearrange("p (n t) -> p n t", t=P)[:, 0:3:2, :]
                    v.tensor_tensor(d, d, over2(causalpos), ALU.add).then_inc(S.exr, 1)
                    smp = slice(TP, T)
                    wv, dec = sw[:, 0:8], sw[:, 8:16]
                    link(v.tensor_tensor(s8a[:], vs[:, smp], wv, ALU.mult))
                    link(v.tensor_tensor(s8c[:], lp[:, bds(i * NB + N0, NB)], dec, ALU.mult))
                    link(v.tensor_tensor(s8b[:], ks[:, smp], wv, ALU.mult))
                    v.tensor_tensor(s8c[:], s8c[:], s8b[:], ALU.add).then_inc(S.nnr, 1)
                    dve.wait_ge(S.nnr, i + 1)
                    v.tensor_tensor(s8b[:], s8c[:], qs[:, smp], ALU.mult).then_inc(S.nqr, 1)
                    dve.wait_ge(S.dmr, i + 1)
                    v.tensor_tensor(wt, dm, ps[:, M1, 0:384], ALU.mult)
                    v.tensor_scalar(vw2[:, 0, :], vk[:, 0, :], dm[:, TP - 1:TP], None, ALU.mult)
                    v.tensor_scalar(vw2[:, 1, :], vk[:, 1, :], dm[:, TP + P - 1:TP + P], None, ALU.mult)\
                        .then_inc(S.vwr, 1)
                    value_rows(i * 2)
                    dve.wait_ge(S.adr, i + 1)
                    link(v.tensor_tensor(w1[:, 0:TP], w1[:, 0:TP], w3[:, 0:TP], ALU.max))
                    link(v.reciprocal(w1[:, 0:TP], w1[:, 0:TP]))
                    v.tensor_tensor(ot[:, 0:TP], ps[:, M0, 0:TP], w1[:, 0:TP], ALU.mult).then_inc(S.htr, 1)
                    dve.wait_ge(S.kbr, i + 1)
                    bank2 = ps[:, M1:M1 + 2, :].rearrange("p a (b k) -> p (a b) k", k=P)
                    link(v.tensor_tensor(tt8, bank2, s8a[:].unsqueeze(2).broadcast_to([P, NB, P]), ALU.mult))
                    dve.wait_ge(S.cnp, i + 1)
                    v.tensor_tensor(sn8[:], sn8[:], tt8, ALU.add).then_inc(S.cnr, 1)
                    dve.wait_ge(S.cnr, i + 1)
                    dve.wait_ge(S.qbr, i + 1)
                    link(v.tensor_tensor(tt8, sn8[:], bank2, ALU.mult))
                    link(v.tensor_reduce(w3[:, smp], tt8, AX.X, ALU.add))
                    dve.wait_ge(S.dna, i + 1)
                    link(v.tensor_tensor(w1[:, smp], w1[:, smp], sw[:, 16:24], ALU.max))
                    link(v.reciprocal(w1[:, smp], w1[:, smp]))
                    v.tensor_tensor(ot[:, smp], w3[:, smp], w1[:, smp], ALU.mult).then_inc(S.otr, 1)
                    value_rows(i * 2 + 1)
                    dve.wait_ge(S.rsb, i + 1)
                    link(v.scalar_tensor_tensor(ot[:], ot[:], lp[:, bds(i + MLG, 1)], rs[:], ALU.mult, ALU.mult))
                    v.tensor_tensor(oc[:, i, :], ot[:], mo[:, i, :], ALU.mult).then_inc(S.dve_it, 1)
                    dve.wait_ge(S.dve_it, i + HEADS + 2)

                dve.wait_ge(S.vrd, NB + 1)
                for h in range(2):
                    a, e = 64 * h, 64 * h + 64
                    last = v.tensor_copy(ob[a:e, :, TP:T],
                                         ps[a:e, 2, 0:64].rearrange("p (b c h) -> p c b h", c=HEADS, h=2)[:, :, :, h])
                last.then_inc(S.dve_it, 1)
                dve.wait_ge(S.sig, 2 * HEADS)
                products.pos = 0
                for s in range(4):
                    r, _, before = slots.take(6)
                    for n in range(2):
                        c = s * 2 + n
                        for br in range(3):
                            b, count = products.take()
                            dve.wait_ge(slot_done[r], before + n * 3 + br + 2)
                            dst = merged[:, c, :] if br == 0 else ft[:, br - 1, :]
                            v.tensor_tensor(dst, ps[:, b, 0:T], gates[:, br * KC + c, :], ALU.mult).then_inc(S.evac, 1)
                            dve.wait_ge(S.evac, count + 5)
                            if br:
                                ins_ = v.tensor_tensor(merged[:, c, :], merged[:, c, :], dst, ALU.add)
                                if br == 2:
                                    ins_.then_inc(S.mg, 1)
                                    dve.wait_ge(S.mg, c + 1)
                                else:
                                    link(ins_)
                clear_sum()
                for s in range(4):
                    slots.take(2)
                    for n in range(2):
                        sum_squares()
                residual(2)
                scale_table(2)
                gate_table(2)
                ahead.follow(slots)
                split(2 * KC)
                scale_samples(3)
                modulate_samples(3)
                scale_prompt()
                split_input(3)
                with dve.Fori(0, 5) as i, slots.loop(i, 5, [2] * 4), ahead.loop(i, 5, [2] * 4), \
                        products.count.loop(i, 5, 8), pieces.count.loop(i, 5, 8), hids.loop(i, 5, 4), \
                        exps.loop(i, 5, 4), link.loop(i, 5, 4):
                    for k in range(4):
                        split(2 * KC)
                        ffn_slot(k, i * 4 + k, slots.take(2))
                for k in range(2):
                    split(FC if k else 2 * KC)
                    ffn_slot(k, 20 + k, slots.take(2))
                down()
                residual(3)

            @block.scalar
            def _(act):
                slots, products, exps, sums = Slots(), Products(), Count(), Count()
                ahead, pieces = Slots(), Products()
                link = Chain(act, S.achain)
                A = nc.scalar.activation
                nc.scalar.preload_act_table_set("natural_log_exp_and_others")
                act.sem_inc(S.rsh, 1)
                act.sem_inc(S.store, 16)

                def squares(n):
                    for c in range(KC):
                        if n > 1:
                            act.wait_ge(S.x_fin, (n - 2) * KC + c + 1)
                            act.wait_ge(S.xsum, n - 1)
                        A(xn[:, c, :], x[:, c, :], ACT.Square).then_inc(S.x2_ready, 1)

                def rsqrt(bank, width):
                    link(A(rs[:], ps[:, bank, 0:T], ACT.Ln, scale=1.0 / width, bias=eps[:]))
                    return A(rs[:], rs[:], ACT.Exp, scale=-0.5)

                def pre(n):
                    squares(n)
                    act.wait_ge(S.ss_ready, n)
                    rsqrt(Z, D).then_inc(S.rs_ready, 1)

                def post(n):
                    act.wait_ge(S.yss_ready, n)
                    rsqrt(Z, D).then_inc(S.yrs_ready, 1)

                def split(tiles):
                    r, loads, _ = ahead.take(2 if tiles == 2 * KC else 1)
                    act.wait_ge(slot_full[r], loads * 16 + 16)
                    for at in range(0, tiles, PIECE):
                        place, m = pieces.take()
                        n = min(PIECE, tiles - at)
                        act.wait_ge(S.whi_done, m + 1)
                        A(whi[:, place, 0:n * P], ring[:, r, at * P:(at + n) * P], ACT.Copy).then_inc(S.whi_ready, 1)

                def modulate(n):
                    act.wait_ge(S.xsmp, n)
                    for c in range(KC):
                        act.wait_ge(S.xp_ready, (n - 1) * KC + c + 1)
                        A(xn[:, c, 0:TP], xn[:, c, 0:TP], ACT.Identity, scale=atab[:, c, 0:1],
                          bias=ada[:, (n - 1) * 3 * KC + c, 0:1]).then_inc(S.xmod, 1)

                def ffn_slot(k, chunk):
                    r, _, before = slots.take(2)
                    b, _ = products.take()
                    _, n = products.take()
                    exps()
                    act.wait_ge(slot_done[r], before + 2)
                    t = fe[:, k % 2, :]
                    link(A(t, ps[:, b, 0:T], ACT.Exp, scale=-1.0))
                    link(A(t, t, ACT.Ln, bias=1.0))
                    A(t, t, ACT.Exp, scale=-1.0).then_inc(S.e_ready, 1)
                    act.wait_ge(S.evac, n + 5)
                    A(hid[:, chunk, :], ft[:, k % 2, :], ACT.Copy).then_inc(S.hhi_ready, 1)

                def y_chunk(r, done, c):
                    n = sums()
                    b, _ = products.take()
                    act.wait_ge(slot_done[r], done)
                    act.wait_ge(S.accd, n + 1)
                    A(y[:, c, :], ps[:, b, 0:T], ACT.Copy)
                    A(sq[:, sums.n % 2, :], ps[:, b, 0:T], ACT.Square).then_inc(S.evac, 1)

                def down():
                    for c in range(KC):
                        if c < KC - 1:
                            split(FC)
                        r, _, before = slots.take(1)
                        y_chunk(r, before + 2, c)

                for k in range(8):
                    slots.take(1)
                ahead.follow(slots)
                pre(1)
                modulate(1)
                split(2 * KC)
                with act.Fori(0, 4) as i, slots.loop(i, 4, [2, 1] * 4), ahead.loop(i, 4, [1, 2] * 4), \
                        products.count.loop(i, 4, 8), pieces.count.loop(i, 4, 8), exps.loop(i, 4, 4), link.loop(i, 4, 8):
                    for k in range(4):
                        ahead.take(1)
                        split(2 * KC)
                        ffn_slot(k, i * 4 + k)
                        slots.take(1)
                for k in range(16, FC):
                    if k < 20:
                        ahead.take(1)
                    split(2 * KC if k < FC - 1 else FC)
                    ffn_slot(k, k)
                    if k < 20:
                        slots.take(1)
                down()
                post(1)
                pre(2)
                modulate(2)

                def evac(r, done, dst, exp=False):
                    b, _ = products.take()
                    act.wait_ge(slot_done[r], done)
                    A(dst, ps[:, b, 0:T], ACT.Exp if exp else ACT.Copy, scale=-1.0 if exp else 1.0).then_inc(S.evac, 1)

                for s in range(2):
                    r, _, before = slots.take(2)
                    for n in range(2):
                        evac(r, before + 2 + n, ob[:, s * 2 + n, :])

                def softplus_tail(t, src):
                    link(A(t, src, ACT.Abs))
                    link(A(t, t, ACT.Exp, scale=-1.0))
                    return A(t, t, ACT.Ln, bias=1.0)

                def sigmoid_tail(g):
                    link(A(g, g, ACT.Ln, bias=1.0))
                    apart(act)
                    A(g, g, ACT.Exp, scale=-1.0).then_inc(S.sig, 1)

                before_a = products.count.n
                with act.Fori(0, HEADS) as i, slots.loop(i, HEADS, [3] * 4), products.count.loop(i, HEADS, 12), \
                        link.loop(i, HEADS, 15):
                    act.wait_ge(S.dve_it, i + 1)
                    act.wait_ge(S.pool_it, i + 1)
                    act.dma_start(hp[:], ins.head_par[layer, i]).then_inc(S.hpar, 16)
                    act.dma_start(st8[:], ins.hgrn[layer, i]).then_inc(S.hpar, 16)
                    dests = [pj[:, SK_, :], pj[:, SV_, :], xp[:, 3:3 + T], pj[:, HQ_, :], pj[:, HF_, :], pj[:, HI_, :],
                             pj[:, HG_, :], sgt[:, 1, :], gates[:, i * 4, :]]
                    for k in range(2):
                        r, _, before = slots.take(3)
                        for n in range(3):
                            evac(r, before + 2 + n, dests[3 * k + n])
                    act.wait_ge(S.evac, i * 12 + (before_a + 6 + 4))
                    act.dma_start(outs.k[layer, :, i, :], pj[:, SK_, :]).then_inc(S.store, 16)
                    act.dma_start(outs.v[layer, :, i, :], pj[:, SV_, :]).then_inc(S.store, 16)
                    act.dma_start(outs.conv_p[layer, i], xp[:, TP:TP + 3]).then_inc(S.store, 16)
                    softplus_tail(w1, pj[:, HF_, :]).then_inc(S.l1r, 1)
                    act.wait_ge(S.pchain, i + 1)
                    act.dma_start(outs.conv_s[layer, i], nbs[:].rearrange("p j b -> p (j b)")).then_inc(S.store, 16)
                    act.wait_ge(S.zpr, i + 1)
                    softplus_tail(sbt, zp).then_inc(S.lnr, 1)
                    r, _, before = slots.take(3)
                    evac(r, before + 2, dests[6])
                    evac(r, before + 3, dests[7], exp=True)
                    act.wait_ge(S.evac, i * 12 + (before_a + 8 + 4))
                    link(A(sgt[:, 0, :], pj[:, HG_, :], ACT.Exp, scale=-1.0))
                    link(A(sgt[:], sgt[:], ACT.Ln, bias=1.0))
                    A(sgt[:], sgt[:], ACT.Exp, scale=-1.0).then_inc(S.sge, 1)
                    act.wait_ge(S.accr, i + 1)
                    link(A(fe[:, 0, :], xc[:], ACT.Exp, scale=-1.0))
                    link(A(fe[:, 0, :], fe[:, 0, :], ACT.Ln, bias=1.0))
                    A(fe[:, 0, :], fe[:, 0, :], ACT.Exp, scale=-1.0).then_inc(S.xer, 1)
                    act.wait_ge(S.t_ready, i + 1)
                    A(sbt, zp, ACT.Exp).then_inc(S.ar, 1)
                    act.wait_ge(S.ur, i + 1)
                    softplus_tail(w3, w3).then_inc(S.l2r, 1)
                    act.wait_ge(S.tzr, i + 1)
                    A(w4, w4, ACT.Exp).then_inc(S.khr, 1)
                    evac(r, before + 4, dests[8], exp=True)
                    act.wait_ge(S.qkv_ps, i + 1)
                    for j, b in enumerate((M1, M2, M0)):
                        last = A(qkv[:, j, i, :], ps[:, b, 0:T], ACT.Copy)
                    last.then_inc(S.qkv_sb, 1)
                    r, _, before = slots.take(3)
                    evac(r, before + 2, gates[:, i * 4 + 1, :], exp=True)
                    act.wait_ge(S.dlr, i + 1)
                    link(A(e8, e8, ACT.Abs))
                    A(e8, e8, ACT.Exp, scale=-1.0).then_inc(S.elr, 1)
                    A(w6[:, 0:TP], w6[:, 0:TP], ACT.Exp, scale=-1.0).then_inc(S.kder, 1)
                    A(s8a[:], w5[:, TP:T], ACT.Exp).then_inc(S.fsr, 1)
                    evac(r, before + 3, gates[:, i * 4 + 2, :], exp=True)
                    act.wait_ge(S.ho, i + 1)
                    A(ot[:, 0:TP], ps[:, M0, 0:TP], ACT.Copy)
                    link(A(hsp[:], ps[:, M0, 384:512], ACT.Copy))
                    act.dma_start(outs.hgrn_p[layer, i], hsp[:]).then_inc(S.store, 16)
                    act.wait_ge(S.snr, i + 1)
                    act.dma_start(outs.hgrn_s[layer, i], sn8[:].rearrange("p b k -> p (b k)")).then_inc(S.store, 16)
                    evac(r, before + 4, gates[:, i * 4 + 3, :], exp=True)
                    act.wait_ge(S.hos, i + 1)
                    link(A(ot[:, TP:T], ps[:, M1, 0:NB], ACT.Copy))
                    A(w2, ot[:], ACT.Square).then_inc(S.osq, 1)
                    act.wait_ge(S.hss, i + 1)
                    rsqrt(M2, P).then_inc(S.rsh, 1)
                    act.wait_ge(S.evac, i * 12 + (before_a + 12 + 4))
                    apart(act)
                    sigmoid_tail(gates[:, bds(i * 4, 4), :])
                    act.wait_ge(S.store, i * (16 * STORES_A) + 16 * (STORES_A + 1))

                act.wait_ge(S.dve_it, HEADS + 1)
                softplus_tail(zt, zs[:]).then_inc(S.lnsr, 1)
                act.wait_ge(S.rl1, 1)
                softplus_tail(r4[:, 1, :], gf[:]).then_inc(S.rl1, 1)
                act.wait_ge(S.rw2, 1)
                A(rows[:, TP:TP + 24], rows[:, TP:TP + 24], ACT.Exp).then_inc(S.rw3, 1)
                act.dma_start(outs.m_p[layer], rows[:, 2 * TP + 23:2 * TP + 24]).then_inc(S.store, 16)
                act.dma_start(outs.m_s[layer], r4[:, 2, 8:16]).then_inc(S.store, 16)
                act.wait_ge(S.t2r, 1)
                A(zs[:], zs[:], ACT.Exp).then_inc(S.asr, 1)
                act.wait_ge(S.store, 16 * (STORES_A * HEADS + 3))

                at, products.pos = slots.pos, 0
                before_b = products.count.n
                with act.Fori(0, HEADS) as i, slots.loop(i, HEADS, [2], at), products.count.loop(i, HEADS, 2), \
                        link.loop(i, HEADS, 2):
                    act.wait_ge(S.snp, i * 2 + HEADS)
                    apart(act)
                    A(vs, qkv[:, 2, i, :], ACT.Copy).then_inc(S.stg, 1)
                    A(ks, qkv[:, 1, i, :], ACT.Copy, scale=ML_SCALE).then_inc(S.stg, 1)
                    A(qs, qkv[:, 0, i, :], ACT.Copy).then_inc(S.stg, 1)
                    act.wait_ge(S.dve_it, i + HEADS + 1)
                    act.dma_start(st8[:], ins.ml_c[layer, i]).then_inc(S.hpar, 16)
                    r, _, before = slots.take(2, at)
                    gate_banks = [products.take(2)[0] for _ in range(2)]

                    def gate(n):
                        act.wait_ge(slot_done[r], before + 2 + n)
                        A(gates[:, i * 2 + (16 + n), :], ps[:, gate_banks[n], 0:T], ACT.Exp, scale=-1.0)\
                            .then_inc(S.evac, 1)

                    gate(0)
                    act.wait_ge(S.exr, i + 1)
                    A(dm, dm, ACT.Exp, scale=-1.0).then_inc(S.dmr, 1)
                    act.wait_ge(S.nnr, i + 1)
                    act.dma_start(outs.n_s[layer, :, i, :], s8c[:]).then_inc(S.store, 16)
                    act.wait_ge(S.ndr, i + 1)
                    A(w1[:, 0:TP], ps[:, M1, 0:TP], ACT.Abs)
                    A(w3[:, 0:TP], ps[:, Z, 0:TP], ACT.Exp, scale=-1.0).then_inc(S.adr, 1)
                    act.wait_ge(S.cst, i + 1)
                    A(hsp[:], ps[:, M2, 0:P], ACT.Copy)
                    A(nst[:], ps[:, M2, P:P + 1], ACT.Copy).then_inc(S.cev, 1)
                    act.wait_ge(S.cev, i + 1)
                    act.dma_start(outs.c_p[layer, i], hsp[:]).then_inc(S.store, 16)
                    act.dma_start(outs.n_p[layer, i], nst[:]).then_inc(S.store, 16)
                    gate(1)
                    act.wait_ge(S.dns, i + 1)
                    A(w1[:, TP:T], ps[:, M0, 0:NB], ACT.Abs).then_inc(S.dna, 1)
                    act.wait_ge(S.cnr, i + 1)
                    act.dma_start(outs.c_s[layer, i], sn8[:].rearrange("p b k -> p (b k)")).then_inc(S.store, 16)
                    act.wait_ge(S.otr, i + 1)
                    A(w2, ot[:], ACT.Square).then_inc(S.sqh, 1)
                    act.wait_ge(S.hbs, i + 1)
                    rsqrt(M0, P).then_inc(S.rsb, 1)
                    act.wait_ge(S.evac, i * 2 + (before_b + 2 + 4))
                    apart(act)
                    sigmoid_tail(gates[:, bds(i * 2 + 16, 2), :])
                    act.wait_ge(S.store, i * (16 * STORES_B) + 16 * (STORES_A * HEADS + 3 + STORES_B))

                products.pos = 0
                for s in range(4):
                    slots.take(6)
                    for n in range(6):
                        products.take()
                for s in range(4):
                    r, _, before = slots.take(2)
                    for n in range(2):
                        y_chunk(r, before + 2 + n, s * 2 + n)
                post(2)
                ahead.follow(slots)
                split(2 * KC)
                pre(3)
                modulate(3)
                with act.Fori(0, 5) as i, slots.loop(i, 5, [2] * 4), ahead.loop(i, 5, [2] * 4), \
                        products.count.loop(i, 5, 8), pieces.count.loop(i, 5, 8), exps.loop(i, 5, 4), link.loop(i, 5, 8):
                    for k in range(4):
                        split(2 * KC)
                        ffn_slot(k, i * 4 + k)
                for k in range(2):
                    split(FC if k else 2 * KC)
                    ffn_slot(k, 20 + k)
                down()
                post(3)

            @block.gpsimd
            def _(pool):
                g = nc.gpsimd
                pool.sem_inc(S.pool_it, 1)
                identb = consts[:, 0:1, :].broadcast_to([P, NB, P])
                before_a = 2 * FC + KC + HEADS

                def residual(n):
                    for c in range(KC):
                        pool.wait_ge(S.res, (n - 1) * KC + c + 1)
                        g.tensor_tensor(x[:, c, 0:TP], x[:, c, 0:TP], residual_part(c), ALU.add).then_inc(S.x_fin, 1)


                residual(1)

                def diagonal(src):
                    return g.tensor_tensor(dg8, identb, src.unsqueeze(2).broadcast_to([P, NB, P]), ALU.mult)

                with pool.Fori(0, HEADS) as i:
                    pool.wait_ge(S.dve_it, i + 1)
                    pool.wait_ge(S.store, i * (16 * STORES_A) + 16)
                    pool.wait_ge(S.evac, i * 12 + (before_a + 4))
                    apart(pool)
                    g.tensor_copy(pj[:, SQ_, :], ob[:, i, :]).then_inc(S.sqc, 1)
                    pool.wait_ge(S.hpar, i * 32 + 32)
                    pool.wait_ge(S.evac, i * 12 + (before_a + 3 + 4))
                    apart(pool)
                    g.tensor_copy(nbs[:, 0:2, :], hp[:, CST + 8:CST + 24].rearrange("p (j b) -> p j b", j=2))
                    g.tensor_copy(nbs[:, 2, :], xp[:, 3 + TP:3 + T]).then_inc(S.pchain, 1)
                    pool.wait_ge(S.qmr, 1)
                    for e in range(2):
                        last = g.tensor_copy(qst[:, e, :, :], qm[:, i * 2 + e, :, :])
                    last.then_inc(S.qstr, 1)
                    pool.wait_ge(S.fsr, i + 1)
                    g.tensor_tensor(sn8[:], st8[:], s8a[:].unsqueeze(2).broadcast_to([P, NB, P]), ALU.mult)\
                        .then_inc(S.snm, 1)
                    pool.wait_ge(S.khr, i + 1)
                    pool.wait_ge(S.qlr, i + 1)
                    g.tensor_tensor(kl[:, KL_DVE:, :], e8[:, KL_DVE:, :],
                                    w4[:, 0:TP].unsqueeze(1).broadcast_to([P, LEVELS - KL_DVE, TP]), ALU.mult)\
                        .then_inc(S.klr, 1)
                    pool.wait_ge(S.lvc, i * 5 + 5)
                    diagonal(pj[:, HI_, TP:T]).then_inc(S.snp, 1)
                    pool.wait_ge(S.snp, i + 1)
                    pool.sem_inc(S.pool_it, 1)

                with pool.Fori(0, HEADS) as i:
                    pool.wait_ge(S.dve_it, i + (HEADS + 1))
                    pool.wait_ge(S.store, i * (16 * STORES_B) + 16 * (STORES_A * HEADS + 3))
                    pool.wait_ge(S.vrd, i * 2 + 1)
                    pool.wait_ge(S.asr, 1)
                    for e in range(2):
                        last = g.tensor_copy(ast[:, e, :], zs[:, bds(i * 128 + e * 64, 64)])
                    last.then_inc(S.astr, 1)
                    pool.wait_ge(S.stg, i * 3 + 3)
                    diagonal(ks[:, TP:T]).then_inc(S.snp, 1)
                    pool.wait_ge(S.hpar, i * 16 + (32 * HEADS + 16))
                    pool.wait_ge(S.exr, i + 1)
                    g.tensor_tensor(sn8[:], st8[:], sw[:, 8:16].unsqueeze(2).broadcast_to([P, NB, P]), ALU.mult)\
                        .then_inc(S.cnp, 1)
                    pool.wait_ge(S.kbr, i + 1)
                    diagonal(qs[:, TP:T]).then_inc(S.snp, 1)
                residual(2)
                residual(3)

        with nc.Fori(0, DEPTH) as layer:
            with nc.Block() as block:
                one_layer(block, layer)
            clear_all()

        with nc.Block() as block:
            @block.sync
            def _(sp):
                sp.dma_start(outs.y, x[:]).then_inc(S.store, 16)
                sp.wait_ge(S.store, 16)


def over2(mask):
    return mask.unsqueeze(1).broadcast_to([P, 2, P])


def diag_blocks(t, h):
    return t[:, h, :].rearrange("p (n t) -> p n t", t=P)[:, 0:3:2, :]


def kernel(**inputs):
    import numpy as np
    import concourse.bacc as bacc
    from concourse.bass_utils import run_bass_kernel_spmd

    a = {k: np.asarray(v) for k, v in inputs.items()}

    def tokens(prompt, sample):
        t = np.concatenate([prompt.reshape(-1, D), sample.reshape(-1, D)], 0)
        return t.T.reshape(KC, P, -1).transpose(1, 0, 2)

    def tiles(w, per_slot):
        *lead, k, n = w.shape
        n_lead = len(lead)
        t = w.reshape(*lead, k // P, P, n // P // per_slot, per_slot, P)
        ax = list(range(n_lead))
        t = t.transpose(*ax, n_lead + 2, n_lead + 1, n_lead + 3, n_lead, n_lead + 4)
        return t.reshape(*lead, n // P // per_slot, P, per_slot * (k // P) * P)

    def chunk_cols(v, last=False):
        return v.reshape(DEPTH, -1, P).transpose(0, 2, 1)

    w_in = a["w_in"].reshape(DEPTH, D, -1, P)
    first = dict(hq=0, hf=4, hi=8, hg=12, sq=16, sk=20, sv=24, mx=28, mo=32, ga=36)
    g0 = first["ga"]
    order_a, order_b = [], []
    for i in range(HEADS):
        order_a += [first[k] + i for k in ("sk", "sv", "mx", "hq", "hf", "hi", "hg", "mo")] + \
                   [g0 + 4 * i + j for j in range(4)]
        order_b += [g0 + 16 + 2 * i + j for j in range(2)]

    def in_cols(order):
        return w_in[:, :, order, :].reshape(DEPTH, D, len(order) * P)

    ffn = a["w_ffn_in"].reshape(DEPTH, 2, D, 2, FC, P).transpose(0, 1, 2, 4, 3, 5).reshape(DEPTH, 2, D, 2 * DFF)
    proj = np.stack([a["w_hg_proj"], a["w_sb_proj"], a["w_ml_proj"]], 1)
    proj = proj.reshape(DEPTH, 3, HEADS, P, 4, 2, P).transpose(0, 4, 3, 5, 1, 2, 6).reshape(DEPTH, 4, P, 24 * P)

    layer_par = np.zeros((DEPTH, P, LPN), np.float32)
    layer_par[:, :, BADA:BADA + ADA_N] = chunk_cols(a["b_ada"])
    layer_par[:, :, GPRE:GPRE + 24] = chunk_cols(a["g_pre"].reshape(DEPTH, -1))
    layer_par[:, :, GPOST:GPOST + 24] = chunk_cols(a["g_post"].reshape(DEPTH, -1))
    layer_par[:, :, SBB:SBB + SBH] = a["sb_bias"][:, None, :]
    layer_par[:, :, N0:N0 + 32] = a["state_mlstm_n"].transpose(1, 3, 2, 0).reshape(DEPTH, P, 32)
    layer_par[:, :, MLG:MLG + 4] = chunk_cols(a["ml_gain"])
    layer_par4 = np.zeros((DEPTH, 4, 2 + NB), np.float32)
    layer_par4[:, :, 0] = a["ml_b_if"][:, 0:4]
    layer_par4[:, :, 1] = a["ml_b_if"][:, 4:8]
    layer_par4[:, :, 2:] = a["state_mlstm_m"].transpose(1, 2, 0)
    head_par = np.zeros((DEPTH, HEADS, P, HPN), np.float32)
    for j, k in enumerate(("ml_wq", "ml_wk", "ml_wv")):
        head_par[:, :, :, WQ + j * P:WQ + (j + 1) * P] = a[k]
    head_par[:, :, :, WIF:WIF + 24] = a["ml_w_if"].reshape(DEPTH, 3, HEADS, P, 8).transpose(0, 2, 3, 1, 4)\
        .reshape(DEPTH, HEADS, P, 24)
    head_par[:, :, :, CW:CW + 4] = a["ml_conv_w"].reshape(DEPTH, 4, HEADS, P).transpose(0, 2, 3, 1)
    head_par[:, :, :, CBIAS] = a["ml_conv_b"].reshape(DEPTH, HEADS, P)
    head_par[:, :, :, HGG] = a["hg_gain"].reshape(DEPTH, HEADS, P)
    head_par[:, :, :, CST:CST + 24] = a["state_mlstm_conv"].reshape(NB, DEPTH, 3, HEADS, P)\
        .transpose(1, 3, 4, 2, 0).reshape(DEPTH, HEADS, P, 24)
    head_par[:, :, :, SBB2:SBB2 + 2] = a["sb_bias"].reshape(DEPTH, HEADS, 1, 2)

    r = np.arange(P)
    k, q = r[:, None], r[None, :]
    consts = np.stack([k == q, k + q >= 0, k >= q, k < q], 1).astype(np.float32)
    consts = np.concatenate([consts, np.where(k < q, 0.0, NEVER)[:, None], np.where(k > q, -NEVER, 0.0)[:, None]], 1)
    masks = [k == q]
    for lv in range(LEVELS - 1):
        half = 1 << lv
        masks.append((k // (2 * half) == q // (2 * half)) & (k % (2 * half) < half) & (q % (2 * half) >= half))
    masks = np.stack(masks, 1)

    def ada_slots(first, group, groups):
        w = a["w_ada"][:, :, first * P:(first + group * groups) * P]
        w = w.reshape(DEPTH, KC // 2, 2, P, groups, 4, group // 4 * P).transpose(0, 4, 1, 3, 2, 5, 6)
        return w.reshape(DEPTH, groups * 4, P, 2 * group * P)

    w_ada8 = np.concatenate([ada_slots(0, 8, 2), ada_slots(ADA_N - 8, 8, 1)], 1)
    feeds = dict(
        consts=consts.astype(np.float32), masks=masks.astype(np.float32),
        x=tokens(a["x_prompt"], a["x_sample"]), c=tokens(a["c_prompt"], a["c_sample"]),
        lb=a["hg_lb_logits"].reshape(DEPTH, HEADS, P).transpose(2, 0, 1),
        page_table=a["page_table"].reshape(1, NB * PAGES),
        w_ada8=w_ada8, w_ada12=ada_slots(ADA_LOOP, 12, 4),
        sel=np.equal(r[:, None] % 32, np.arange(SBH)).astype(np.float32),
        w_ffn_in=tiles(ffn, 2), w_ffn_down=tiles(a["w_ffn_down"], 1),
        w_sq=tiles(in_cols([first["sq"] + i for i in range(4)]), 2),
        w_a=tiles(in_cols(order_a), 3), w_b=tiles(in_cols(order_b), 2), w_proj=proj, w_out=tiles(a["w_out"], 2),
        k_pages=a["cache_sb_k"].reshape(PHYS, DEPTH, P, HEADS, P).transpose(1, 0, 4, 3, 2).reshape(DEPTH, PHYS, P, 512),
        v_pages=a["cache_sb_v"].reshape(PHYS, DEPTH, P, 512).transpose(1, 0, 2, 3),
        layer_par=layer_par, layer_par4=layer_par4, head_par=head_par,
        hgrn=a["state_hgrn"].transpose(1, 2, 3, 0, 4).reshape(DEPTH, HEADS, P, NB * P),
        ml_c=a["state_mlstm_c"].transpose(1, 2, 3, 0, 4).reshape(DEPTH, HEADS, P, NB * P),
    )
    results = dict(
        y=(P, KC, T), k=(DEPTH, P, HEADS, T), v=(DEPTH, P, HEADS, T), hgrn_p=(DEPTH, HEADS, P, P),
        hgrn_s=(DEPTH, HEADS, P, NB * P), c_p=(DEPTH, HEADS, P, P), c_s=(DEPTH, HEADS, P, NB * P),
        n_p=(DEPTH, HEADS, P, 1), n_s=(DEPTH, P, HEADS, NB), m_p=(DEPTH, HEADS, 1), m_s=(DEPTH, HEADS, NB),
        conv_p=(DEPTH, HEADS, P, 3), conv_s=(DEPTH, HEADS, P, 3 * NB),
    )
    nc = bacc.Bacc("TRN2", target_bir_lowering=False, num_devices=1)
    arrays, ins, outs = {}, {}, {}
    for name, v in feeds.items():
        v = np.ascontiguousarray(v)
        arrays["in_" + name] = v
        ins[name] = nc.dram_tensor("in_" + name, v.shape, mybir.dt.from_np(v.dtype), kind="ExternalInput").ap()
    for name, shape in results.items():
        outs[name] = nc.dram_tensor("out_" + name, shape, F32, kind="ExternalOutput").ap()
    build(nc, namedtuple("Inputs", ins)(**ins), namedtuple("Outputs", outs)(**outs))
    got = run_bass_kernel_spmd(nc, [arrays], core_ids=[0]).results[0]
    o = {name: np.asarray(got["out_" + name]) for name in results}

    yt = o["y"].transpose(2, 1, 0).reshape(T, D)
    kk, vv = (o[n].transpose(0, 3, 2, 1).reshape(DEPTH, T, SBH, 64) for n in ("k", "v"))
    hs = o["hgrn_s"].reshape(DEPTH, HEADS, P, NB, P).transpose(3, 0, 1, 2, 4)
    cs = o["c_s"].reshape(DEPTH, HEADS, P, NB, P).transpose(3, 0, 1, 2, 4)
    conv_s = o["conv_s"].reshape(DEPTH, HEADS, P, 3, NB).transpose(4, 0, 3, 1, 2).reshape(NB, DEPTH, 3, 512)
    conv_p = o["conv_p"].transpose(0, 3, 1, 2).reshape(1, DEPTH, 3, 512)
    c = np.ascontiguousarray
    return (c(yt[None, 0:TP]), c(yt[TP:, None]), c(kk[None, :, 0:TP]), c(vv[None, :, 0:TP]),
            c(kk[:, TP:].transpose(1, 0, 2, 3)[:, :, None]), c(vv[:, TP:].transpose(1, 0, 2, 3)[:, :, None]),
            c(o["hgrn_p"][None]), c(hs), c(o["c_p"][None]), c(cs), c(o["n_p"][None, :, :, :, 0]),
            c(o["n_s"].transpose(3, 0, 2, 1)), c(o["m_p"].transpose(2, 0, 1)), c(o["m_s"].transpose(2, 0, 1)),
            conv_p, c(conv_s))
```
